# Optimizing a Trainium2 kernel written in Bass

```python
import math
import jax
import jax.numpy as jnp
from jax import lax
import numpy as np
import jax, jax.numpy as jnp

D_MODEL = 1024
BATCH = 1
SEQ = 256
DEPTH = 1

CHUNK = 64
HEAD_DIM = 64
N_BRANCH = 4
BRANCH_WIDTH = D_MODEL // N_BRANCH
CONV_WIDTH = 3
SC_WIDTH = BRANCH_WIDTH
SB_HEADS = BRANCH_WIDTH // HEAD_DIM
SB_WIDTH = SB_HEADS * HEAD_DIM
SB_BLOCK = 128
RW_HEADS = BRANCH_WIDTH // HEAD_DIM
RW_WIDTH = RW_HEADS * HEAD_DIM
RW_DECAY_LORA = 64
RW_A_LORA = 64
RW_GATE_LORA = 128
RW_GN_EPS = 64e-5
RW_DECAY_SCALE = math.exp(-0.5)
SG_GROUPS = 4
SG_WIDTH = BRANCH_WIDTH
SG_GROUP_WIDTH = SG_WIDTH // SG_GROUPS
SG_CHUNK = 128
D_FF = ((8 * D_MODEL // 3 + 127) // 128) * 128
RMS_EPS = 1e-6
LN_EPS = 1e-5

SC_OFF = 0
SB_OFF = SC_OFF + 3 * SC_WIDTH
RW_OFF = SB_OFF + 3 * SB_WIDTH
RW_COLS = 3 * RW_WIDTH + RW_DECAY_LORA + RW_A_LORA + RW_GATE_LORA
SG_OFF = RW_OFF + RW_COLS
GATE_OFF = SG_OFF + 2 * SG_WIDTH
IN_COLS = GATE_OFF + N_BRANCH * D_MODEL


def rms_norm(x, g):
    xf = x.astype(jnp.float32)
    y = xf * lax.rsqrt(jnp.mean(xf * xf, axis=-1, keepdims=True) + RMS_EPS)
    return (y * g.astype(jnp.float32)).astype(x.dtype)

def layer_norm(x, g, b):
    xf = x.astype(jnp.float32)
    mu = jnp.mean(xf, axis=-1, keepdims=True)
    var = jnp.mean(jnp.square(xf - mu), axis=-1, keepdims=True)
    y = (xf - mu) * lax.rsqrt(var + LN_EPS) * g.astype(jnp.float32) + b.astype(jnp.float32)
    return y.astype(x.dtype)

def causal_dwconv(x, w):
    k = w.shape[0]
    t = x.shape[1]
    xp = jnp.pad(x, ((0, 0), (k - 1, 0), (0, 0)))
    out = xp[:, 0:t] * w[0]
    for i in range(1, k):
        out = out + xp[:, i:i + t] * w[i]
    return out

def token_shift(x):
    return jnp.pad(x, ((0, 0), (1, 0), (0, 0)))[:, :-1]

def short_conv_mixer(z, conv_w):
    b_gate, c_gate, xin = jnp.split(z, 3, axis=-1)
    return b_gate * causal_dwconv(c_gate * xin, conv_w)

def stick_breaking_attention(q, k, v):
    bsz, t, h, dh = q.shape
    nb = t // SB_BLOCK
    scale = 1.0 / math.sqrt(dh)
    qb = q.reshape(bsz, nb, SB_BLOCK, h, dh).transpose(1, 0, 3, 2, 4)
    kh = k.transpose(0, 2, 1, 3)
    vh = v.transpose(0, 2, 1, 3)
    kpos = jnp.arange(t)

    def block(args):
        qi, bi = args
        z = jnp.einsum('bhqd,bhkd->bhqk', qi, kh).astype(jnp.float32) * scale
        qpos = bi * SB_BLOCK + jnp.arange(SB_BLOCK)
        mask = kpos[None, :] < qpos[:, None]
        log_beta = jax.nn.log_sigmoid(z)
        log_keep = jnp.where(mask, log_beta - z, 0.0)
        suffix = lax.cumsum(log_keep, axis=3, reverse=True) - log_keep
        attn = jnp.where(mask, jnp.exp(log_beta + suffix), 0.0)
        return jnp.einsum('bhqk,bhkd->bhqd', attn.astype(vh.dtype), vh)

    out = lax.map(block, (qb, jnp.arange(nb)))
    return out.transpose(1, 0, 3, 2, 4).reshape(bsz, t, h * dh)

def rwkv7_scan(r, w, k, v, a_vec, b_vec):
    bsz, t, h, n = r.shape

    def step(s, inp):
        r_t, w_t, k_t, v_t, a_t, b_t = inp
        sa = jnp.einsum('bhvk,bhk->bhv', s, a_t)
        s = s * w_t[:, :, None, :] + sa[..., None] * b_t[:, :, None, :] + v_t[..., None] * k_t[:, :, None, :]
        return s, jnp.einsum('bhvk,bhk->bhv', s, r_t)

    xs = tuple(u.astype(jnp.float32).transpose(1, 0, 2, 3) for u in (r, w, k, v, a_vec, b_vec))
    s0 = jnp.zeros((bsz, h, n, n), jnp.float32)
    _, y = lax.scan(step, s0, xs)
    return y.transpose(1, 0, 2, 3)

def rwkv7_mixer(z, mu, w0, w2, a0, a2, g2, k_k, k_a, r_k, gn_g, gn_b):
    bsz, t, _ = z.shape
    z = z + (token_shift(z) - z) * mu
    c0, c1, c2 = RW_WIDTH, 2 * RW_WIDTH, 3 * RW_WIDTH
    c3, c4 = c2 + RW_DECAY_LORA, c2 + RW_DECAY_LORA + RW_A_LORA
    r, k, v = z[..., :c0], z[..., c0:c1], z[..., c1:c2]
    xw, xa, xg = z[..., c2:c3], z[..., c3:c4], z[..., c4:]
    decay = jnp.exp(-RW_DECAY_SCALE * jax.nn.sigmoid((w0 + jnp.tanh(xw) @ w2).astype(jnp.float32)))
    a = jax.nn.sigmoid(a0 + xa @ a2)
    g = jax.nn.sigmoid(xg) @ g2
    hs = (bsz, t, RW_HEADS, HEAD_DIM)
    kk = (k * k_k).reshape(hs).astype(jnp.float32)
    kk = kk / jnp.maximum(jnp.sqrt(jnp.sum(kk * kk, axis=-1, keepdims=True)), 1e-12)
    k = k * (1.0 + (a - 1.0) * k_a)
    rh, kh, vh, ah = r.reshape(hs), k.reshape(hs), v.reshape(hs), a.reshape(hs)
    y = rwkv7_scan(rh, decay.reshape(hs), kh, vh, -kk, kk * ah.astype(jnp.float32))
    mean = jnp.mean(y, axis=-1, keepdims=True)
    var = jnp.mean(jnp.square(y - mean), axis=-1, keepdims=True)
    y = ((y - mean) * lax.rsqrt(var + RW_GN_EPS)).reshape(bsz, t, RW_WIDTH)
    y = y * gn_g.astype(jnp.float32) + gn_b.astype(jnp.float32)
    bonus = jnp.sum((rh * kh * r_k).astype(jnp.float32), axis=-1, keepdims=True) * vh.astype(jnp.float32)
    y = (y + bonus.reshape(bsz, t, RW_WIDTH)).astype(z.dtype)
    return y * g

def spatial_gating(z, ln_g, ln_b, w_s, b_s):
    bsz, t, _ = z.shape
    u, v = jnp.split(jax.nn.gelu(z), 2, axis=-1)
    v = layer_norm(v, ln_g, ln_b)
    vb = v.reshape(bsz, t // SG_CHUNK, SG_CHUNK, SG_GROUPS, SG_GROUP_WIDTH)
    w_causal = jnp.tril(w_s)
    mixed = jnp.einsum('gts,bnsgc->bntgc', w_causal, vb) + b_s.T[:, :, None]
    return u * mixed.reshape(bsz, t, SG_WIDTH)

def hybrid_mixer(h, w_in, gate_b, sc_conv_w, sc_out, sb_out, rw_mu, rw_w0, rw_w2, rw_a0, rw_a2,
                 rw_g2, rw_k_k, rw_k_a, rw_r_k, rw_gn_g, rw_gn_b, rw_out, sg_ln_g, sg_ln_b,
                 sg_w, sg_b, sg_out, w_o):
    bsz, t, _ = h.shape
    proj = h @ w_in
    y_a = short_conv_mixer(proj[..., SC_OFF:SB_OFF], sc_conv_w)
    q, k, v = jnp.split(proj[..., SB_OFF:RW_OFF], 3, axis=-1)
    hs = (bsz, t, SB_HEADS, HEAD_DIM)
    y_b = stick_breaking_attention(q.reshape(hs), k.reshape(hs), v.reshape(hs))
    y_c = rwkv7_mixer(proj[..., RW_OFF:SG_OFF], rw_mu, rw_w0, rw_w2, rw_a0, rw_a2, rw_g2,
                      rw_k_k, rw_k_a, rw_r_k, rw_gn_g, rw_gn_b)
    y_d = spatial_gating(proj[..., SG_OFF:GATE_OFF], sg_ln_g, sg_ln_b, sg_w, sg_b)
    gates = jax.nn.sigmoid((proj[..., GATE_OFF:] + gate_b).astype(jnp.float32)).astype(h.dtype)
    gates = gates.reshape(bsz, t, N_BRANCH, D_MODEL)
    merged = (gates[:, :, 0] * (y_a @ sc_out) + gates[:, :, 1] * (y_b @ sb_out)
              + gates[:, :, 2] * (y_c @ rw_out) + gates[:, :, 3] * (y_d @ sg_out))
    return merged @ w_o

def conv_glu_ffn(h, w_up, conv_w, w_down):
    up = causal_dwconv(h @ w_up, conv_w)
    gate, val = jnp.split(up, 2, axis=-1)
    return (jax.nn.silu(gate) * val) @ w_down

def first_inputs(seed: int = 0) -> dict:
    key = jax.random.key(seed)
    keys = iter(jax.random.split(key, 40))
    f32 = jnp.float32
    L = DEPTH

    def nrm(shape, scale):
        return jax.random.normal(next(keys), shape, f32) * scale

    return {
        "x": nrm((BATCH, SEQ, D_MODEL), 1.0),
        "mix_norm_g": 1.0 + nrm((L, D_MODEL), 0.05),
        "w_in": nrm((L, D_MODEL, IN_COLS), D_MODEL ** -0.5),
        "gate_b": nrm((L, N_BRANCH * D_MODEL), 0.1),
        "sc_conv_w": nrm((L, CONV_WIDTH, SC_WIDTH), CONV_WIDTH ** -0.5),
        "sc_out": nrm((L, SC_WIDTH, D_MODEL), SC_WIDTH ** -0.5),
        "sb_out": nrm((L, SB_WIDTH, D_MODEL), SB_WIDTH ** -0.5),
        "rw_mu": jax.random.uniform(next(keys), (L, RW_COLS), f32),
        "rw_w0": nrm((L, RW_WIDTH), 0.5),
        "rw_w2": nrm((L, RW_DECAY_LORA, RW_WIDTH), 0.1),
        "rw_a0": nrm((L, RW_WIDTH), 0.1),
        "rw_a2": nrm((L, RW_A_LORA, RW_WIDTH), 0.1),
        "rw_g2": nrm((L, RW_GATE_LORA, RW_WIDTH), RW_GATE_LORA ** -0.5),
        "rw_k_k": 0.85 + nrm((L, RW_WIDTH), 0.05),
        "rw_k_a": 1.0 + nrm((L, RW_WIDTH), 0.05),
        "rw_r_k": nrm((L, RW_HEADS, HEAD_DIM), 0.1),
        "rw_gn_g": 1.0 + nrm((L, RW_WIDTH), 0.05),
        "rw_gn_b": nrm((L, RW_WIDTH), 0.01),
        "rw_out": nrm((L, RW_WIDTH, D_MODEL), RW_WIDTH ** -0.5),
        "sg_ln_g": 1.0 + nrm((L, SG_WIDTH), 0.05),
        "sg_ln_b": nrm((L, SG_WIDTH), 0.01),
        "sg_w": nrm((L, SG_GROUPS, SG_CHUNK, SG_CHUNK), 0.05),
        "sg_b": 1.0 + nrm((L, SG_GROUPS, SG_CHUNK), 0.05),
        "sg_out": nrm((L, SG_WIDTH, D_MODEL), SG_WIDTH ** -0.5),
        "w_o": nrm((L, D_MODEL, D_MODEL), 0.5 * D_MODEL ** -0.5),
        "ffn_norm_g": 1.0 + nrm((L, D_MODEL), 0.05),
        "w_up": nrm((L, D_MODEL, 2 * D_FF), D_MODEL ** -0.5),
        "ffn_conv_w": nrm((L, CONV_WIDTH, 2 * D_FF), CONV_WIDTH ** -0.5),
        "w_down": nrm((L, D_FF, D_MODEL), 0.5 * D_FF ** -0.5),
        "final_norm_g": 1.0 + nrm((D_MODEL,), 0.05),
    }

def first_block(x, mix_norm_g, w_in, gate_b, sc_conv_w, sc_out, sb_out, rw_mu, rw_w0, rw_w2,
              rw_a0, rw_a2, rw_g2, rw_k_k, rw_k_a, rw_r_k, rw_gn_g, rw_gn_b, rw_out, sg_ln_g,
              sg_ln_b, sg_w, sg_b, sg_out, w_o, ffn_norm_g, w_up, ffn_conv_w, w_down,
              final_norm_g):
    for l in range(DEPTH):
        h = rms_norm(x, mix_norm_g[l])
        x = x + hybrid_mixer(h, w_in[l], gate_b[l], sc_conv_w[l], sc_out[l], sb_out[l], rw_mu[l],
                             rw_w0[l], rw_w2[l], rw_a0[l], rw_a2[l], rw_g2[l], rw_k_k[l],
                             rw_k_a[l], rw_r_k[l], rw_gn_g[l], rw_gn_b[l], rw_out[l], sg_ln_g[l],
                             sg_ln_b[l], sg_w[l], sg_b[l], sg_out[l], w_o[l])
        h = rms_norm(x, ffn_norm_g[l])
        x = x + conv_glu_ffn(h, w_up[l], ffn_conv_w[l], w_down[l])
    return rms_norm(x, final_norm_g)


DEPTH_2 = 2

N_A = DEPTH_2 // 2
N_B = DEPTH_2 - N_A
MIX_WIDTH = D_MODEL
MEM_LEN = 256
MEM_HEADS = 4
MEM_WIDTH = MEM_HEADS * HEAD_DIM
MAIN_WIDTH = MIX_WIDTH - MEM_WIDTH
POOL_WINDOWS = (2, 4, 8, 16)
POOL_GROUPS = len(POOL_WINDOWS)
POOL_GROUP_DIM = MAIN_WIDTH // POOL_GROUPS
SWA_Q_HEADS = MAIN_WIDTH // HEAD_DIM
SWA_KV_HEADS = 4
SWA_GROUP = SWA_Q_HEADS // SWA_KV_HEADS
KV_WIDTH = 2 * SWA_KV_HEADS * HEAD_DIM
MEM_KV_WIDTH = 2 * MEM_WIDTH
WINDOW = 128
BLOCK = 128
D_FF_2 = 4 * D_MODEL
EPS = 1e-6


def rmsnorm(x, g):
    xf = x.astype(jnp.float32)
    y = xf * lax.rsqrt(jnp.mean(xf * xf, axis=-1, keepdims=True) + EPS)
    return (y * g.astype(jnp.float32)).astype(x.dtype)

def alibi_slopes(n):
    return jnp.exp2(-8.0 * jnp.arange(1, n + 1, dtype=jnp.float32) / n)

def pool_mixer(u, pool_w, pool_scale):
    B, S, _ = u.shape
    uf = u.astype(jnp.float32).reshape(B, S, POOL_GROUPS, POOL_GROUP_DIM)
    csum = jnp.concatenate([jnp.zeros((B, 1, POOL_GROUPS, POOL_GROUP_DIM), jnp.float32),
                            jnp.cumsum(uf, axis=1)], axis=1)
    win = jnp.array(POOL_WINDOWS, jnp.int32)
    t = jnp.arange(S, dtype=jnp.int32)[:, None]
    lo = jnp.maximum(t + 1 - win[None, :], 0)
    cnt = jnp.minimum(t + 1, win[None, :]).astype(jnp.float32)
    window_sum = csum[:, 1:] - csum[:, lo, jnp.arange(POOL_GROUPS)[None, :]]
    d = (window_sum / cnt[None, :, :, None] - uf).astype(u.dtype)
    mixed = jnp.einsum('bsgc,gcd->bsgd', d, pool_w)
    return mixed.reshape(B, S, MAIN_WIDTH) * pool_scale

def swa_sink_attention(q, k, v, sinks):
    B, S = q.shape[0], q.shape[1]
    nb = S // BLOCK
    qb = q.reshape(B, nb, BLOCK, SWA_KV_HEADS, SWA_GROUP, HEAD_DIM)

    def with_prev(a):
        ab = a.reshape(B, nb, BLOCK, SWA_KV_HEADS, HEAD_DIM)
        prev = jnp.pad(ab[:, :-1], ((0, 0), (1, 0), (0, 0), (0, 0), (0, 0)))
        return jnp.concatenate([prev, ab], axis=2)

    kb, vb = with_prev(k), with_prev(v)
    s = jnp.einsum('bnqkgd,bnpkd->bnkgqp', qb, kb).astype(jnp.float32) * (HEAD_DIM ** -0.5)
    blk = jnp.arange(nb, dtype=jnp.int32)[:, None] * BLOCK
    qpos = blk + jnp.arange(BLOCK, dtype=jnp.int32)[None, :]
    kpos = blk - BLOCK + jnp.arange(2 * BLOCK, dtype=jnp.int32)[None, :]
    dist = qpos[:, :, None] - kpos[:, None, :]
    valid = (dist >= 0) & (dist < WINDOW) & (kpos[:, None, :] >= 0)
    slopes = alibi_slopes(SWA_Q_HEADS).reshape(SWA_KV_HEADS, SWA_GROUP)
    s = s - slopes[None, None, :, :, None, None] * dist.astype(jnp.float32)[None, :, None, None]
    s = jnp.where(valid[None, :, None, None], s, jnp.finfo(jnp.float32).min)
    sink = sinks.astype(jnp.float32).reshape(SWA_KV_HEADS, SWA_GROUP)[None, None, :, :, None, None]
    m = jnp.maximum(jnp.max(s, axis=-1, keepdims=True), sink)
    e = jnp.exp(s - m)
    p = e / (jnp.sum(e, axis=-1, keepdims=True) + jnp.exp(sink - m))
    o = jnp.einsum('bnkgqp,bnpkd->bnqkgd', p.astype(vb.dtype), vb)
    return o.reshape(B, S, SWA_Q_HEADS * HEAD_DIM)

def memory_attention(q, mk, mv):
    s = jnp.einsum('bshd,bmhd->bhsm', q, mk).astype(jnp.float32) * (HEAD_DIM ** -0.5)
    p = jax.nn.softmax(s, axis=-1)
    o = jnp.einsum('bhsm,bmhd->bshd', p.astype(mv.dtype), mv)
    return o.reshape(q.shape[0], q.shape[1], MEM_WIDTH)

def sq_relu_mlp(x, w_up, w_down):
    h = jax.nn.relu(x @ w_up)
    return (h * h) @ w_down

def second_inputs(seed: int = 0) -> dict:
    key = jax.random.key(seed)
    ks = jax.random.split(key, 20)
    f32 = jnp.float32

    def nrm(k, shape, scale):
        return jax.random.normal(k, shape, f32) * scale

    def gain(k, shape):
        return 1.0 + 0.02 * jax.random.normal(k, shape, f32)

    return {
        "x": nrm(ks[0], (BATCH, SEQ, D_MODEL), 1.0),
        "mem": nrm(ks[1], (BATCH, MEM_LEN, D_MODEL), 1.0),
        "norm_mix": gain(ks[2], (DEPTH_2, D_MODEL)),
        "w_in": nrm(ks[3], (DEPTH_2, D_MODEL, MIX_WIDTH), D_MODEL ** -0.5),
        "pool_w": nrm(ks[4], (N_A, POOL_GROUPS, POOL_GROUP_DIM, POOL_GROUP_DIM), POOL_GROUP_DIM ** -0.5),
        "pool_scale": gain(ks[5], (N_A, MAIN_WIDTH)),
        "kv_norm": gain(ks[6], (D_MODEL,)),
        "w_kv": nrm(ks[7], (D_MODEL, KV_WIDTH), D_MODEL ** -0.5),
        "k_norm": gain(ks[8], (HEAD_DIM,)),
        "q_norm": gain(ks[9], (N_B, HEAD_DIM)),
        "sinks": nrm(ks[10], (N_B, SWA_Q_HEADS), 0.5),
        "mem_norm": gain(ks[11], (DEPTH_2, D_MODEL)),
        "w_mem_kv": nrm(ks[12], (DEPTH_2, D_MODEL, MEM_KV_WIDTH), D_MODEL ** -0.5),
        "mem_q_norm": gain(ks[13], (DEPTH_2, HEAD_DIM)),
        "mem_k_norm": gain(ks[14], (DEPTH_2, HEAD_DIM)),
        "w_out": nrm(ks[15], (DEPTH_2, MIX_WIDTH, D_MODEL), MIX_WIDTH ** -0.5),
        "norm_mlp": gain(ks[16], (DEPTH_2, D_MODEL)),
        "w_up": nrm(ks[17], (DEPTH_2, D_MODEL, D_FF_2), D_MODEL ** -0.5),
        "w_down": nrm(ks[18], (DEPTH_2, D_FF_2, D_MODEL), D_FF_2 ** -0.5),
    }

def second_block(x, mem, norm_mix, w_in, pool_w, pool_scale, kv_norm, w_kv, k_norm, q_norm, sinks,
              mem_norm, w_mem_kv, mem_q_norm, mem_k_norm, w_out, norm_mlp, w_up, w_down):
    B, S, _ = x.shape
    h = x
    k_shared = None
    v_shared = None
    for l in range(DEPTH_2):
        if l == N_A:
            kv = rmsnorm(h, kv_norm) @ w_kv
            k_shared = rmsnorm(kv[..., :KV_WIDTH // 2].reshape(B, S, SWA_KV_HEADS, HEAD_DIM), k_norm)
            v_shared = kv[..., KV_WIDTH // 2:].reshape(B, S, SWA_KV_HEADS, HEAD_DIM)

        proj = rmsnorm(h, norm_mix[l]) @ w_in[l]
        main, mq = proj[..., :MAIN_WIDTH], proj[..., MAIN_WIDTH:]
        if l < N_A:
            main_out = pool_mixer(main, pool_w[l], pool_scale[l])
        else:
            j = l - N_A
            q = rmsnorm(main.reshape(B, S, SWA_Q_HEADS, HEAD_DIM), q_norm[j])
            main_out = swa_sink_attention(q, k_shared, v_shared, sinks[j])

        mkv = rmsnorm(mem, mem_norm[l]) @ w_mem_kv[l]
        mk = rmsnorm(mkv[..., :MEM_WIDTH].reshape(B, MEM_LEN, MEM_HEADS, HEAD_DIM), mem_k_norm[l])
        mv = mkv[..., MEM_WIDTH:].reshape(B, MEM_LEN, MEM_HEADS, HEAD_DIM)
        mqh = rmsnorm(mq.reshape(B, S, MEM_HEADS, HEAD_DIM), mem_q_norm[l])
        mem_out = memory_attention(mqh, mk, mv)

        h = h + jnp.concatenate([main_out, mem_out], axis=-1) @ w_out[l]
        h = h + sq_relu_mlp(rmsnorm(h, norm_mlp[l]), w_up[l], w_down[l])
    return h


def setup_inputs(seed=0):
    out = dict(first_inputs(seed))
    for name, value in second_inputs(seed + 1).items():
        if name != "x":
            out[name + "_2"] = value
    return out


def reference(
    x, mix_norm_g, w_in, gate_b, sc_conv_w, sc_out, sb_out, rw_mu, rw_w0, rw_w2, rw_a0, rw_a2,
    rw_g2, rw_k_k, rw_k_a, rw_r_k, rw_gn_g, rw_gn_b, rw_out, sg_ln_g, sg_ln_b, sg_w, sg_b,
    sg_out, w_o, ffn_norm_g, w_up, ffn_conv_w, w_down, final_norm_g, mem_2, norm_mix_2, w_in_2,
    pool_w_2, pool_scale_2, kv_norm_2, w_kv_2, k_norm_2, q_norm_2, sinks_2, mem_norm_2,
    w_mem_kv_2, mem_q_norm_2, mem_k_norm_2, w_out_2, norm_mlp_2, w_up_2, w_down_2,
):
    x = first_block(
        x, mix_norm_g, w_in, gate_b, sc_conv_w, sc_out, sb_out, rw_mu, rw_w0, rw_w2, rw_a0,
        rw_a2, rw_g2, rw_k_k, rw_k_a, rw_r_k, rw_gn_g, rw_gn_b, rw_out, sg_ln_g, sg_ln_b, sg_w,
        sg_b, sg_out, w_o, ffn_norm_g, w_up, ffn_conv_w, w_down, final_norm_g,
    )
    return second_block(
        x, mem_2, norm_mix_2, w_in_2, pool_w_2, pool_scale_2, kv_norm_2, w_kv_2, k_norm_2,
        q_norm_2, sinks_2, mem_norm_2, w_mem_kv_2, mem_q_norm_2, mem_k_norm_2, w_out_2,
        norm_mlp_2, w_up_2, w_down_2,
    )


_drawn_inputs = setup_inputs


def setup_inputs(seed=0):
    import zlib

    import numpy as np

    out = dict(_drawn_inputs(seed))
    spreads = {}
    factors = {'gate_b': 3.319,
     'rw_w2': 3.731,
     'rw_a0': 6.818,
     'rw_k_k': 8.0,
     'rw_k_a': 6.116,
     'rw_gn_g': 6.726,
     'rw_gn_b': 8.0,
     'sg_ln_g': 8.0,
     'sg_ln_b': 29.939,
     'sg_b': 5.686,
     'norm_mix_2': 4.231,
     'pool_scale_2': 4.195,
     'kv_norm_2': 8.0,
     'k_norm_2': 21.74,
     'q_norm_2': 22.258,
     'mem_norm_2': 8.0,
     'mem_q_norm_2': 8.0,
     'mem_k_norm_2': 8.0,
     'sinks_2': 64.0,
     'norm_mlp_2': 5.162}
    for name, (base, spread) in spreads.items():
        noise = np.random.default_rng([zlib.crc32(name.encode()), seed]).standard_normal(out[name].shape)
        drawn = base * np.exp(spread * noise) if base else spread * noise
        out[name] = jnp.asarray(drawn.astype(out[name].dtype))
    for name, factor in factors.items():
        out[name] = (out[name] * factor).astype(out[name].dtype)
    return out
```

```python
import math
from contextlib import ExitStack

import numpy as np

import concourse.bass as bass
from concourse import mybir

F32 = mybir.dt.float32
F32R = mybir.dt.float32r
BF16 = mybir.dt.bfloat16
ALU = mybir.AluOpType
ACT = mybir.ActivationFunctionType
AX_X = mybir.AxisListType.X

P = 128
T = 256
D = 1024
KT = D // P
BW = 256
DFF1 = ((8 * D // 3 + 127) // 128) * 128
FT1 = DFF1 // P
DFF2 = 4 * D
NI1 = FT1 // 2
NI2 = DFF2 // P // 2
PT = 16
SLOTS = 3
DECAY = math.exp(-0.5)
QH, KVH = 12, 4
PG, PGW = 4, 96
LN2 = math.log(2.0)

_ORDER = [("rw", 4), ("sc", 3), ("sg", 2), ("sb", 3),
          ("gate0", 4), ("out0", 1), ("gate1", 4), ("out1", 1), ("gate2", 4), ("out2", 1),
          ("gate3", 4), ("out3", 1), ("wo", 4), ("ffn", 3 * NI1),
          ("mkv0", 2), ("in0q", 1), ("in0m", 4), ("wout0", 4), ("ffn0", 2 * NI2),
          ("mkv1", 2), ("kv", 2), ("in1", 4), ("wout1", 4), ("ffn1", 2 * NI2)]
PAN = {}
_at = 0
for _n, _c in _ORDER:
    PAN[_n] = _at
    _at += _c
NPAN = _at
NARROW = PAN["in0m"]

_PCOLS = [("mix_g", 8), ("gate_b", 32), ("sc_w", 6), ("mu", 8), ("w0", 2), ("a0", 2), ("k_k", 2),
          ("k_a", 2), ("r_k", 2), ("gn_g", 2), ("gn_b", 2), ("ln_g", 2), ("ln_b", 2), ("ffn_g", 8),
          ("conv", 6 * FT1), ("fin_g", 8), ("mix2_g", 16), ("pool_s", 6), ("kv_g", 8), ("k_g", 1),
          ("q_g", 1), ("mem_g", 16), ("mq_g", 2), ("mk_g", 2), ("mlp_g", 16), ("sinks", 12)]
PC = {}
_at = 0
for _n, _c in _PCOLS:
    PC[_n] = _at
    _at += _c
NPC = _at

_CCOLS = [("ident", 128), ("ones", 128), ("bones", 128), ("suffix", 128), ("strict", 128),
          ("incl", 128), ("dist", 384), ("count", 64), ("eps", 8)]
CC = {}
_at = 0
for _n, _c in _CCOLS:
    CC[_n] = _at
    _at += _c
NCC = _at
EPS6, EPS5, EPSG, KKB, ONE = range(5)
LEVELS = (1, 2, 4, 8, 16, 32, 64)


def shape_constants():
    c = np.zeros((P, NCC), np.float32)
    r = np.arange(P)

    def put(name, a):
        c[:, CC[name]:CC[name] + a.shape[1]] = a

    put("ident", np.eye(P))
    put("ones", np.ones((P, P)))
    put("bones", (r[:, None] // 64 == r[None, :] // 64) * 1.0)
    put("suffix", (r[:, None] >= r[None, :]) * 1.0)
    put("strict", (r[:, None] < r[None, :]) * 1.0)
    put("incl", (r[:, None] <= r[None, :]) * 1.0)
    key = np.arange(2 * P)[None, :]
    own = r[:, None] - r[None, :]
    both = r[:, None] + P - key
    put("dist", np.concatenate([np.where(own >= 0, -own, -1e32),
                                np.where((both >= 0) & (both < P), -both, -1e32)], 1))
    t = np.arange(16)
    put("count", np.tile(np.concatenate([1.0 / np.minimum(t + 1, w) for w in (2, 4, 8, 16)])[None], (P, 1)))
    e = np.zeros((P, 8))
    e[:, EPS6], e[:, EPS5], e[:, EPSG], e[:, KKB], e[:, ONE] = 1e-6, 1e-5, 64e-5, 10 * LN2, 1.0
    put("eps", e)
    lv = np.zeros((P, len(LEVELS), P), np.float32)
    for i, b in enumerate(LEVELS):
        lv[:, i] = ((r[:, None] // (2 * b) == r[None, :] // (2 * b)) & (r[:, None] % (2 * b) < b)
                    & (r[None, :] % (2 * b) >= b))
    return c, lv


def build(nc, A):
    ctx = ExitStack()
    sems = {}

    def S(name):
        if name not in sems:
            sems[name] = ctx.enter_context(nc.semaphore(name))
        return sems[name]

    base = 16512
    top = [base]

    def place(name, shape, dt=F32, at=None):
        size = int(np.prod(shape[1:])) * (2 if dt == BF16 else 4)
        size = (size + 31) // 32 * 32
        off = top[0] if at is None else at
        h = nc.alloc_sbuf_tensor_at(name, shape, dt, offset=off)
        if at is None:
            top[0] += size
        h_end[name] = off + size
        return h

    h_end = {}
    K = 1024
    raw = place("raw", [P, SLOTS, PT * P])
    whi = place("whi", [P, SLOTS, PT * P], F32R)
    wlo = place("wlo", [P, SLOTS, PT * P], F32R)
    xh = place("xh", [P, KT, T], F32R)
    xl = place("xl", [P, KT, T], F32R)
    x = place("x", [P, KT, T])
    cst = place("cst", [P, NCC])
    lvl = place("lvl", [P, len(LEVELS), P], BF16)
    par = place("par", [P, NPC])
    neg = place("neg", [P, 36])
    gq8 = place("gq8", [P, 4])
    rstd = place("rstd", [P, T])
    arena = top[0]

    lora = place("lora", [P, 2, T])
    sgw = place("sgw", [P, 4, P])
    z_rw = place("z_rw", [P, 8, T + 1])
    mt1 = place("mt1", [P, 8, P], at=h_end["sgw"])
    mx = place("mx", [P, 8, P], at=h_end["mt1"])
    zs = place("zs", [P, 8, T])
    y = place("y", [P, 2, T], at=h_end["zs"] - 8 * K)
    b0 = place("b0", [P, 2, 4, 64], at=h_end["zs"] - 6 * K)
    uu = place("uu", [P, 2, 4, 64], at=h_end["zs"] - 2 * K)
    z_sb = place("z_sb", [P, 6, T])
    r4 = top[0]
    gm = place("gm", [P, 8, 4, P])
    z_sc = place("z_sc", [P, 6, T], at=r4)
    ucv = place("ucv", [P, 2, T + 2], at=r4 + 6 * K)
    ycv = place("ycv", [P, 2, T], at=h_end["ucv"])
    z_sg = place("z_sg", [P, 4, T], at=h_end["ycv"])
    sig = place("sig", [P, KT, T])
    sgt = place("sgt", [P, 4, T], at=h_end["sig"] - 8 * K)
    sgv = place("sgv", [P, 2, T], at=h_end["sig"] - 4 * K)
    sgn = place("sgn", [P, 2, T], at=h_end["sig"] - 2 * K)
    merged = place("merged", [P, KT, T])
    wk = place("wk", [P, KT, T], at=h_end["merged"] - 8 * K)
    cum = place("cum", [P, 4, P + 1])
    em = place("em", [P, 4, P + 1])
    ei = place("ei", [P, 4, P])
    ew = place("ew", [P, 4, T])
    mxt = place("mxt", [P, 8, P], at=h_end["merged"])
    mnt = place("mnt", [P, 8, P], at=h_end["em"])
    kk = place("kk", [P, 2, T])
    sbv = place("sbv", [P, 2, T], at=h_end["kk"] - 2 * K)
    ar = place("ar", [P, 4, 2, P])
    bt = place("bt", [P, 4, P])
    kt = place("kt", [P, 4, P])
    kp = place("kp", [P, 2, T])
    bkn = place("bkn", [P, 4, P])
    e2 = place("e2", [P, 2, T], at=h_end["bkn"] - 2 * K)
    vn = place("vn", [P, 2, T])
    bon = place("bon", [P, 2, T])
    gg = place("gg", [P, 2, T])
    st = place("st", [P, 2, 64])
    esc = place("esc", [P, 2])
    mid = place("mid", [P, 4, 1])
    z3 = place("z3", [P, 3 * P])
    l3 = place("l3", [P, 3 * P])
    ysq = place("ysq", [P, 2, T], at=h_end["em"])
    yr = place("yr", [P, 2, T], at=h_end["em"] + 2 * K)
    hh1 = place("hh1", [P, 2, 2, T], F32R)
    hl1 = place("hl1", [P, 2, 2, T], F32R)
    sgb = place("sgb", [1, 4 * P], at=h_end["mid"])

    top[0] = arena
    mh = place("mh", [P, KT, T], F32R)
    ml = place("ml", [P, KT, T], F32R)
    mem = place("mem", [P, KT, T])
    mwk = place("mwk", [P, KT, T])
    at16 = arena + 16 * K
    ffn = top[0]
    upad = place("upad", [P, 2, 2, T + 2])
    cv = place("cv", [P, 2, 2, T])
    sgm = place("sgm", [P, 2, T])
    hid = place("hid", [P, 3, 2, T])
    rel = place("rel", [P, 3, 2, T])
    hh = place("hh", [P, 3, 2, T], F32R)
    hl = place("hl", [P, 3, 2, T], F32R)
    mrstd = place("mrstd", [P, T])
    poolw = place("poolw", [PGW, PG, 2, 2 * PGW])
    l0 = top[0]
    top[0] = ffn
    mk = place("mk", [P, 2, T])
    mv = place("mv", [P, 2, T])
    mvn = place("mvn", [P, 2, T])
    mq = place("mq", [P, 2, T])
    hsq = place("hsq", [P, 2, T])
    hy = place("hy", [P, 2, T])
    ht = place("ht", [P, 2, T])
    ha = place("ha", [P, 2, T])
    hmax = place("hmax", [P, 3, 24])
    wmax = place("wmax", [P, 3, 24])
    mat_end = top[0]
    pm0 = place("pm0", [P, 8, T], at=at16)
    ptm0 = place("ptm0", [P, 4, 2, T], at=at16 + 8 * K)
    top[0] = l0
    zp = place("zp", [PGW, 8, T + 16])
    s2 = place("s2", [PGW, 8, T + 16])
    s4 = place("s4", [PGW, 8, T + 16])
    top[0] = mat_end
    qs = place("qs", [P, 6, T])
    ks = place("ks", [P, 2, T])
    ksw = place("ksw", [P, 2, T])
    vs = place("vs", [P, 2, T])
    vsn = place("vsn", [P, 2, T])
    ss = place("ss", [P, QH, 3 * P])
    pt = place("pt", [P, 8, 3 * P], at=at16)
    pm1 = place("pm1", [P, 8, T], at=h_end["vsn"])
    ptm1 = place("ptm1", [P, 4, 2, T], at=at16)
    wk2 = place("wk2", [P, KT, T], at=h_end["zp"])

    G = [nc.alloc_psum_tensor(f"G{i}", [P, 2, T], F32) for i in range(2)]
    DB = [nc.alloc_psum_tensor(f"D{i}", [P, 2, T], F32) for i in range(4)]
    M = [nc.alloc_psum_tensor(f"M{i}", [P, 2, T], F32) for i in range(2)]
    GR = [G[0], G[1], M[0]]

    def c(name, lo=0, n=P, rows=slice(0, P)):
        return cst[rows, CC[name] + lo:CC[name] + lo + n]

    def eps(i):
        return cst[:, CC["eps"] + i:CC["eps"] + i + 1]

    def pcol(name, i=0, rows=slice(0, P)):
        return par[rows, PC[name] + i:PC[name] + i + 1]

    def four(h):
        return h.rearrange("p j (c t) -> p (j c) t", c=2)

    def flat(bank):
        return bank[:, :, :].rearrange("p a b -> p (a b)")

    class Pan:

        def __init__(self, p, it=0, step=0):
            self.p0 = p
            self.p, self.slot, self.turn = p + it * step, p % SLOTS, p // SLOTS + it * (step // SLOTS)

    def reach(eng, sem, value):
        if not (isinstance(value, int) and value <= 0):
            eng.wait_ge(S(sem), value)

    class Own:

        def __init__(self, eng, sem):
            self.eng, self.sem, self.n = eng, S(sem), 0

        def __call__(self, ins):
            ins.then_inc(self.sem, 1)
            self.n += 1
            self.eng.wait_ge(self.sem, self.n)

    W = [("norm", 0)] + [("panel", PAN["rw"] + i) for i in range(4)]
    W += [("rw_low",), ("panel", PAN["sc"]), ("rw_gates",), ("panel", PAN["sc"] + 1), ("rw_cum",),
          ("panel", PAN["sc"] + 2), ("rw_key",), ("panel", PAN["sg"]), ("rw_mix",), ("panel", PAN["sg"] + 1),
          ("sc",), ("sg_gelu",), ("panel", PAN["sb"]), ("rw_turn",), ("panel", PAN["sb"] + 1),
          ("sg_mean",), ("panel", PAN["sb"] + 2), ("sg_var",), ("sg_turn",)]
    rw = [("rw_prod", i) for i in range(4)] + [("inv_first",)]
    for l in range(1, len(LEVELS)):
        rw += [("inv_t", l), ("inv_x", l)]
    rw += [("rw_rhs", 0), ("rw_sol", 0), ("rw_state",), ("rw_rhs", 1), ("rw_sol", 1), ("rw_out",),
           ("rw_gn1",), ("rw_gn2",)]
    sbs = [[("sg_mix",), ("sb_turn",)]]
    for h in range(4):
        sbs += [[("sb_z", h), ("sb_e", h)], [("sb_q", h), ("sb_a", h)], [("sb_o", h)]]
    fill = []
    for b in range(4):
        fill += [("panel", PAN[f"gate{b}"] + i) for i in range(4)] + ([("panel", PAN[f"out{b}"])] if b < 3 else [])
    for i, f in enumerate(fill):
        W.append(f)
        if i < len(sbs):
            W += sbs[i]
        W += rw[i * len(rw) // len(fill):(i + 1) * len(rw) // len(fill)]
    W += [("panel", PAN["out3"]), ("merge_split",)]
    W += [("mem_load",), ("mem_stat",)]
    W += [("panel", PAN["wo"]), ("panel", PAN["wo"] + 1), ("mem_norm", 0)]
    W += [("panel", PAN["wo"] + 2), ("panel", PAN["wo"] + 3), ("norm", 1), ("ffn", 0), ("norm", 2)]
    W += [("stat3",), ("panel", PAN["mkv0"]), ("panel", PAN["mkv0"] + 1), ("norm3",)]
    W += [("hn", 0), ("turn_mv", 0)]
    W += [("panel", PAN["in0q"]), ("hn", 1), ("mem_norm", 1)]
    W += [("panel", PAN["in0m"] + i) for i in range(4)]
    W += [("pool",), ("score_m", 0), ("turn_p", 0), ("pool_mm",), ("pv_m", 0)]
    W += [("panel", PAN["wout0"] + i) for i in range(4)] + [("norm", 4), ("ffn", 1)]
    W += [("stat5",), ("panel", PAN["mkv1"]), ("panel", PAN["mkv1"] + 1), ("norm5",),
          ("panel", PAN["kv"]), ("panel", PAN["kv"] + 1), ("norm5b",), ("hn", 2), ("turn_mv", 1),
          ("panel", PAN["in1"]), ("hn", 3), ("hn", 4), ("swap_k",), ("turn_v",)]
    W += [("panel", PAN["in1"] + 1), ("score_m", 1), ("panel", PAN["in1"] + 2), ("hn", 5), ("turn_p", 1),
          ("panel", PAN["in1"] + 3), ("hn", 6), ("pv_m", 1), ("hn", 7)]
    W += [("score_s", g) for g in range(3)] + [("pv_s", j) for j in range(6)]
    W += [("panel", PAN["wout1"] + i) for i in range(4)] + [("norm", 6), ("ffn", 2), ("store",)]

    WHAT = {}
    for name, n in _ORDER:
        for i in range(n):
            WHAT[PAN[name] + i] = (name, i)

    OUTS = ("out0", "out1", "out2", "out3")
    RES = ("wo", "wout0", "wout1")

    FF = [(NI1, 2, PAN["ffn"], 1), (NI2, 1, PAN["ffn0"], 3), (NI2, 1, PAN["ffn1"], 5)]

    XLN = {"rw": 4, "wo": 8, "ffn": 12, "in0q": 16, "wout0": 20, "ffn0": 24, "kv": 28, "wout1": 32, "ffn1": 36}
    RESN = {"wo": 0, "wout0": 3, "wout1": 5}
    FRES = [1, 4, 6]

    gbank, gcount = {}, {}
    use = 0
    for step in W:
        if step[0] == "panel":
            if WHAT[step[1]][0] in OUTS:
                use += 4
            elif WHAT[step[1]][0] not in RES:
                gbank[step[1]] = use % 2
                gcount[step[1]] = len(gcount) + 1
                use += 1

    def projected(eng, name, i):
        eng.wait_ge(S("g_act"), gcount[PAN[name] + i])

    def walk(eng, handlers):
        for step in W:
            if step[0] in handlers:
                handlers[step[0]](*step[1:])

    def ffn_walk(eng, f, up, down, done=None):
        ni, nu, p0, _ = FF[f]
        body = 3
        up(0, [Pan(p0 + u) for u in range(nu)], 0)

        def pair(i, it, step):
            at = p0 + nu + i * (nu + 1)
            idx = i + it * body
            up(idx + 1, [Pan(at + u, it, step) for u in range(nu)], i + 1)
            down(idx, Pan(at + nu, it, step), i, False)

        pair(0, 0, 0)
        n = (ni - 2) // body
        with eng.Fori(0, n) as it:
            for u in range(body):
                pair(1 + u, it, body * (nu + 1))
        if done is not None:
            done[0] = p0 + nu + (1 + n * body) * (nu + 1) + 2
        for i in range(1 + n * body, ni - 1):
            pair(i, 0, 0)
        down(ni - 1, Pan(p0 + ni * (nu + 1) - 1), ni - 1, True)

    block = ctx.enter_context(nc.Block())

    @block.sync
    def _(sp):
        def load(pan, src, width=PT * P):
            if not (isinstance(pan.p, int) and pan.p < SLOTS):
                sp.wait_ge(S("w_lo"), pan.p - SLOTS + 1)
            sp.dma_start(raw[:, pan.slot, 0:width], src).then_inc(S(f"w_land{pan.slot}"), 16)

        def run(lo, hi, skip):
            n = (hi - lo) // SLOTS
            with sp.Fori(0, n) as it:
                for u in range(SLOTS):
                    load(Pan(lo + u, it, SLOTS), A["wall"][bass.ds(it * SLOTS + (lo + u - skip), 1), :, :]
                         .rearrange("a p n -> p (a n)"))
            for p in range(lo + n * SLOTS, hi):
                load(Pan(p), A["wall"][p - skip])

        for p in range(SLOTS):
            load(Pan(p), A["wall"][p])
        run(SLOTS, NARROW, 0)
        for i in range(4):
            load(Pan(NARROW + i), A["wnarrow"][i], PT * PGW)
        run(NARROW + 4, NPAN, 4)
        for i in range(4):
            sp.wait_ge(S("x_ready"), 4 * 6 + i + 1)
            sp.dma_start(A["out"][:, 2 * i:2 * i + 2, :], x[:, 2 * i:2 * i + 2, :]).then_inc(S(f"stored{i}"), 16)
        for i in range(4):
            sp.wait_ge(S(f"stored{i}"), 16)

    @block.gpsimd
    def _(pool):
        def inv_mask(l):
            if l == 0:
                pool.wait_ge(S("ld_lvl"), 16)
                pool.wait_ge(S("rw_prod"), 8)
            else:
                reach(pool, "inv_T", l - 1)
                pool.wait_ge(S("rw_prod"), 8)
            if l == 1:
                pool.wait_ge(S("inv_x"), 1)
            nc.gpsimd.tensor_tensor(mnt[:], gm[:, :, 0, :], lvl[:, l:l + 1, :].broadcast_to([P, 8, P]),
                                    ALU.mult).then_inc(S("inv_n"), 1)

        def mem_load():
            pool.wait_ge(S("branch"), 4)
            pool.wait_ge(S("pe_panel"), PAN["out3"] + 1)
            pool.dma_start(mem[:], A["mem"]).then_inc(S("ld_mem"), 16)
            pool.dma_start(poolw[:], A["pool_w"]).then_inc(S("ld_pool"), 16)

        walk(pool, {"inv_first": lambda: inv_mask(0),
                    "inv_t": lambda l: inv_mask(l), "mem_load": mem_load})
        pool.wait_ge(S("ld_mem"), 16)
        pool.wait_ge(S("ld_pool"), 16)

    @block.tensor
    def _(pe):
        mm = nc.tensor.matmul
        ident, ones, bones = c("ident"), c("ones"), c("bones")
        used = {"g": 0}
        freed = {}
        gact = [0]
        gdve = [0]

        def free(bank):
            if bank in freed:
                pe.wait_ge(S(freed[bank][0]), freed[bank][1])

        def tile3(out, pan, q, width, hi, lo, start, stop, skip=False):
            w_h = whi[:, pan.slot, q * width:(q + 1) * width]
            w_l = wlo[:, pan.slot, q * width:(q + 1) * width]
            mm(out, w_h, hi, start=start, stop=False, skip_group_check=skip)
            mm(out, w_h, lo, start=False, stop=False, skip_group_check=skip)
            return mm(out, w_l, hi, start=False, stop=stop, skip_group_check=skip)

        pe.wait_ge(S("ld_cst"), 16)

        def norm_stat(n):
            free("M1")
            for i in range(4):
                pe.wait_ge(S("sq"), 4 * n + i + 1)
                for k in (2 * i, 2 * i + 1):
                    ins = mm(M[1][:, 0, :], ones, (wk if n == 0 else wk2)[:, k, :], start=k == 0, stop=k == KT - 1)
            ins.then_inc(S("stat"), 1)
            freed["M1"] = ("rs", n + 1)

        def panel(p):
            name, i = WHAT[p]
            pan = Pan(p)
            pe.wait_ge(S("w_lo"), p + 1)
            if name in OUTS:
                b = int(name[3])
                pe.wait_ge(S("branch"), b + 1)
                for i in range(4):
                    k = used["g"] % 2
                    used["g"] += 1
                    free(f"G{k}")
                    for n in (2 * i, 2 * i + 1):
                        for q in range(2):
                            ins = tile3(G[k][:, n % 2, :], pan, n * 2 + q, P, hh1[:, b % 2, q, :],
                                        hl1[:, b % 2, q, :], q == 0, q == 1)
                    if i < 3:
                        ins.then_inc(S("out_pair"), 1)
                    gdve[0] += 1
                    freed[f"G{k}"] = ("g_dve", gdve[0])
                ins.then_inc(S("pe_panel"), 1)
                return
            a_h, a_l = xh, xl
            if name[:3] == "mkv":
                pe.wait_ge(S("ml"), 1 + int(name[3]))
                a_h, a_l = mh, ml
            elif name == "in1":
                pe.wait_ge(S("ml"), 3)
                a_h, a_l = mh, ml
            elif i == 0 and name in XLN:
                pe.wait_ge(S("xl"), XLN[name])
            if name in RES:
                bank = f"D{i}"
                out = DB[i]
                free(bank)
            else:
                k = used["g"] % 2
                used["g"] += 1
                bank, out = f"G{k}", G[k]
                free(bank)
                gact[0] += 1
                freed[bank] = ("g_act", gact[0])
            narrow = name == "in0m"
            w = PGW if narrow else P
            for n in range(2):
                for k in range(KT):
                    ins = tile3(out[0:w, n, :], pan, n * KT + k, w, a_h[:, k, :], a_l[:, k, :], k == 0, k == KT - 1)
            ins.then_inc(S("pe_panel"), 1)
            if name in RES:
                freed[bank] = ("x_ready", 4 * RESN[name] + i + 1)

        def rw_gates():
            pe.wait_ge(S("ld_lora"), 16)
            pe.wait_ge(S("rw_e2"), 1)
            for j in range(2):
                mm(DB[0][:, j, :], lora[0:64, 0, j * P:(j + 1) * P], e2[0:64, 0, :])
            for j in range(2):
                mm(DB[1][:, j, :], lora[64:128, 0, j * P:(j + 1) * P], zs[64:128, 6, :])
            for j in range(2):
                ins = mm(DB[2][:, j, :], lora[:, 1, j * P:(j + 1) * P], e2[:, 1, :])
            ins.then_inc(S("rw_low"), 1)

        def rw_key():
            pe.wait_ge(S("rw_ksq"), 1)
            mm(DB[3][:, :, :], bones, bon[:, :, :]).then_inc(S("rw_kss"), 1)

        def rw_turn():
            pe.wait_ge(S("rw_low_read"), 1)
            pe.wait_ge(S("rw_kt"), 1)
            for ch in range(2):
                for j in range(2):
                    nc.tensor.transpose(DB[0][:, ch, j * P:(j + 1) * P], zs[:, 4 + j, ch * P:(ch + 1) * P], ident)
            for j in range(2):
                nc.tensor.transpose(DB[1][:, 0, j * P:(j + 1) * P], bt[:, 2 * j, :], ident)
            for j in range(2):
                nc.tensor.transpose(DB[1][:, 1, j * P:(j + 1) * P], kt[:, 2 * j, :], ident)
            mm(DB[2][:, :, :], bones, bon[:, :, :]).then_inc(S("rw_turned"), 1)

        def rw_prod(i):
            for m in (2 * i, 2 * i + 1):
                ch, h = divmod(m, 4)
                j, o = h // 2, 64 * (h % 2)
                bank = m % 2
                free(f"M{bank}")
                if m >= 2:
                    pe.wait_ge(S("rw_prod"), m - 1)
                jc = 2 * j + ch
                rhs = ar[o:o + 64, jc, :, :]
                mm(M[bank][:, 0, :], bt[o:o + 64, jc, :], rhs)
                mm(M[bank][:, 1, :], kt[o:o + 64, jc, :], rhs).then_inc(S("rw_gp"), 1)
                freed[f"M{bank}"] = ("rw_prod", m + 1)

        def inv_first():
            pe.wait_ge(S("inv_x"), 1)
            for g in range(2):
                free(f"M{g}")
                for m in range(4):
                    ins = nc.tensor.transpose(M[g][:, m // 2, (m % 2) * P:(m % 2 + 1) * P], mxt[:, 4 * g + m, :], ident)
            ins.then_inc(S("inv_t0"), 1)
            freed["M0"] = freed["M1"] = ("inv_x0", 1)

        def inv_t(l):
            pe.wait_ge(S("inv_n"), l + 1)
            pe.wait_ge(S("inv_x0"), 1)
            if l >= 2:
                pe.wait_ge(S("inv_x"), l)
            for g in range(2):
                free(f"M{g}")
                for m in range(4):
                    ins = mm(M[g][:, m // 2, (m % 2) * P:(m % 2 + 1) * P], mnt[:, 4 * g + m, :], mx[:, 4 * g + m, :])
            ins.then_inc(S("inv_T"), 1)
            freed["M0"] = freed["M1"] = ("inv_c", l)

        def inv_x(l):
            pe.wait_ge(S("inv_c"), l)
            if l == 1:
                pe.wait_ge(S("rw_bonus"), 1)
                pe.wait_ge(S("sg_y"), 1)
            for g in range(2):
                if l >= 2:
                    pe.wait_ge(S("inv_x"), l)
                for m in range(4):
                    ins = mm(DB[2 + g][:, m // 2, (m % 2) * P:(m % 2 + 1) * P], mt1[:, 4 * g + m, :], mxt[:, 4 * g + m, :])
            if l < len(LEVELS) - 1:
                for g in range(2):
                    for m in range(4):
                        ins = mm(M[g][:, m // 2, (m % 2) * P:(m % 2 + 1) * P], mxt[:, 4 * g + m, :], mt1[:, 4 * g + m, :])
                freed["M0"] = freed["M1"] = ("inv_x", l + 1)
            ins.then_inc(S("inv_p"), 1)

        def rw_rhs(ch):
            free("M0")
            free("M1")
            if ch == 0:
                pe.wait_ge(S("inv_x"), len(LEVELS))
            else:
                pe.wait_ge(S("rw_state"), 1)
            for h in range(4):
                j, o = h // 2, 64 * (h % 2)
                out = M[h % 2][:, 0, j * 64:(j + 1) * 64]
                ins = mm(out, gm[:, 4 * ch + h, 2, :], vn[:, ch, h * 64:(h + 1) * 64],
                         start=True, stop=ch == 0)
                if ch:
                    ins = mm(out, ar[o:o + 64, 2 * j + ch, 0, :], st[o:o + 64, j, :],
                             start=False, stop=True)
            ins.then_inc(S("rw_rhs"), 1)
            freed["M0"] = freed["M1"] = ("rw_b0", 2 * ch + 2)

        def rw_sol(ch):
            free("M0")
            for h in range(4):
                ins = mm(M[0][:, 0, h * 64:(h + 1) * 64], mxt[:, 4 * ch + h, :], b0[:, ch, h, :])
            ins.then_inc(S("rw_sol"), 1)
            freed["M0"] = ("rw_uu", ch + 1)

        def rw_state():
            pe.wait_ge(S("rw_uu"), 1)
            free("M1")
            for h in range(4):
                j, o = h // 2, 64 * (h % 2)
                out = M[1][o:o + 64, j, 0:64]
                mm(out, bkn[:, j, o:o + 64], uu[:, 0, h, :], start=True, stop=False)
                ins = mm(out, bkn[:, 2 + j, o:o + 64], vn[:, 0, h * 64:(h + 1) * 64], start=False, stop=True)
            ins.then_inc(S("rw_sp"), 1)
            freed["M1"] = ("rw_state", 1)

        def rw_out():
            pe.wait_ge(S("rw_uu"), 2)
            for h in range(4):
                j, o = h // 2, 64 * (h % 2)
                for ch in range(2):
                    out = DB[2][o:o + 64, j, ch * P:(ch + 1) * P]
                    mm(out, uu[:, ch, h, :], gm[:, 4 * ch + h, 1, :], start=True, stop=False)
                    ins = mm(out, vn[:, ch, h * 64:(h + 1) * 64], gm[:, 4 * ch + h, 3, :], start=False, stop=ch == 0)
                    if ch:
                        ins = mm(out, st[o:o + 64, j, :], ar[o:o + 64, 2 * j + ch, 1, :], start=False, stop=True)
            ins.then_inc(S("rw_yp"), 1)

        def rw_gn1():
            pe.wait_ge(S("rw_y"), 1)
            mm(DB[3][:, :, :], bones, y[:, :, :]).then_inc(S("rw_mean"), 1)

        def rw_gn2():
            pe.wait_ge(S("rw_ysq"), 1)
            mm(DB[3][:, :, :], bones, ysq[:, :, :]).then_inc(S("rw_var"), 1)
            freed.update({"D0": ("sb_out", 4), "D1": ("sb_arg", 4), "D2": ("rw_y", 1), "D3": ("rw_rs", 1)})

        def sg_sum(src, sem, need):
            pe.wait_ge(S(need[0]), need[1])
            for j in range(2):
                ins = mm(DB[3][:, 0, :], ones, src[:, j, :], start=j == 0, stop=j == 1)
            ins.then_inc(S(sem), 1)

        def sg_turn():
            pe.wait_ge(S("sg_norm"), 1)
            for n in range(2):
                for j in range(2):
                    ins = nc.tensor.transpose(DB[3][:, n, j * P:(j + 1) * P], sgv[:, j, n * P:(n + 1) * P], ident)
            ins.then_inc(S("sg_turned"), 1)

        def sg_mix():
            pe.wait_ge(S("sg_vn"), 1)
            pe.wait_ge(S("sg_tril"), 1)
            pe.wait_ge(S("ld_sgb"), 16)
            for n in range(2):
                for g in range(4):
                    j, o = g // 2, 64 * (g % 2)
                    out = DB[3][o:o + 64, j, n * P:(n + 1) * P]
                    mm(out, sgn[:, n, g * 64:(g + 1) * 64], sgw[:, g, :], start=True, stop=False)
                    ins = mm(out, ones[0:1, 0:64], sgb[0:1, g * P:(g + 1) * P], start=False, stop=True)
            ins.then_inc(S("sg_mixed"), 1)

        def sb_turn():
            projected(pe, "sb", 2)
            pe.wait_ge(S("rw_nat"), 1)
            for s_ in range(2):
                for j in range(2):
                    ins = nc.tensor.transpose(DB[1][:, s_, j * P:(j + 1) * P], z_sb[:, 4 + j, s_ * P:(s_ + 1) * P], ident)
            ins.then_inc(S("sb_turned"), 1)

        d0 = DB[0]
        d1 = DB[1]

        def sb_z(h):
            j, o = h // 2, 64 * (h % 2)
            if h:
                pe.wait_ge(S("sb_out"), h)
            mm(flat(d0)[:, 0:256], z_sb[o:o + 64, 2 + j, 0:P], z_sb[o:o + 64, j, :])
            mm(flat(d0)[:, 256:384], z_sb[o:o + 64, 2 + j, P:T], z_sb[o:o + 64, j, P:T]).then_inc(S("sb_zp"), 1)

        def sb_q(h):
            pe.wait_ge(S("sb_sp"), h + 1)
            if h == 0:
                pe.wait_ge(S("sb_vn"), 1)
            mm(flat(d1)[:, 0:256], c("suffix"), l3[:, 0:256], start=True, stop=False, skip_group_check=True)
            mm(flat(d1)[:, 128:256], ones, l3[:, 256:384], start=False, stop=True, skip_group_check=True)
            mm(flat(d1)[:, 256:384], c("suffix"), l3[:, 256:384], skip_group_check=True).then_inc(S("sb_qp"), 1)

        def sb_o(h):
            o = 64 * (h % 2)
            pe.wait_ge(S("sb_att"), h + 1)
            out = flat(d0)[o:o + 64, 0:256]
            mm(out, sbv[:, 0, h * 64:(h + 1) * 64], l3[:, 0:256], start=True, stop=False, skip_group_check=True)
            mm(out[:, 128:256], sbv[:, 1, h * 64:(h + 1) * 64], l3[:, 256:384], start=False, stop=True,
               skip_group_check=True).then_inc(S("sb_op"), 1)

        def ffn(f):
            ni, nu, p0, r0 = FF[f]
            ring = G if nu == 2 else GR
            pe.wait_ge(S("xl"), XLN[WHAT[p0][0]])
            for b in ("G0", "G1", "M0", "D0", "D1", "D2", "D3"):
                free(b)

            def up(j, pans, js):
                for u, pan in enumerate(pans):
                    pe.wait_ge(S("w_lo"), pan.p + 1)
                    if js >= nu % 2 + 1:
                        pe.wait_ge(S(f"up_read{f}"), nu * (j - 1) + u + 1 if nu == 2 else j - 1)
                    bank = ring[u if nu == 2 else js % 3]
                    for n in range(2):
                        for k in range(KT):
                            ins = tile3(bank[:, n, :], pan, n * KT + k, P, xh[:, k, :], xl[:, k, :], k == 0, k == KT - 1)
                    ins.then_inc(S("pe_panel"), 1)

            def down(i, pan, js, last):
                pe.wait_ge(S("w_lo"), pan.p + 1)
                pe.wait_ge(S(f"hid{f}"), nu * i + nu)
                for n in range(8):
                    for q in range(2):
                        ins = tile3(DB[n // 2][:, n % 2, :], pan, 2 * n + q, P, hh[:, js % 3, q, :],
                                    hl[:, js % 3, q, :], js == 0 and n % 2 == 0 and q == 0, last and q == 1, skip=True)
                ins.then_inc(S("pe_panel"), 1)

            ffn_walk(pe, f, up, down)
            for i in range(4):
                freed[f"D{i}"] = ("x_ready", 4 * FRES[f] + i + 1)
            n = ni * nu
            for b in ("G0", "G1", "M0"):
                freed[b] = (f"up_read{f}", n)

        def mem_stat():
            free("M1")
            pe.wait_ge(S("mem_sq"), 4)
            for k in range(KT):
                ins = mm(M[1][:, 0, :], ones, mwk[:, k, :], start=k == 0, stop=k == KT - 1)
            ins.then_inc(S("mem_st"), 1)
            freed["M1"] = ("mem_rs", 1)

        def hn(i):
            pe.wait_ge(S("hn_sq"), i + 1)
            free("M1")
            mm(M[1][:, :, :], bones, hsq[:, :, :]).then_inc(S("hn_ss"), 1)
            freed["M1"] = ("hn_read", i + 1)

        def turn(src, need, sem, bank):
            projected(pe, *need)
            free(bank)
            b = {"M0": M[0], "D3": DB[3]}[bank]
            for s_ in range(2):
                for j in range(2):
                    ins = nc.tensor.transpose(b[:, s_, j * P:(j + 1) * P], src[:, j, s_ * P:(s_ + 1) * P], ident)
            ins.then_inc(S(sem), 1)

        def turn_mv(l):
            turn(mv, (f"mkv{l}", 1), "mv_t", "M0")
            freed["M0"] = ("mvn", l + 1)

        def turn_v():
            turn(vs, ("kv", 1), "vs_t", "M0")
            freed["M0"] = ("vsn", 1)

        def score_m(l):
            pe.wait_ge(S("hn"), 2 if l == 0 else 4)
            for h in range(4):
                j, o = h // 2, 64 * (h % 2)
                free(f"D{h}")
                for tt in range(2):
                    ins = mm(DB[h][:, tt, :], mq[o:o + 64, j, tt * P:(tt + 1) * P], mk[o:o + 64, j, :])
                ins.then_inc(S("sm"), 1)
                freed[f"D{h}"] = ("sm_exp", 8 * l + 2 * h + 2)

        def turn_p(l):
            pm = (pm0, pm1)[l]
            for h in range(4):
                free(f"D{h}")
                pe.wait_ge(S("sm_p"), 4 * l + h + 1)
                for mt in range(2):
                    for tt in range(2):
                        ins = nc.tensor.transpose(DB[h][:, mt, tt * P:(tt + 1) * P],
                                                  pm[:, 2 * h + tt, mt * P:(mt + 1) * P], ident)
                ins.then_inc(S("sm_t"), 1)
                freed[f"D{h}"] = ("sm_pt", 4 * l + h + 1)

        def pv_m(l):
            ptm = (ptm0, ptm1)[l]
            free("M0")
            pe.wait_ge(S("mvn"), l + 1)
            pe.wait_ge(S("sm_pt"), 4 * l + 4)
            for h in range(4):
                j, o = h // 2, 64 * (h % 2)
                for mt in range(2):
                    ins = mm(M[0][o:o + 64, j, :], mvn[:, mt, h * 64:(h + 1) * 64], ptm[:, h, mt, :],
                             start=mt == 0, stop=mt == 1)
            ins.then_inc(S("pvm"), 1)
            freed["M0"] = ("xl", 20 if l == 0 else 29)

        def pool_mm():
            pe.wait_ge(S("pool_d"), 1)
            pe.wait_ge(S("ld_pool"), 16)
            parts = [(g, d0_, d1_) for g in range(PG) for d0_, d1_ in ([(0, 128), (128, 192)], [(0, 64), (64, 192)])[g % 2]]
            at = 0
            for i in range(3):
                free(f"D{i}")
            for g, lo, hi in parts:
                t, o = divmod(at, P)
                for ck in range(2):
                    ins = mm(DB[t // 2][o:o + hi - lo, t % 2, :], poolw[:, g, ck, lo:hi], zp[:, 2 * g + ck, 16:16 + T],
                             start=ck == 0, stop=ck == 1)
                at += hi - lo
                if at % 256 == 0:
                    ins.then_inc(S("pool_p"), 1)
                    freed[f"D{t // 2}"] = ("xl", 16 + at // 256)

        def score_s(g):
            pe.wait_ge(S("hn"), 8)
            pe.wait_ge(S("ksw"), 1)
            for h in range(4 * g, 4 * g + 4):
                b = h % 4
                free(f"D{b}")
                j, o = h // 2, 64 * (h % 2)
                kvh = h // 3
                src = ks if kvh % 2 == h % 2 else ksw
                f_ = flat(DB[b])
                mm(f_[:, 0:P], qs[o:o + 64, j, 0:P], src[o:o + 64, kvh // 2, 0:P])
                mm(f_[:, P:3 * P], qs[o:o + 64, j, P:T], src[o:o + 64, kvh // 2, :]).then_inc(S("ws"), 1)
                freed[f"D{b}"] = ("ws_read", h + 1)

        def pv_s(j):
            for h in (2 * j, 2 * j + 1):
                b = h % 2
                free(f"D{b}")
                pe.wait_ge(S("ws_p"), h + 1)
                for i in range(3):
                    ins = nc.tensor.transpose(flat(DB[b])[:, i * P:(i + 1) * P], ss[:, h, i * P:(i + 1) * P], ident)
                ins.then_inc(S("ws_t"), 1)
                freed[f"D{b}"] = ("ws_pt", h + 1)
            bank = ("D2", "D3", "M1")[j // 2]
            B = (DB[2], DB[3], M[1])[j // 2]
            if j % 2 == 0:
                free(bank)
            pe.wait_ge(S("vsn"), 1)
            for h in (2 * j, 2 * j + 1):
                o, kvh = 64 * (h % 2), h // 3
                pe.wait_ge(S("ws_pt"), h + 1)
                v = [vsn[:, i, kvh * 64:(kvh + 1) * 64] for i in range(2)]
                pr = [pt[:, h % 8, i * P:(i + 1) * P] for i in range(3)]
                mm(B[o:o + 64, j % 2, 0:P], v[0], pr[0])
                mm(B[o:o + 64, j % 2, P:T], v[0], pr[1], start=True, stop=False)
                ins = mm(B[o:o + 64, j % 2, P:T], v[1], pr[2], start=False, stop=True)
            ins.then_inc(S("ws_o"), 1)
            freed[bank] = ("xl", 30 + j // 2)

        walk(pe, {"norm": norm_stat, "stat3": lambda: norm_stat(3),
                  "stat5": lambda: norm_stat(5), "panel": panel,
                  "rw_gates": rw_gates, "rw_key": rw_key, "rw_turn": rw_turn, "rw_prod": rw_prod,
                  "inv_first": inv_first, "inv_t": inv_t, "inv_x": inv_x, "rw_rhs": rw_rhs, "rw_sol": rw_sol,
                  "rw_state": rw_state, "rw_out": rw_out, "rw_gn1": rw_gn1, "rw_gn2": rw_gn2,
                  "sg_mean": lambda: sg_sum(z_sg[:, 2:4, :], "sg_s", ("sg_gelu", 1)),
                  "sg_var": lambda: sg_sum(sgn, "sg_v", ("sg_sq", 1)),
                  "sg_turn": sg_turn, "sg_mix": sg_mix, "sb_turn": sb_turn, "sb_z": sb_z, "sb_q": sb_q,
                  "sb_o": sb_o, "ffn": ffn, "mem_stat": mem_stat, "hn": hn, "turn_mv": turn_mv,
                  "turn_v": turn_v, "score_m": score_m, "turn_p": turn_p, "pv_m": pv_m, "pool_mm": pool_mm,
                  "score_s": score_s, "pv_s": pv_s})

    HEADS = [(mk, "mk_g", 0, ("mkv0", 0)), (mq, None, 0, ("in0q", 0)), (mk, "mk_g", 1, ("mkv1", 0)),
             (mq, None, 1, ("in1", 0)), (ks, "k_g", 0, ("kv", 0)), (qs[:, 0:2, :], None, 2, ("in1", 1)),
             (qs[:, 2:4, :], None, 2, ("in1", 2)), (qs[:, 4:6, :], None, 2, ("in1", 3))]
    NORMS = {0: (0, 0, 0, ("mix_g", 0)), 1: (4, 8, PAN["wo"] + 4, ("ffn_g", 0)),
             3: (8, 12, PAN["mkv0"], ("mix2_g", 0)), 4: (12, 20, PAN["wout0"] + 4, ("mlp_g", 0)),
             5: (16, 24, PAN["mkv1"], ("kv_g", 0)), 6: (24, 32, PAN["wout1"] + 4, ("mlp_g", 8))}
    slopes = [2.0 ** (-8.0 * (i + 1) / QH) for i in range(QH)]

    @block.scalar
    def _(act):
        fn = nc.scalar.activation
        own = Own(act, "act_own")

        def signal(ins, name):
            ins.then_inc(S(name), 1)

        for name, dst, src in (("x", x[:], A["x"]), ("par", par[:], A["par"]), ("cst", cst[:], A["cst"]),
                               ("lora", lora[:], A["lora"]), ("sgw", sgw[:], A["sg_w"]), ("lvl", lvl[:], A["lvl"]),
                               ("sgb", sgb[:], A["sg_b"])):
            act.dma_start(dst, src).then_inc(S("ld_" + name), 16)

        done = [0]

        def split(pan):
            w = PT * (PGW if isinstance(pan.p, int) and NARROW <= pan.p < NARROW + 4 else P)
            act.wait_ge(S(f"w_land{pan.slot}"), 16 * (pan.turn + 1))
            if not (isinstance(pan.p, int) and pan.p < SLOTS):
                act.wait_ge(S("pe_panel"), pan.p - SLOTS + 1)
            signal(fn(whi[:, pan.slot, 0:w], raw[:, pan.slot, 0:w], ACT.Copy), "w_hi")

        def split_to(p):
            while done[0] < min(p, NPAN):
                split(Pan(done[0]))
                done[0] += 1

        def squares(n):
            w = wk if n == 0 else wk2
            for i in range(4):
                if n == 0:
                    act.wait_ge(S("ld_x"), 16)
                else:
                    act.wait_ge(S("x_ready"), 4 * (n - 1) + i + 1)
                if i == 0:
                    if n == 1:
                        act.wait_ge(S("branch"), 4)
                        act.wait_ge(S("pe_panel"), PAN["out3"] + 1)
                    if n in (2, 4, 5, 6):
                        act.wait_ge(S("xl"), {2: 12, 4: 20, 5: 24, 6: 32}[n])
                    if n >= 3:
                        act.wait_ge(S("stat"), n)
                    if n == 4:
                        act.wait_ge(S("pool_d"), 1)
                    if n == 6:
                        act.wait_ge(S("ws_t"), QH)
                signal(fn(w[:, 2 * i:2 * i + 2, :], x[:, 2 * i:2 * i + 2, :], ACT.Square), "sq")
            act.wait_ge(S("stat"), n + 1)
            if n == 0:
                act.wait_ge(S("ld_cst"), 16)
            if n in (1, 2, 4, 5, 6):
                act.wait_ge(S("nrm"), {1: 4, 2: 8, 4: 12, 5: 16, 6: 24}[n])
            if n == 1:
                act.wait_ge(S("sg_norm"), 1)
            own(fn(rstd[:], M[1][:, 0, :], ACT.Ln, bias=eps(EPS6), scale=1.0 / D))
            signal(fn(rstd[:], rstd[:], ACT.Exp, scale=-0.5), "rs")

        def high(n):
            a, b, pan, _ = NORMS[n]
            reach(act, "pe_panel", pan)
            if b:
                act.wait_ge(S("xl"), b)
            for i in range(4):
                act.wait_ge(S("nrm"), a + i + 1)
                signal(fn(xh[:, 2 * i:2 * i + 2, :], (wk if n == 0 else wk2)[:, 2 * i:2 * i + 2, :], ACT.Copy), "xh")

        def norm(n):
            squares(n)
            if n != 2:
                high(n)

        def high_m(k, src):
            if k == 1:
                act.wait_ge(S("branch"), 4)
            act.wait_ge(S("pe_panel"), (0, PAN["out3"] + 1, PAN["mkv0"] + 2, PAN["mkv1"] + 2)[k])
            signal(fn(mh[:], src[:], ACT.Copy), "mh")

        def norm5b():
            act.wait_ge(S("nrm"), 24)
            high_m(3, wk2)

        def panel(p):
            split_to(p + 3)
            name, i = WHAT[p]
            if name in RES or name in OUTS:
                return
            bank = G[gbank[p]]
            act.wait_ge(S("pe_panel"), p + 1)
            src = bank[:, :, :]
            if name[:4] == "gate":
                if name == "gate0" and i == 0:
                    act.wait_ge(S("sg_vn"), 1)
                if name == "gate0" and i >= 2:
                    act.wait_ge(S("sg_y"), 1)
                if name == "gate1":
                    act.wait_ge(S("g_dve"), i + 1)
                elif name != "gate0":
                    act.wait_ge(S("merged"), 4 * (int(name[4]) - 2) + i + 1)
                for u in range(2):
                    col = 8 * int(name[4]) + 2 * i + u
                    ins = fn(sig[:, 2 * i + u, :], bank[:, u, :], ACT.Exp, bias=neg[:, col:col + 1], scale=-1.0)
                signal(ins, "g_act")
                return
            if name == "rw":
                if i == 0:
                    act.wait_ge(S("zeros"), 1)
                dst = z_rw[:, 2 * i:2 * i + 2, 1:T + 1]
            elif name == "sc":
                dst = z_sc[:, 2 * i:2 * i + 2, :]
            elif name == "sg":
                dst = z_sg[:, 2 * i:2 * i + 2, :]
            elif name == "sb":
                dst = z_sb[:, 2 * i:2 * i + 2, :]
            elif name[:3] == "mkv":
                dst = (mk, mv)[i][:, :, :]
            elif name == "in0q" or (name == "in1" and i == 0):
                dst = mq[:, :, :]
            elif name == "in0m":
                dst, src = zp[:, 2 * i:2 * i + 2, 16:16 + T], bank[0:PGW, :, :]
            elif name == "kv":
                dst = (ks, vs)[i][:, :, :]
            else:
                dst = qs[:, 2 * i - 2:2 * i, :]
            signal(fn(dst, src, ACT.Copy), "g_act")

        def rw_low():
            act.wait_ge(S("rw_shift"), 4)
            own(fn(e2[:, 0, :], zs[:, 6, :], ACT.Exp, scale=-2.0))
            signal(fn(e2[:, 1, :], zs[:, 7, :], ACT.Exp, scale=-1.0), "rw_e")

        def rw_gates():
            act.wait_ge(S("rw_low"), 1)
            act.wait_ge(S("neg"), 1)
            for j in range(2):
                fn(ew[:, j, :], DB[0][:, j, :], ACT.Exp, bias=neg[:, 32 + j:33 + j], scale=-1.0)
            for j in range(2):
                fn(ew[:, 2 + j, :], DB[1][:, j, :], ACT.Exp, bias=neg[:, 34 + j:35 + j], scale=-1.0)
            signal(fn(gg[:], DB[2][:, :, :], ACT.Copy), "rw_low_read")

        def rw_cum():
            act.wait_ge(S("rw_cum"), 1)
            fn(em[:], cum[:], ACT.Exp, scale=-DECAY)
            fn(ei[:], cum[:, :, 1:P + 1], ACT.Exp, scale=DECAY)
            signal(fn(esc[:], esc[:], ACT.Exp, scale=-DECAY), "rw_dec")

        def rw_key():
            act.wait_ge(S("rw_kmax"), 1)
            own(fn(bon[:], bon[:], ACT.Ln, scale=2.0 ** 20))
            signal(fn(bon[:], bon[:], ACT.Exp, bias=eps(KKB), scale=-0.5), "rw_krs")

        def rw_turn():
            act.wait_ge(S("rw_turned"), 1)
            act.wait_ge(S("rw_e2"), 1)
            fn(vn[:], DB[0][:, :, :], ACT.Copy)
            signal(fn(bkn[:].rearrange("p a b -> p (a b)"), flat(DB[1]), ACT.Copy), "rw_nat")

        def inv_first():
            act.wait_ge(S("inv_t0"), 1)
            for g in range(2):
                ins = fn(mx[:, 4 * g:4 * g + 4, :].rearrange("p a b -> p (a b)"), flat(M[g]), ACT.Copy)
            signal(ins, "inv_x0")

        def inv_t(l):
            act.wait_ge(S("inv_T"), l)
            for g in range(2):
                ins = fn(mt1[:, 4 * g:4 * g + 4, :].rearrange("p a b -> p (a b)"), flat(M[g]), ACT.Copy)
            signal(ins, "inv_c")

        def rw_rhs(ch):
            act.wait_ge(S("rw_rhs"), ch + 1)
            for half in range(2):
                signal(fn(b0[:, ch, half::2, :], M[half][:, 0, 0:P].rearrange("p (j v) -> p j v", j=2), ACT.Copy),
                       "rw_b0")

        def rw_sol(ch):
            act.wait_ge(S("rw_sol"), ch + 1)
            signal(fn(uu[:, ch, :, :].rearrange("p h v -> p (h v)"), M[0][:, 0, :], ACT.Copy), "rw_uu")

        def rw_out():
            act.wait_ge(S("rw_yp"), 1)
            signal(fn(y[:], DB[2][:, :, :], ACT.Copy), "rw_y")

        def rw_gn1():
            act.wait_ge(S("rw_yc"), 1)
            signal(fn(ysq[:], y[:], ACT.Square), "rw_ysq")

        def rw_gn2():
            act.wait_ge(S("rw_var"), 1)
            own(fn(yr[:], DB[3][:, :, :], ACT.Ln, bias=eps(EPSG), scale=1.0 / 64))
            signal(fn(yr[:], yr[:], ACT.Exp, scale=-0.5), "rw_rs")
            act.wait_ge(S("rw_fin"), 1)
            act.wait_ge(S("pe_panel"), PAN["out1"] + 1)
            signal(fn(hh1[:, 1, :, :], y[:], ACT.Copy), "branch_h")

        def sc():
            act.wait_ge(S("sc_y"), 1)
            signal(fn(hh1[:, 0, :, :], ycv[:], ACT.Copy), "branch_h")

        def sg_gelu():
            projected(act, "sg", 1)
            signal(fn(sgt[:], z_sg[:], ACT.Square), "sg_z2")
            act.wait_ge(S("sg_z3"), 1)
            signal(fn(sgt[:], sgt[:], ACT.Exp, scale=-2.0 * math.sqrt(2.0 / math.pi)), "sg_e")

        def sg_mean():
            act.wait_ge(S("sg_c"), 1)
            signal(fn(sgn[:], sgv[:], ACT.Square), "sg_sq")

        def sg_var():
            act.wait_ge(S("sg_v"), 1)
            act.wait_ge(S("nrm"), 4)
            own(fn(rstd[:], DB[3][:, 0, :], ACT.Ln, bias=eps(EPS5), scale=1.0 / BW))
            signal(fn(rstd[:], rstd[:], ACT.Exp, scale=-0.5), "sg_rs")

        def sg_turn():
            act.wait_ge(S("sg_turned"), 1)
            signal(fn(sgn[:], DB[3][:, :, :], ACT.Copy), "sg_vn")

        def sg_mix():
            act.wait_ge(S("sg_y"), 1)
            signal(fn(hh1[:, 1, :, :], z_sg[:, 0:2, :], ACT.Copy), "branch_h")

        def sb_turn():
            act.wait_ge(S("sb_turned"), 1)
            act.wait_ge(S("rw_kt"), 1)
            signal(fn(sbv[:], DB[1][:, :, :], ACT.Copy), "sb_vn")

        def sb_e(h):
            act.wait_ge(S("sb_zp"), h + 1)
            if h == 0:
                act.wait_ge(S("sg_mixed"), 1)
            else:
                act.wait_ge(S("sb_att"), h)
            signal(fn(z3[:], flat(DB[0])[:, 0:3 * P], ACT.Copy, scale=0.125), "sb_zs")
            act.wait_ge(S("sb_abs"), h + 1)
            own(fn(l3[:], l3[:], ACT.Exp))
            signal(fn(l3[:], l3[:], ACT.Ln, bias=eps(ONE)), "sb_ln")

        def sb_a(h):
            act.wait_ge(S("sb_arg"), h + 1)
            signal(fn(z3[:], z3[:], ACT.Exp), "sb_exp")

        def sb_o(h):
            j, o = h // 2, 64 * (h % 2)
            act.wait_ge(S("sb_op"), h + 1)
            ins = fn(z_sb[o:o + 64, j, :], flat(DB[0])[o:o + 64, 0:T], ACT.Copy)
            signal(ins, "sb_out")
            if h == 3:
                act.wait_ge(S("sb_out"), 4)
                act.wait_ge(S("pe_panel"), PAN["out0"] + 1)
                signal(fn(hh1[:, 0, :, :], z_sb[:, 0:2, :], ACT.Copy), "branch_h")

        def merge_split():
            act.wait_ge(S("pe_panel"), PAN["gate3"] + 4)
            for i in range(4):
                act.wait_ge(S("merged"), 8 + i + 1)
                signal(fn(xh[:, 2 * i:2 * i + 2, :], merged[:, 2 * i:2 * i + 2, :], ACT.Copy), "xh")

        def ffn(f):
            ni, nu, p0, _ = FF[f]

            def high_hid(j, u, js):
                act.wait_ge(S("prod"), 2 * j + u + 1)
                if u == 0 and js >= 2:
                    act.wait_ge(S("pe_panel"), p0 + 2 * nu + (j - 3) * (nu + 1) + 1)
                signal(fn(hh[:, js % 3, u, :], hid[:, js % 3, u, :], ACT.Copy), f"hid_h{f}")

            def up(j, pans, js):
                for u, pan in enumerate(pans):
                    more(pan, 2)
                    act.wait_ge(S("pe_panel"), pan.p + 1)
                    if nu == 2:
                        if js == 0 and u == 0:
                            act.wait_ge(S("zeros2"), 1)
                        if js >= 1:
                            act.wait_ge(S("prod"), 2 * j + u - 1)
                        fn(upad[:, u, :, 2:T + 2], G[u][:, :, :], ACT.Copy)
                        for s_ in range(2):
                            w2 = par[:, bass.ds(2 * j + (PC["conv"] + 2 * 2 * FT1 + s_ * FT1 + u), 1)]
                            ins = fn(cv[:, u, s_, :], G[u][:, s_, :], ACT.Copy, scale=w2)
                        signal(ins, f"up_read{f}")
                        if u:
                            high_hid(j, 0, js)
                        act.wait_ge(S("conv"), 2 * j + u + 1)
                        signal(fn(sgm[:, u, :], cv[:, u, 0, :], ACT.Exp, scale=-1.0), "silu_e")
                    else:
                        if js >= 2:
                            act.wait_ge(S(f"hid{f}"), j - 1)
                        signal(fn(rel[:, js % 3, :, :], GR[js % 3][:, :, :], ACT.Relu), f"up_read{f}")
                        act.wait_ge(S(f"up_read{f}"), j + 1)
                        if js >= 2:
                            act.wait_ge(S("pe_panel"), p0 + 2 * nu + (j - 3) * (nu + 1) + 1)
                        signal(fn(hh[:, js % 3, :, :], rel[:, js % 3, :, :], ACT.Square), f"hid_h{f}")
                if nu == 2 and js == 0:
                    high_hid(0, 1, 0)

            def down(i, pan, js, last):
                more(pan, 2)
                if nu == 2 and not last:
                    high_hid(i + 1, 1, js + 1)

            def more(pan, ahead):
                q = Pan(pan.p0 + ahead)
                if isinstance(pan.p, int):
                    split_to(pan.p + ahead + 1)
                else:
                    q.p = pan.p + ahead
                    q.turn = pan.turn + (pan.p0 + ahead) // SLOTS - pan.p0 // SLOTS
                    split(q)

            ffn_walk(act, f, up, down, done)

        def mem_stat():
            for i in range(4):
                act.wait_ge(S("ld_mem"), 16)
                signal(fn(mwk[:, 2 * i:2 * i + 2, :], mem[:, 2 * i:2 * i + 2, :], ACT.Square), "mem_sq")
            act.wait_ge(S("mem_st"), 1)
            own(fn(mrstd[:], M[1][:, 0, :], ACT.Ln, bias=eps(EPS6), scale=1.0 / D))
            signal(fn(mrstd[:], mrstd[:], ACT.Exp, scale=-0.5), "mem_rs")

        def mem_norm(l):
            act.wait_ge(S("mem_n"), l + 1)
            high_m(l + 1, mwk)

        def hn(i):
            src, _, _, need = HEADS[i]
            projected(act, *need)
            if i:
                act.wait_ge(S("hn_ss"), i)
            signal(fn(hsq[:], src if i > 4 else src[:], ACT.Square), "hn_sq")
            act.wait_ge(S("hn_ss"), i + 1)
            if i:
                act.wait_ge(S("hn"), i)
            own(fn(hy[:], M[1][:, :, :], ACT.Ln, bias=eps(EPS6), scale=1.0 / 64))
            signal(fn(hy[:], hy[:], ACT.Exp, scale=-0.5), "hn_y")

        def turn_mv(l):
            act.wait_ge(S("mv_t"), l + 1)
            signal(fn(mvn[:], M[0][:, :, :], ACT.Copy), "mvn")

        def turn_v():
            act.wait_ge(S("vs_t"), 1)
            signal(fn(vsn[:], M[0][:, :, :], ACT.Copy), "vsn")

        def score_m(l):
            for h in range(4):
                act.wait_ge(S("sm_max"), 4 * l + h + 1)
                if h == 0:
                    act.wait_ge(S("ml"), 2)
                for tt in range(2):
                    a = 2 * h + tt
                    signal(fn((pm0, pm1)[l][:, a, :], DB[h][:, tt, :], ACT.Exp, bias=hmax[:, 1, a:a + 1],
                              accum_out=hmax[:, 2, a:a + 1]), "sm_exp")

        def turn_p(l):
            for h in range(4):
                act.wait_ge(S("sm_t"), 4 * l + h + 1)
                signal(fn((ptm0, ptm1)[l][:, h, :, :], DB[h][:, :, :], ACT.Copy), "sm_pt")

        def pv_m(l):
            act.wait_ge(S("pvm"), l + 1)
            act.wait_ge(S("pe_panel"), (PAN["in0m"] + 4, PAN["kv"] + 2)[l])
            signal(fn(xh[:, 6:8, :], M[0][:, :, :], ACT.Copy), "xh")

        def pool_mm():
            act.wait_ge(S("pe_panel"), PAN["in0m"] + 4)
            for i in range(3):
                act.wait_ge(S("pool_p"), i + 1)
                for u in range(2):
                    ins = fn(xh[:, 2 * i + u, :], DB[i][:, u, :], ACT.Copy, scale=pcol("pool_s", 2 * i + u))
                signal(ins, "xh")

        def score_s(g):
            act.wait_ge(S("ws_max"), g + 1)
            own(fn(wmax[:, 0, 8 * g:8 * g + 8], wmax[:, 0, 8 * g:8 * g + 8], ACT.Exp))
            for h in range(4 * g, 4 * g + 4):
                for b, (lo, hi) in enumerate(((0, P), (P, 3 * P))):
                    a = 2 * h + b
                    ins = fn(ss[:, h, lo:hi], ss[:, h, lo:hi], ACT.Exp, bias=wmax[:, 1, a:a + 1],
                             accum_out=wmax[:, 2, a:a + 1])
            signal(ins, "ws_exp")

        def pv_s(j):
            for h in (2 * j, 2 * j + 1):
                act.wait_ge(S("ws_t"), h + 1)
                if h >= 8:
                    act.wait_ge(S("ws_o"), (h - 8) // 2 + 1)
                if h == 0:
                    act.wait_ge(S("pvm"), 2)
                signal(fn(pt[:, h % 8, :], flat(DB[h % 2])[:, 0:3 * P], ACT.Copy), "ws_pt")
            if j % 2:
                act.wait_ge(S("ws_o"), j + 1)
                act.wait_ge(S("pe_panel"), PAN["kv"] + 2)
                signal(fn(xh[:, j - 1:j + 1, :], (DB[2], DB[3], M[1])[j // 2][:, :, :], ACT.Copy), "xh")

        split_to(3)
        walk(act, {"norm": norm, "stat3": lambda: squares(3), "norm3": lambda: high(3),
                   "stat5": lambda: squares(5), "norm5": lambda: high(5), "norm5b": norm5b, "panel": panel,
                   "rw_low": rw_low, "rw_gates": rw_gates, "rw_cum": rw_cum, "rw_key": rw_key,
                   "rw_turn": rw_turn, "inv_first": inv_first, "inv_t": inv_t, "rw_rhs": rw_rhs,
                   "rw_sol": rw_sol, "rw_out": rw_out, "rw_gn1": rw_gn1, "rw_gn2": rw_gn2, "sc": sc,
                   "sg_gelu": sg_gelu, "sg_mean": sg_mean, "sg_var": sg_var, "sg_turn": sg_turn,
                   "sg_mix": sg_mix, "sb_turn": sb_turn, "sb_e": sb_e, "sb_a": sb_a, "sb_o": sb_o,
                   "merge_split": merge_split, "ffn": ffn, "mem_stat": mem_stat, "mem_norm": mem_norm,
                   "hn": hn, "turn_mv": turn_mv, "turn_v": turn_v, "score_m": score_m, "turn_p": turn_p,
                   "pv_m": pv_m, "pool_mm": pool_mm, "score_s": score_s, "pv_s": pv_s})

    @block.vector
    def _(dve):
        tt, ts, stt = nc.vector.tensor_tensor, nc.vector.tensor_scalar, nc.vector.scalar_tensor_tensor
        own = Own(dve, "dve_own")
        MUL, ADD, SUB, MAX, MIN = ALU.mult, ALU.add, ALU.subtract, ALU.max, ALU.min
        done = [0]

        def signal(ins, name):
            ins.then_inc(S(name), 1)

        def f32(ap):
            return ap.bitcast(F32)

        def split(pan):
            w = PT * (PGW if isinstance(pan.p, int) and NARROW <= pan.p < NARROW + 4 else P)
            dve.wait_ge(S("w_hi"), pan.p + 1)
            signal(tt(wlo[:, pan.slot, 0:w], raw[:, pan.slot, 0:w], f32(whi[:, pan.slot, 0:w]), SUB), "w_lo")

        def split_to(p):
            while done[0] < min(p, NPAN):
                split(Pan(done[0]))
                done[0] += 1

        def low(k, i, src):
            dve.wait_ge(S("xh"), k)
            signal(tt(xl[:, 2 * i:2 * i + 2, :], src, f32(xh[:, 2 * i:2 * i + 2, :]), SUB), "xl")

        def low_b(k, slot, src):
            dve.wait_ge(S("branch_h"), k)
            signal(tt(hl1[:, slot, :, :], src, f32(hh1[:, slot, :, :]), SUB), "branch")

        def scaled(dst, src, scale, gain, i, name, g0):
            stt(dst[:, 2 * i, :], src[:, 2 * i, :], pcol(gain, g0 + 2 * i), scale[:], MUL, MUL)
            signal(stt(dst[:, 2 * i + 1, :], src[:, 2 * i + 1, :], pcol(gain, g0 + 2 * i + 1), scale[:], MUL, MUL), name)

        def apply(n):
            dve.wait_ge(S("rs"), n + 1)
            if n == 2:
                for i in range(4):
                    scaled(x, x, rstd, "fin_g", i, "x_ready", 0)
                return
            a, b, _, (gain, g0) = NORMS[n]
            w = wk if n == 0 else wk2
            for i in range(4):
                scaled(w, x, rstd, gain, i, "nrm", g0)
                if i:
                    low(b + i, i - 1, w[:, 2 * i - 2:2 * i, :])
            low(b + 4, 3, w[:, 6:8, :])

        def norm(n):
            apply(n)
            if n == 1:
                dve.wait_ge(S("pe_panel"), PAN["out3"] + 1)
                signal(nc.vector.memset(upad[:, :, :, 0:2], 0.0), "zeros2")
            if n == 2:
                nc.vector.memset(zp[:, :, 0:16], 0.0)

        def norm5b():
            dve.wait_ge(S("xh"), 28)
            dve.wait_ge(S("xl"), 28)
            for i in range(4):
                scaled(wk2, x, rstd, "mix2_g", i, "nrm", 8)
            dve.wait_ge(S("mh"), 3)
            signal(tt(ml[:], wk2[:], f32(mh[:]), SUB), "ml")

        def panel(p):
            split_to(p + 3)
            name, i = WHAT[p]
            if name in RES:
                dve.wait_ge(S("pe_panel"), p + 1)
                signal(tt(x[:, 2 * i:2 * i + 2, :], x[:, 2 * i:2 * i + 2, :], DB[i][:, :, :], ADD), "x_ready")
            elif name in OUTS:
                b = int(name[3])
                for i in range(4):
                    if i < 3:
                        dve.wait_ge(S("out_pair"), 3 * b + i + 1)
                    else:
                        dve.wait_ge(S("pe_panel"), p + 1)
                    prs = slice(2 * i, 2 * i + 2)
                    out = merged if b == 0 else sig
                    dve.wait_ge(S("gate"), 4 * b + i + 1)
                    signal(tt(out[:, prs, :], sig[:, prs, :], G[i % 2 if OUT_EVEN[b] else 1 - i % 2][:, :, :], MUL), "g_dve")
                    if b:
                        dve.wait_ge(S("g_dve"), 4 * b + i + 1)
                        signal(tt(merged[:, prs, :], merged[:, prs, :], sig[:, prs, :], ADD), "merged")
            elif name[:4] == "gate":
                projected(dve, name, i)
                prs = slice(2 * i, 2 * i + 2)
                own(ts(sig[:, prs, :], sig[:, prs, :], 1.0, None, ADD))
                signal(nc.vector.reciprocal(sig[:, prs, :], sig[:, prs, :]), "gate")
            elif name == "rw":
                projected(dve, name, i)
                prs = slice(2 * i, 2 * i + 2)
                own(tt(zs[:, prs, :], z_rw[:, prs, 0:T], z_rw[:, prs, 1:T + 1], SUB))
                stt(zs[:, 2 * i, :], zs[:, 2 * i, :], pcol("mu", 2 * i), z_rw[:, 2 * i, 1:T + 1], MUL, ADD)
                signal(stt(zs[:, 2 * i + 1, :], zs[:, 2 * i + 1, :], pcol("mu", 2 * i + 1),
                           z_rw[:, 2 * i + 1, 1:T + 1], MUL, ADD), "rw_shift")

        use, OUT_EVEN = 0, {}
        for step in W:
            if step[0] == "panel":
                nm = WHAT[step[1]][0]
                if nm in OUTS:
                    OUT_EVEN[int(nm[3])] = use % 2 == 0
                    use += 4
                elif nm not in RES:
                    use += 1

        def rw_low():
            dve.wait_ge(S("rw_e"), 1)
            own(ts(e2[:], e2[:], 1.0, None, ADD))
            own(nc.vector.reciprocal(e2[:], e2[:]))
            signal(ts(e2[:, 0, :], e2[:, 0, :], 2.0, -1.0, MUL, ADD), "rw_e2")

        def rw_gates():
            dve.wait_ge(S("rw_low_read"), 1)
            own(ts(ew[:], ew[:], 1.0, None, ADD))
            own(nc.vector.reciprocal(ew[:], ew[:]))

        def rw_cum():
            for jc in range(4):
                j, ch = divmod(jc, 2)
                ins = nc.vector.tensor_tensor_scan(cum[:, jc, 1:P + 1], c("ones"), ew[:, j, ch * P:(ch + 1) * P],
                                                   0.0, MUL, ADD)
            own(ins)
            own(nc.vector.tensor_copy(mid[:], cum[:, :, 64:65]))
            own(tt(cum[:], cum[:], mid[:].broadcast_to([P, 4, P + 1]), SUB))
            signal(tt(esc[:], cum[:, 0:4:2, P:P + 1].rearrange("p a b -> p (a b)"),
                      mid[:, 1:4:2, :].rearrange("p a b -> p (a b)"), ADD), "rw_cum")

        def rw_key():
            for j in range(2):
                ins = ts(kk[:, j, :], zs[:, 2 + j, :], pcol("k_k", j), None, MUL)
            own(ins)
            signal(tt(bon[:], kk[:], kk[:], MUL), "rw_ksq")
            for j in range(2):
                ins = ts(kp[:, j, :], ew[:, 2 + j, :], 1.0, pcol("k_a", j), SUB, MUL)
            own(ins)
            own(stt(kp[:], kp[:], 1.0, zs[:, 2:4, :], ADD, MUL))
            dve.wait_ge(S("rw_kss"), 1)
            signal(ts(bon[:], DB[3][:, :, :], 1e-24, None, MAX), "rw_kmax")
            dve.wait_ge(S("rw_krs"), 1)
            own(stt(kk[:], kk[:], -1.0, bon[:], MUL, MUL))
            own(stt(ew[:, 2:4, :], kk[:], -1.0, ew[:, 2:4, :], MUL, MUL))

        def rw_mix():
            dve.wait_ge(S("rw_dec"), 1)
            tt(ar[:, :, 0, :], four(kk), em[:, :, 0:P], MUL)
            tt(ar[:, :, 1, :], four(zs[:, 0:2, :]), em[:, :, 1:P + 1], MUL)
            tt(bt[:], four(ew[:, 2:4, :]), ei[:], MUL)
            tt(kt[:], four(kp), ei[:], MUL)
            for j in range(2):
                ins = stt(bon[:, j, :], zs[:, j, :], pcol("r_k", j), kp[:, j, :], MUL, MUL)
            signal(ins, "rw_kt")

        def rw_turn():
            dve.wait_ge(S("rw_turned"), 1)
            signal(tt(bon[:], DB[2][:, :, :], zs[:, 4:6, :], MUL), "rw_bonus")

        def rw_prod(i):
            mask = cst[:, CC["strict"]:CC["strict"] + 2 * P].unsqueeze(1).broadcast_to([P, 2, 2 * P])
            for m in (2 * i, 2 * i + 1):
                dve.wait_ge(S("rw_gp"), m + 1)
                if m == 0:
                    dve.wait_ge(S("branch"), 2)
                signal(tt(gm[:, m, :, :].rearrange("p (a b) t -> p a (b t)", a=2), M[m % 2][:, :, :], mask, MUL), "rw_prod")

        def inv_first():
            dve.wait_ge(S("inv_n"), 1)
            signal(tt(mxt[:], mnt[:], c("ident").unsqueeze(1).broadcast_to([P, 8, P]), ADD), "inv_x")

        def inv_x(l):
            dve.wait_ge(S("inv_p"), l)
            for g in range(2):
                dst = mxt[:, 4 * g:4 * g + 4, :].rearrange("p a b -> p (a b)")
                ins = tt(dst, dst, flat(DB[2 + g]), ADD)
            if l < len(LEVELS) - 1:
                for g in range(2):
                    dst = mx[:, 4 * g:4 * g + 4, :].rearrange("p a b -> p (a b)")
                    ins = tt(dst, dst, flat(M[g]), ADD)
            signal(ins, "inv_x")

        def rw_state():
            dve.wait_ge(S("rw_sp"), 1)
            for j in range(2):
                ins = ts(st[:, j, :], M[1][:, j, 0:64], esc[:, j:j + 1], None, MUL)
            signal(ins, "rw_state")

        def rw_gn1():
            dve.wait_ge(S("rw_mean"), 1)
            signal(stt(y[:], DB[3][:, :, :], -1.0 / 64, y[:], MUL, ADD), "rw_yc")

        def rw_gn2():
            dve.wait_ge(S("rw_rs"), 1)
            for j in range(2):
                ins = stt(y[:, j, :], y[:, j, :], pcol("gn_g", j), yr[:, j, :], MUL, MUL)
            own(ins)
            for j in range(2):
                ins = stt(y[:, j, :], y[:, j, :], pcol("gn_b", j), bon[:, j, :], ADD, ADD)
            own(ins)
            signal(tt(y[:], y[:], gg[:], MUL), "rw_fin")
            low_b(4, 1, y[:])

        def sc():
            projected(dve, "sc", 2)
            own(tt(ucv[:, :, 2:T + 2], z_sc[:, 2:4, :], z_sc[:, 4:6, :], MUL))
            for j in range(2):
                ins = ts(ycv[:, j, :], ucv[:, j, 0:T], pcol("sc_w", j), None, MUL)
            own(ins)
            for i in (1, 2):
                for j in range(2):
                    ins = stt(ycv[:, j, :], ucv[:, j, i:i + T], pcol("sc_w", 2 * i + j), ycv[:, j, :], MUL, ADD)
                own(ins)
            signal(tt(ycv[:], ycv[:], z_sc[:, 0:2, :], MUL), "sc_y")
            low_b(1, 0, ycv[:])

        def sg_gelu():
            dve.wait_ge(S("sg_z2"), 1)
            own(ts(sgt[:], sgt[:], 0.044715, 1.0, MUL, ADD))
            signal(tt(sgt[:], sgt[:], z_sg[:], MUL), "sg_z3")
            dve.wait_ge(S("sg_e"), 1)
            own(ts(sgt[:], sgt[:], 1.0, None, ADD))
            own(nc.vector.reciprocal(sgt[:], sgt[:]))
            signal(tt(z_sg[:], z_sg[:], sgt[:], MUL), "sg_gelu")

        def sg_mean():
            dve.wait_ge(S("sg_s"), 1)
            dve.wait_ge(S("sg_gelu"), 1)
            for j in range(2):
                ins = stt(sgv[:, j, :], DB[3][:, 0, :], -1.0 / BW, z_sg[:, 2 + j, :], MUL, ADD)
            signal(ins, "sg_c")

        def sg_var():
            dve.wait_ge(S("sg_rs"), 1)
            for j in range(2):
                ins = stt(sgv[:, j, :], sgv[:, j, :], pcol("ln_g", j), rstd[:], MUL, MUL)
            own(ins)
            for j in range(2):
                ins = ts(sgv[:, j, :], sgv[:, j, :], pcol("ln_b", j), None, ADD)
            signal(ins, "sg_norm")

        def sg_mix():
            dve.wait_ge(S("sg_mixed"), 1)
            signal(tt(z_sg[:, 0:2, :], z_sg[:, 0:2, :], DB[3][:, :, :], MUL), "sg_y")
            low_b(2, 1, z_sg[:, 0:2, :])

        strict = c("strict").unsqueeze(1).broadcast_to([P, 2, P])

        def diag(h):
            return h[:].rearrange("p (a t) -> p a t", a=3)[:, 0:3:2, :]

        def sb_e(h):
            dve.wait_ge(S("sb_zs"), h + 1)
            reach(dve, "sb_op", h)
            signal(stt(l3[:], z3[:], -1.0, z3[:], MUL, MIN), "sb_abs")
            dve.wait_ge(S("sb_ln"), h + 1)
            own(stt(l3[:], z3[:], 0.0, l3[:], MAX, ADD))
            signal(tt(diag(l3), diag(l3), strict, MUL), "sb_sp")

        def sb_a(h):
            dve.wait_ge(S("sb_qp"), h + 1)
            own(tt(z3[:], z3[:], flat(DB[1])[:, 0:3 * P], SUB))
            signal(ts(z3[:], z3[:], 0.0, None, MIN), "sb_arg")
            dve.wait_ge(S("sb_exp"), h + 1)
            nc.vector.tensor_copy(l3[:, P:2 * P], z3[:, P:2 * P])
            signal(tt(diag(l3), diag(z3), strict, MUL), "sb_att")

        def sb_o(h):
            if h == 3:
                low_b(3, 0, z_sb[:, 0:2, :])

        def merge_split():
            for i in range(4):
                dve.wait_ge(S("merged"), 8 + i + 1)
                low(4 + i + 1, i, merged[:, 2 * i:2 * i + 2, :])

        def ffn(f):
            ni, nu, p0, _ = FF[f]

            class Step:

                def __init__(self, item, n):
                    self.item, self.n, self.k = item, n, 0

                def __call__(self, ins):
                    ins.then_inc(S(f"ffn_own{f}"), 1)
                    self.k += 1
                    dve.wait_ge(S(f"ffn_own{f}"), self.item * self.n + self.k)

            def more(pan, ahead):
                if isinstance(pan.p, int):
                    split_to(pan.p + ahead + 1)
                else:
                    q = Pan(pan.p0 + ahead)
                    q.p = pan.p + ahead
                    split(q)

            def low_hid(j, u, js):
                dve.wait_ge(S(f"hid_h{f}"), 2 * j + u + 1)
                signal(tt(hl[:, js % 3, u, :], hid[:, js % 3, u, :], f32(hh[:, js % 3, u, :]), SUB), f"hid{f}")

            def up(j, pans, js):
                for u, pan in enumerate(pans):
                    more(pan, 2)
                    if nu == 2:
                        t = 2 * j + u
                        step = Step(t, 4)
                        dve.wait_ge(S(f"up_read{f}"), t + 1)
                        for i, sh in ((1, 1), (0, 0)):
                            for s_ in range(2):
                                w = par[:, bass.ds(2 * j + (PC["conv"] + i * 2 * FT1 + s_ * FT1 + u), 1)]
                                ins = stt(cv[:, u, s_, :], upad[:, u, s_, sh:sh + T], w, cv[:, u, s_, :], MUL, ADD)
                            if i:
                                step(ins)
                            else:
                                signal(ins, "conv")
                        if u:
                            low_hid(j, 0, js)
                        dve.wait_ge(S("silu_e"), t + 1)
                        step(ts(sgm[:, u, :], sgm[:, u, :], 1.0, None, ADD))
                        step(nc.vector.reciprocal(sgm[:, u, :], sgm[:, u, :]))
                        step(tt(sgm[:, u, :], sgm[:, u, :], cv[:, u, 0, :], MUL))
                        signal(tt(hid[:, js % 3, u, :], sgm[:, u, :], cv[:, u, 1, :], MUL), "prod")
                    else:
                        dve.wait_ge(S(f"up_read{f}"), j + 1)
                        Step(j, 1)(tt(hid[:, js % 3, :, :], rel[:, js % 3, :, :], rel[:, js % 3, :, :], MUL))
                        dve.wait_ge(S(f"hid_h{f}"), j + 1)
                        signal(tt(hl[:, js % 3, :, :], hid[:, js % 3, :, :], f32(hh[:, js % 3, :, :]), SUB), f"hid{f}")
                if nu == 2 and js == 0:
                    low_hid(0, 1, 0)

            def down(i, pan, js, last):
                more(pan, 2)
                if nu == 2 and not last:
                    low_hid(i + 1, 1, js + 1)

            ffn_walk(dve, f, up, down, done)
            dve.wait_ge(S("pe_panel"), p0 + ni * (nu + 1))
            for i in range(4):
                signal(tt(x[:, 2 * i:2 * i + 2, :], x[:, 2 * i:2 * i + 2, :], DB[i][:, :, :], ADD), "x_ready")

        def mem_norm(l):
            dve.wait_ge(S("mem_rs"), 1)
            if l:
                dve.wait_ge(S("ml"), 1)
            for k in range(KT):
                ins = stt(mwk[:, k, :], mem[:, k, :], pcol("mem_g", 8 * l + k), mrstd[:], MUL, MUL)
            signal(ins, "mem_n")
            dve.wait_ge(S("mh"), l + 1)
            signal(tt(ml[:], mwk[:], f32(mh[:]), SUB), "ml")

        def hn(i):
            src, gain, g0, _ = HEADS[i]
            src = src if i > 4 else src[:]
            gain = pcol(gain, g0) if gain else gq8[:, g0:g0 + 1]
            dve.wait_ge(S("hn_y"), i + 1)
            signal(ts(ha[:], M[1][:, :, :], 1.0 / 64, 1e-6, MUL, ADD), "hn_read")
            dve.wait_ge(S("hn_read"), i + 1)
            own(tt(ht[:], ha[:], hy[:], MUL))
            own(tt(ht[:], ht[:], hy[:], MUL))
            own(ts(ht[:], ht[:], -0.5, 1.5, MUL, ADD))
            own(tt(hy[:], hy[:], ht[:], MUL))
            signal(stt(src, src, gain, hy[:], MUL, MUL), "hn")

        def swap_k():
            dve.wait_ge(S("hn"), 5)
            nc.vector.tensor_copy(ksw[0:64, :, :], ks[64:128, :, :])
            signal(nc.vector.tensor_copy(ksw[64:128, :, :], ks[0:64, :, :]), "ksw")

        def score_m(l):
            pm = (pm0, pm1)[l]
            for h in range(4):
                a = slice(2 * h, 2 * h + 2)
                dve.wait_ge(S("sm"), 4 * l + h + 1)
                own(nc.vector.tensor_reduce(hmax[:, 0, a], DB[h][:, :, :], AX_X, MAX))
                signal(ts(hmax[:, 1, a], hmax[:, 0, a], -1.0, None, MUL), "sm_max")
            for h in range(4):
                a = slice(2 * h, 2 * h + 2)
                dve.wait_ge(S("sm_exp"), 8 * l + 2 * h + 2)
                own(nc.vector.reciprocal(hmax[:, 0, a], hmax[:, 2, a]))
                for t_ in range(2):
                    b = 2 * h + t_
                    ins = ts(pm[:, b, :], pm[:, b, :], hmax[:, 0, b:b + 1], None, MUL)
                signal(ins, "sm_p")

        def pv_m(l):
            low((20, 29)[l], 3, M[0][:, :, :])

        def pool():
            projected(dve, "in0m", 3)
            own(tt(s2[:, :, 1:T + 16], zp[:, :, 1:T + 16], zp[:, :, 0:T + 15], ADD))
            own(tt(s4[:, 2:8, 3:T + 16], s2[:, 2:8, 3:T + 16], s2[:, 2:8, 1:T + 14], ADD))
            own(tt(s2[:, 4:8, 7:T + 16], s4[:, 4:8, 7:T + 16], s4[:, 4:8, 3:T + 12], ADD))
            own(tt(s4[:, 6:8, 15:T + 16], s2[:, 6:8, 15:T + 16], s2[:, 6:8, 7:T + 8], ADD))
            for g, (s_, win) in enumerate(((s2, 2), (s4, 4), (s2, 8), (s4, 16))):
                prs = slice(2 * g, 2 * g + 2)
                count = c("count", 16 * g, 16, slice(0, PGW)).unsqueeze(1).broadcast_to([PGW, 2, 16])
                own(tt(s_[:, prs, 16:32], s_[:, prs, 16:32], count, MUL))
                stt(zp[:, prs, 32:T + 16], s_[:, prs, 32:T + 16], 1.0 / win, zp[:, prs, 32:T + 16], MUL, SUB)
                ins = tt(zp[:, prs, 16:32], s_[:, prs, 16:32], zp[:, prs, 16:32], SUB)
            signal(ins, "pool_d")

        def pool_mm():
            for i in range(3):
                dve.wait_ge(S("xh"), 16 + i + 1)
                for u in range(2):
                    k = 2 * i + u
                    ins = stt(xl[:, k, :], DB[i][:, u, :], pcol("pool_s", k), f32(xh[:, k, :]), MUL, SUB)
                signal(ins, "xl")

        def score_s(g):
            for h in range(4 * g, 4 * g + 4):
                dve.wait_ge(S("ws"), h + 1)
                if h == 0:
                    dve.wait_ge(S("sm_t"), 8)
                signal(stt(ss[:, h, :], cst[:, CC["dist"]:CC["dist"] + 3 * P], slopes[h], flat(DB[h % 4])[:, 0:3 * P],
                           MUL, ADD), "ws_read")
            dve.wait_ge(S("ws_read"), 4 * g + 4)
            hs, a = slice(4 * g, 4 * g + 4), slice(8 * g, 8 * g + 8)
            top_ = wmax[:, 0, a].rearrange("p (h b) -> p h b", b=2)
            neg_ = wmax[:, 1, a].rearrange("p (h b) -> p h b", b=2)
            sink = par[:, PC["sinks"] + 4 * g:PC["sinks"] + 4 * g + 4].unsqueeze(2).broadcast_to([P, 4, 2])
            nc.vector.tensor_reduce(top_[:, :, 0:1], ss[:, hs, 0:P], AX_X, MAX)
            own(nc.vector.tensor_reduce(top_[:, :, 1:2], ss[:, hs, P:3 * P], AX_X, MAX))
            own(tt(top_, top_, sink, MAX))
            own(ts(neg_, top_, -1.0, None, MUL))
            signal(tt(top_, neg_, sink, ADD), "ws_max")
            dve.wait_ge(S("ws_exp"), g + 1)
            own(tt(wmax[:, 2, a], wmax[:, 2, a], wmax[:, 0, a], ADD))
            own(nc.vector.reciprocal(wmax[:, 2, a], wmax[:, 2, a]))
            for h in range(4 * g, 4 * g + 4):
                for b, (lo, hi) in enumerate(((0, P), (P, 3 * P))):
                    ins = ts(ss[:, h, lo:hi], ss[:, h, lo:hi], wmax[:, 2, 2 * h + b:2 * h + b + 1], None, MUL)
                signal(ins, "ws_p")

        def pv_s(j):
            if j % 2:
                low(29 + j // 2 + 1, j // 2, (DB[2], DB[3], M[1])[j // 2][:, :, :])

        signal(nc.vector.memset(z_rw[:, :, 0:1], 0.0), "zeros")
        nc.vector.memset(ucv[:, :, 0:2], 0.0)
        nc.vector.memset(cum[:, :, 0:1], 0.0)
        dve.wait_ge(S("ld_par"), 16)
        ts(neg[:, 0:32], par[:, PC["gate_b"]:PC["gate_b"] + 32], -1.0, None, MUL)
        ts(gq8[:, 0:2], par[:, PC["mq_g"]:PC["mq_g"] + 2], 0.125, None, MUL)
        ts(gq8[:, 2:3], par[:, PC["q_g"]:PC["q_g"] + 1], 0.125, None, MUL)
        signal(ts(neg[:, 32:36], par[:, PC["w0"]:PC["w0"] + 4], -1.0, None, MUL), "neg")
        dve.wait_ge(S("ld_cst"), 16)
        dve.wait_ge(S("ld_sgw"), 16)
        signal(tt(sgw[:], sgw[:], c("incl").unsqueeze(1).broadcast_to([P, 4, P]), MUL), "sg_tril")
        split_to(3)
        walk(dve, {"norm": norm, "norm3": lambda: apply(3), "norm5": lambda: apply(5), "norm5b": norm5b,
                   "panel": panel, "rw_low": rw_low, "rw_gates": rw_gates, "rw_cum": rw_cum, "rw_key": rw_key,
                   "rw_mix": rw_mix, "rw_turn": rw_turn, "rw_prod": rw_prod, "inv_first": inv_first,
                   "inv_x": inv_x, "rw_state": rw_state, "rw_gn1": rw_gn1, "rw_gn2": rw_gn2, "sc": sc,
                   "sg_gelu": sg_gelu, "sg_mean": sg_mean, "sg_var": sg_var, "sg_mix": sg_mix, "sb_e": sb_e,
                   "sb_a": sb_a, "sb_o": sb_o, "merge_split": merge_split, "ffn": ffn, "mem_norm": mem_norm,
                   "hn": hn, "swap_k": swap_k, "score_m": score_m, "pv_m": pv_m, "pool": pool,
                   "pool_mm": pool_mm, "score_s": score_s, "pv_s": pv_s})

    ctx.close()


def kernel(**a):
    import concourse.bacc as bacc
    from concourse.bass_utils import run_bass_kernel_spmd

    a = {k: np.asarray(v) for k, v in a.items()}

    def tiles(w, order=None, width=P):
        k, n = w.shape
        t = w.reshape(k // P, P, n // width, width).transpose(2, 0, 1, 3)
        if order is not None:
            t = t[order]
        return t.reshape(-1, P, width)

    def panels(t):
        n, _, w = t.shape
        return t.reshape(n // PT, PT, P, w).transpose(0, 2, 1, 3).reshape(n // PT, P, PT * w)

    def pairs(w):
        k, n = w.shape
        t = w.reshape(k // (2 * P), 2, P, n // P, P).transpose(0, 3, 1, 2, 4)
        return panels(t.reshape(-1, P, P))

    def interleave(up, down, nu):
        n = down.shape[0]
        up = up.reshape(n, nu, *up.shape[1:])
        parts = [up[0]]
        for i in range(n - 1):
            parts += [up[i + 1], down[i:i + 1]]
        return np.concatenate(parts + [down[n - 1:]])

    w_in = a["w_in"][0]
    sc_o, sb_o, rw_o, sg_o, gate_o = 0, 3 * BW, 6 * BW, 6 * BW + D, 8 * BW + D
    branch = (0, 3, 1, 2)
    outs = ("sc_out", "sg_out", "sb_out", "rw_out")
    gates = [w_in[:, gate_o + b * D:gate_o + (b + 1) * D] for b in branch]
    parts = [tiles(w_in[:, rw_o:rw_o + D]), tiles(w_in[:, sc_o:sc_o + 3 * BW]), tiles(w_in[:, sg_o:sg_o + 2 * BW]),
             tiles(w_in[:, sb_o:sb_o + 3 * BW])]
    parts = [panels(p) for p in parts]
    for g, o in zip(gates, outs):
        parts += [panels(tiles(g)), pairs(a[o][0])]
    parts.append(panels(tiles(a["w_o"][0])))
    order = [t + s * FT1 for t in range(FT1) for s in range(2)]
    parts.append(interleave(panels(tiles(a["w_up"][0], order)), pairs(a["w_down"][0]), 2))
    win2, main = a["w_in_2"], 2 * PG * PGW
    parts += [panels(tiles(a["w_mem_kv_2"][0])), panels(tiles(win2[0][:, main:])), panels(tiles(a["w_out_2"][0])),
              interleave(panels(tiles(a["w_up_2"][0])), pairs(a["w_down_2"][0]), 1),
              panels(tiles(a["w_mem_kv_2"][1])), panels(tiles(a["w_kv_2"])), panels(tiles(win2[1][:, main:])),
              panels(tiles(win2[1][:, :main])), panels(tiles(a["w_out_2"][1])),
              interleave(panels(tiles(a["w_up_2"][1])), pairs(a["w_down_2"][1]), 1)]
    wall = np.concatenate(parts)
    assert wall.shape[0] == NPAN - 4
    narrow = panels(tiles(win2[0][:, :main], width=PGW))

    def cols(v):
        return v.reshape(-1, P).T

    def twice(v):
        return np.concatenate([v, v]).reshape(P, 1)

    gb = a["gate_b"][0].reshape(4, D)
    par = np.concatenate(
        [cols(a["mix_norm_g"][0])] + [cols(gb[b]) for b in branch]
        + [cols(a["sc_conv_w"][0].reshape(-1)), cols(a["rw_mu"][0])]
        + [cols(a[n][0].reshape(-1)) for n in ("rw_w0", "rw_a0", "rw_k_k", "rw_k_a", "rw_r_k", "rw_gn_g", "rw_gn_b",
                                               "sg_ln_g", "sg_ln_b", "ffn_norm_g", "ffn_conv_w")]
        + [cols(a["final_norm_g"]), cols(a["norm_mix_2"].reshape(-1)), cols(a["pool_scale_2"][0]),
           cols(a["kv_norm_2"]), twice(a["k_norm_2"]), twice(a["q_norm_2"][0]), cols(a["mem_norm_2"].reshape(-1)),
           twice(a["mem_q_norm_2"][0]), twice(a["mem_q_norm_2"][1]), twice(a["mem_k_norm_2"][0]),
           twice(a["mem_k_norm_2"][1]), cols(a["norm_mlp_2"].reshape(-1)),
           np.broadcast_to(a["sinks_2"][0][None], (P, QH))], 1)
    assert par.shape == (P, NPC)

    def across(v):
        return v.T.reshape(KT, P, T).transpose(1, 0, 2)

    consts, levels = shape_constants()
    import ml_dtypes
    arrays = {
        "wall": wall, "wnarrow": narrow, "par": par, "cst": consts, "lvl": levels.astype(ml_dtypes.bfloat16),
        "x": across(a["x"][0]), "mem": across(a["mem_2"][0]),
        "lora": np.stack([np.concatenate([a["rw_w2"][0], a["rw_a2"][0]]), a["rw_g2"][0]], 1),
        "sg_w": a["sg_w"][0].transpose(2, 0, 1), "sg_b": a["sg_b"][0].reshape(1, -1),
        "pool_w": a["pool_w_2"][0].reshape(PG, 2, PGW, 2 * PGW).transpose(2, 0, 1, 3),
    }
    arrays = {k: np.ascontiguousarray(v) for k, v in arrays.items()}
    nc = bacc.Bacc("TRN2", target_bir_lowering=False, num_devices=1)
    A = {k: nc.dram_tensor(k + "_dram", v.shape, mybir.dt.from_np(v.dtype), kind="ExternalInput").ap()
         for k, v in arrays.items()}
    A["out"] = nc.dram_tensor("out_dram", (P, KT, T), F32, kind="ExternalOutput").ap()
    build(nc, A)
    r = run_bass_kernel_spmd(nc, [{k + "_dram": v for k, v in arrays.items()}], core_ids=[0])
    y = r.results[0]["out_dram"]
    return y.transpose(1, 0, 2).reshape(D, T).T.reshape(1, T, D)
```

```python
import math
from contextlib import ExitStack

import numpy as np

import concourse.bass as bass
from concourse import mybir

F32 = mybir.dt.float32
F32R = mybir.dt.float32r
BF16 = mybir.dt.bfloat16
ALU = mybir.AluOpType
ACT = mybir.ActivationFunctionType
AX_X = mybir.AxisListType.X

P = 128
T = 256
D = 1024
KT = D // P
BW = 256
DFF1 = ((8 * D // 3 + 127) // 128) * 128
FT1 = DFF1 // P
DFF2 = 4 * D
NI1 = FT1 // 2
NI2 = DFF2 // P // 2
RW_ENDS = 1
PT = 16
SLOTS = 3
DECAY = math.exp(-0.5)
QH, KVH = 12, 4
PG, PGW = 4, 96
LN2 = math.log(2.0)

_ORDER = [("rw", 4), ("sc", 3), ("sg", 2), ("sb", 3),
          ("gate0", 4), ("out0", 1), ("gate1", 4), ("out1", 1), ("gate2", 4), ("out2", 1),
          ("gate3", 4), ("out3", 1), ("wo", 4), ("ffn", 3 * NI1),
          ("mkv0", 2), ("in0q", 1), ("in0m", 4), ("wout0", 4), ("ffn0", 2 * NI2),
          ("mkv1", 2), ("kv", 2), ("in1", 4), ("wout1", 4), ("ffn1", 2 * NI2)]
PAN = {}
_at = 0
for _n, _c in _ORDER:
    PAN[_n] = _at
    _at += _c
NPAN = _at
NARROW = PAN["in0m"]

_PCOLS = [("mix_g", 8), ("gate_b", 32), ("sc_w", 6), ("mu", 8), ("w0", 2), ("a0", 2), ("k_k", 2),
          ("k_a", 2), ("r_k", 2), ("gn_g", 2), ("gn_b", 2), ("ln_g", 2), ("ln_b", 2), ("ffn_g", 8),
          ("conv", 6 * FT1), ("fin_g", 8), ("mix2_g", 16), ("pool_s", 6), ("kv_g", 8), ("k_g", 1),
          ("q_g", 1), ("mem_g", 16), ("mq_g", 2), ("mk_g", 2), ("mlp_g", 16), ("sinks", 12)]
PC = {}
_at = 0
for _n, _c in _PCOLS:
    PC[_n] = _at
    _at += _c
NPC = _at

_CCOLS = [("ident", 128), ("ones", 128), ("bones", 128), ("eps", 8), ("suffix", 128), ("strict", 128),
          ("incl", 128), ("dist", 384), ("count", 64)]
CC = {}
_at = 0
for _n, _c in _CCOLS:
    CC[_n] = _at
    _at += _c
NCC = _at
EPS6, EPS5, EPSG, KKB, ONE = range(5)
LEVELS = (1, 2, 4, 8, 16, 32, 64)


def shape_constants():
    c = np.zeros((P, NCC), np.float32)
    r = np.arange(P)

    def put(name, a):
        c[:, CC[name]:CC[name] + a.shape[1]] = a

    put("ident", np.eye(P))
    put("ones", np.ones((P, P)))
    put("bones", (r[:, None] // 64 == r[None, :] // 64) * 1.0)
    put("suffix", (r[:, None] >= r[None, :]) * 1.0)
    put("strict", (r[:, None] < r[None, :]) * 1.0)
    put("incl", (r[:, None] <= r[None, :]) * 1.0)
    key = np.arange(2 * P)[None, :]
    own = r[:, None] - r[None, :]
    both = r[:, None] + P - key
    put("dist", np.concatenate([np.where(own >= 0, -own, -1e32),
                                np.where((both >= 0) & (both < P), -both, -1e32)], 1))
    t = np.arange(16)
    put("count", np.tile(np.concatenate([1.0 / np.minimum(t + 1, w) for w in (2, 4, 8, 16)])[None], (P, 1)))
    e = np.zeros((P, 8))
    e[:, EPS6], e[:, EPS5], e[:, EPSG], e[:, KKB], e[:, ONE] = 1e-6, 1e-5, 64e-5, 10 * LN2, 1.0
    put("eps", e)
    lv = np.zeros((P, len(LEVELS), P), np.float32)
    for i, b in enumerate(LEVELS):
        lv[:, i] = ((r[:, None] // (2 * b) == r[None, :] // (2 * b)) & (r[:, None] % (2 * b) < b)
                    & (r[None, :] % (2 * b) >= b))
    return c, lv


def build(nc, A):
    ctx = ExitStack()
    sems = {}

    def S(name):
        if name not in sems:
            sems[name] = ctx.enter_context(nc.semaphore(name))
        return sems[name]

    base = 16512
    top = [base]

    def place(name, shape, dt=F32, at=None):
        size = int(np.prod(shape[1:])) * (2 if dt == BF16 else 4)
        size = (size + 31) // 32 * 32
        off = top[0] if at is None else at
        h = nc.alloc_sbuf_tensor_at(name, shape, dt, offset=off)
        if at is None:
            top[0] += size
        h_end[name] = off + size
        return h

    h_end = {}
    K = 1024
    raw = place("raw", [P, SLOTS, PT * P])
    whi = place("whi", [P, SLOTS, PT * P], F32R)
    wlo = place("wlo", [P, SLOTS, PT * P], F32R)
    xh = place("xh", [P, KT, T], F32R)
    xl = place("xl", [P, KT, T], F32R)
    x = place("x", [P, KT, T])
    cst = place("cst", [P, NCC])
    lvl = place("lvl", [P, len(LEVELS), P], BF16)
    par = place("par", [P, NPC])
    half = place("half", [P, 36])
    gq8 = place("gq8", [P, 4])
    rstd = place("rstd", [P, T])
    rtmp = place("rtmp", [P, T])
    arena = top[0]

    lora = place("lora", [P, 2, T])
    sgw = place("sgw", [P, 4, P])
    z_rw = place("z_rw", [P, 8, T + 1])
    mt1 = place("mt1", [P, 8, P], at=h_end["sgw"])
    mx = place("mx", [P, 8, P], at=h_end["mt1"])
    zs = place("zs", [P, 8, T])
    y = place("y", [P, 2, T], at=h_end["zs"] - 8 * K)
    b0 = place("b0", [P, 2, 4, 64], at=h_end["zs"] - 6 * K)
    uu = place("uu", [P, 2, 4, 64], at=h_end["zs"] - 2 * K)
    z_sb = place("z_sb", [P, 6, T])
    r4 = top[0]
    gm = place("gm", [P, 8, 4, P])
    z_sc = place("z_sc", [P, 6, T], at=r4)
    ucv = place("ucv", [P, 2, T + 2], at=r4 + 6 * K)
    ycv = place("ycv", [P, 2, T], at=h_end["ucv"])
    z_sg = place("z_sg", [P, 4, T], at=h_end["ycv"])
    sig = place("sig", [P, KT, T])
    sgt = place("sgt", [P, 4, T], at=h_end["sig"] - 8 * K)
    sgv = place("sgv", [P, 2, T], at=h_end["sig"] - 4 * K)
    sgn = place("sgn", [P, 2, T], at=h_end["sig"] - 2 * K)
    merged = place("merged", [P, KT, T])
    wk = place("wk", [P, KT, T], at=h_end["merged"] - 8 * K)
    cum = place("cum", [P, 4, P + 1])
    em = place("em", [P, 4, P + 1])
    ei = place("ei", [P, 4, P])
    ew = place("ew", [P, 4, T])
    mxt = place("mxt", [P, 8, P], at=h_end["merged"])
    mnt = place("mnt", [P, 8, P], at=h_end["em"])
    kk = place("kk", [P, 2, T])
    sbv = place("sbv", [P, 2, T], at=h_end["kk"] - 2 * K)
    ar = place("ar", [P, 4, 2, P])
    bt = place("bt", [P, 4, P])
    kt = place("kt", [P, 4, P])
    kp = place("kp", [P, 2, T])
    bkn = place("bkn", [P, 4, P])
    e2 = place("e2", [P, 2, T], at=h_end["bkn"] - 2 * K)
    vn = place("vn", [P, 2, T])
    bon = place("bon", [P, 2, T])
    gg = place("gg", [P, 2, T])
    st = place("st", [P, 2, 64])
    esc = place("esc", [P, 2])
    mid = place("mid", [P, 4, 1])
    z3 = place("z3", [P, 3 * P])
    l3 = place("l3", [P, 3 * P])
    ysq = place("ysq", [P, 2, T], at=h_end["em"])
    yr = place("yr", [P, 2, T], at=h_end["em"] + 2 * K)
    hh1 = place("hh1", [P, 2, 2, T], F32R)
    hl1 = place("hl1", [P, 2, 2, T], F32R)
    sgb = place("sgb", [1, 4 * P], at=h_end["mid"])

    top[0] = arena
    mh = place("mh", [P, KT, T], F32R)
    ml = place("ml", [P, KT, T], F32R)
    mem = place("mem", [P, KT, T])
    mwk = place("mwk", [P, KT, T])
    at16 = arena + 16 * K
    ffn = top[0]
    upad = place("upad", [P, 2, 2, T + 2])
    cv = place("cv", [P, 2, 2, T])
    sgm = place("sgm", [P, 2, T])
    hid = place("hid", [P, 3, 2, T])
    rel = place("rel", [P, 3, 2, T])
    hh = place("hh", [P, 3, 2, T], F32R)
    hl = place("hl", [P, 3, 2, T], F32R)
    mrstd = place("mrstd", [P, T])
    poolw = place("poolw", [PGW, PG, 2, 2 * PGW])
    l0 = top[0]
    top[0] = ffn
    mk = place("mk", [P, 2, T])
    mv = place("mv", [P, 2, T])
    mvn = place("mvn", [P, 2, T])
    mq = place("mq", [P, 2, T])
    hsq = place("hsq", [P, 2, T])
    hy = place("hy", [P, 2, T])
    ht = place("ht", [P, 2, T])
    hmax = place("hmax", [P, 3, 24])
    wmax = place("wmax", [P, 3, 24])
    mat_end = top[0]
    pm0 = place("pm0", [P, 8, T], at=at16)
    ptm0 = place("ptm0", [P, 4, 2, T], at=at16 + 8 * K)
    top[0] = l0
    zp = place("zp", [PGW, 8, T + 16])
    s2 = place("s2", [PGW, 8, T + 16])
    s4 = place("s4", [PGW, 8, T + 16])
    top[0] = mat_end
    qs = place("qs", [P, 6, T])
    ks = place("ks", [P, 2, T])
    ksw = place("ksw", [P, 2, T])
    vs = place("vs", [P, 2, T])
    vsn = place("vsn", [P, 2, T])
    ss = place("ss", [P, QH, 3 * P])
    pt = place("pt", [P, 8, 3 * P], at=at16)
    pm1 = place("pm1", [P, 8, T], at=h_end["vsn"])
    ptm1 = place("ptm1", [P, 4, 2, T], at=at16)
    wk2 = place("wk2", [P, KT, T], at=h_end["zp"])

    G = [nc.alloc_psum_tensor(f"G{i}", [P, 2, T], F32) for i in range(2)]
    DB = [nc.alloc_psum_tensor(f"D{i}", [P, 2, T], F32) for i in range(4)]
    M = [nc.alloc_psum_tensor(f"M{i}", [P, 2, T], F32) for i in range(2)]
    GR = [G[0], G[1], M[0]]

    def c(name, lo=0, n=P, rows=slice(0, P)):
        return cst[rows, CC[name] + lo:CC[name] + lo + n]

    def eps(i):
        return cst[:, CC["eps"] + i:CC["eps"] + i + 1]

    def pcol(name, i=0, rows=slice(0, P)):
        return par[rows, PC[name] + i:PC[name] + i + 1]

    def four(h):
        return h.rearrange("p j (c t) -> p (j c) t", c=2)

    def flat(bank):
        return bank[:, :, :].rearrange("p a b -> p (a b)")

    class Pan:

        def __init__(self, p, it=0, step=0):
            self.p0 = p
            self.p, self.slot, self.turn = p + it * step, p % SLOTS, p // SLOTS + it * (step // SLOTS)

    def reach(eng, sem, value):
        if not (isinstance(value, int) and value <= 0):
            eng.wait_ge(S(sem), value)

    class Own:

        def __init__(self, eng, sem):
            self.eng, self.sem, self.n = eng, S(sem), 0

        def __call__(self, ins):
            ins.then_inc(self.sem, 1)
            self.n += 1
            self.eng.wait_ge(self.sem, self.n)

    WHAT = {}
    for name, n in _ORDER:
        for i in range(n):
            WHAT[PAN[name] + i] = (name, i)

    OUTS = ("out0", "out1", "out2", "out3")

    W = [("norm", 0)] + [("panel", PAN["rw"] + i) for i in range(4)]
    W += [("rw_low",), ("panel", PAN["sc"]), ("rw_gates",), ("panel", PAN["sc"] + 1), ("rw_cum",),
          ("panel", PAN["sc"] + 2), ("panel", PAN["sg"]), ("rw_key",), ("panel", PAN["sg"] + 1), ("rw_mix",),
          ("panel", PAN["sb"]), ("sg_gelu",), ("panel", PAN["sb"] + 1), ("rw_turn",), ("sc",),
          ("panel", PAN["sb"] + 2), ("sg_mean",)]
    rw = [("rw_prod", i) for i in range(4)] + [("inv_first",)]
    for l in range(1, len(LEVELS)):
        rw += [("inv_t", l), ("inv_x", l)]
    rw += [("rw_rhs", 0), ("rw_sol", 0), ("rw_state",), ("rw_rhs", 1), ("rw_sol", 1), ("rw_out",),
           ("rw_gn1",), ("rw_gn2",)]
    sbs = [[("sg_turn",)], [("sg_mix",), ("sb_turn",)]]
    for h in range(4):
        sbs += [[("sb_z", h), ("sb_e", h)], [("sb_q", h), ("sb_a", h)], [("sb_o", h)]]
    fill = []
    for b in range(4):
        fill += [("panel", PAN[f"gate{b}"] + i) for i in range(4)] + ([("panel", PAN[f"out{b}"])] if b < 3 else [])
    slots = []
    for f in fill:
        if WHAT[f[1]][0] not in OUTS:
            slots.append(("begin", f[1]))
        slots.append(f)
    held = [i for i in range(len(slots)) if i + 1 < len(slots) and WHAT[slots[i + 1][1]][0] in OUTS]
    put = {i: [] for i in range(len(slots))}
    put[0].append(("sg_var",))
    put[1] += sbs.pop(0)
    put[3] += sbs.pop(0)
    room = [i for i in range(4, slots.index(("panel", PAN["out2"]))) if i not in held]
    for k, steps in enumerate(sbs):
        put[room[k * len(room) // len(sbs)]] += steps
    room = [i for i in range(3, len(slots)) if i not in held][:-RW_ENDS]
    for k, step in enumerate(rw):
        put[room[k * len(room) // len(rw)]].append(step)
    for i, f in enumerate(slots):
        W.append(f)
        W += put[i]
    W += [("panel", PAN["out3"]), ("merge_split",)]
    W += [("mem_load",), ("panel", PAN["wo"]), ("panel", PAN["wo"] + 1), ("mem_squares",)]
    W += [("panel", PAN["wo"] + 2), ("mem_stat",), ("panel", PAN["wo"] + 3)]
    W += [("norm", 1), ("mem_norm", 0), ("ffn", 0), ("squares", 2)]
    W += [("panel", PAN["mkv0"]), ("root", 2), ("final_norm",), ("parts", 3), ("sums", 3)]
    W += [("panel", PAN["mkv0"] + 1), ("panel", PAN["in0q"]), ("hn", 0), ("turn_mv", 0), ("root", 3),
          ("read", PAN["in0q"]), ("panel", PAN["in0m"]), ("hn", 1), ("mem_norm", 1), ("panel", PAN["in0m"] + 1),
          ("score_m", 0), ("panel", PAN["in0m"] + 2), ("pool", 3), ("turn_p", 0), ("panel", PAN["in0m"] + 3),
          ("pool", 2), ("pv_m", 0), ("pool", 1), ("pool", 0), ("pool_mm",)]
    W += [("panel", PAN["wout0"] + i) for i in range(4)]
    W += [("parts", 4), ("sums", 4), ("ffn", 1), ("parts", 5), ("sums", 5)]
    W += [("panel", PAN["mkv1"]), ("panel", PAN["mkv1"] + 1), ("root", 5),
          ("panel", PAN["kv"]), ("parts5b",), ("panel", PAN["kv"] + 1), ("hn", 2), ("turn_mv", 1),
          ("panel", PAN["in1"]), ("hn", 3), ("swap_k",), ("turn_v",), ("panel", PAN["in1"] + 1), ("hn", 4),
          ("panel", PAN["in1"] + 2), ("hn", 5), ("score_m", 1), ("panel", PAN["in1"] + 3), ("hn", 6), ("turn_p", 1),
          ("hn", 7), ("score_s", 0), ("exp_s", 0), ("score_s", 1), ("soft_s", 0), ("pv_m", 1), ("exp_s", 1),
          ("score_s", 2), ("soft_s", 1), ("pv_s", 0), ("pv_s", 1), ("exp_s", 2), ("pv_s", 2), ("pv_s", 3),
          ("soft_s", 2), ("pv_s", 4), ("pv_s", 5)]
    W += [("panel", PAN["wout1"] + i) for i in range(4)] + [("parts", 6), ("sums", 6), ("ffn", 2), ("store",)]

    RES = ("wo", "wout0", "wout1")

    FF = [(NI1, 2, PAN["ffn"], 1), (NI2, 1, PAN["ffn0"], 3), (NI2, 1, PAN["ffn1"], 5)]

    XLN = {"rw": 4, "wo": 8, "ffn": 12, "in0q": 16, "wout0": 20, "ffn0": 24, "kv": 28, "wout1": 32, "ffn1": 36}
    RESN = {"wo": 0, "wout0": 3, "wout1": 5}
    FRES = [1, 4, 6]

    SCALED = ("in0q", "in0m", "kv", "in1")
    gbank, gread = {}, {}
    reads = {"g_act": 0, "g_scaled": 0}
    use = 0
    for step in W:
        if step[0] == "panel":
            if WHAT[step[1]][0] in OUTS:
                use += 4
            elif WHAT[step[1]][0] not in RES:
                gbank[step[1]] = use % 2
                sem = "g_scaled" if WHAT[step[1]][0] in SCALED else "g_act"
                reads[sem] += 1
                gread[step[1]] = (sem, reads[sem])
                use += 1

    def projected(eng, name, i):
        sem, count = gread[PAN[name] + i]
        eng.wait_ge(S(sem), count)

    def walk(eng, handlers):
        for step in W:
            if step[0] in handlers:
                handlers[step[0]](*step[1:])

    def ffn_walk(eng, f, up, down, done=None):
        ni, nu, p0, _ = FF[f]
        body = 3
        up(0, [Pan(p0 + u) for u in range(nu)], 0)

        def pair(i, it, step):
            at = p0 + nu + i * (nu + 1)
            idx = i + it * body
            up(idx + 1, [Pan(at + u, it, step) for u in range(nu)], i + 1)
            down(idx, Pan(at + nu, it, step), i, False)

        pair(0, 0, 0)
        n = (ni - 3) // body
        with eng.Fori(0, n) as it:
            for u in range(body):
                pair(1 + u, it, body * (nu + 1))
        if done is not None:
            done[0] = p0 + nu + (1 + n * body) * (nu + 1) + 2
        for i in range(1 + n * body, ni - 1):
            pair(i, 0, 0)
        down(ni - 1, Pan(p0 + ni * (nu + 1) - 1), ni - 1, True)

    block = ctx.enter_context(nc.Block())

    @block.sync
    def _(sp):
        def load(pan, src, width=PT * P):
            if not (isinstance(pan.p, int) and pan.p < SLOTS):
                sp.wait_ge(S("w_lo"), pan.p - SLOTS + 1)
            sp.dma_start(raw[:, pan.slot, 0:width], src).then_inc(S(f"w_land{pan.slot}"), 16)

        def run(lo, hi, skip):
            n = (hi - lo) // SLOTS
            with sp.Fori(0, n) as it:
                for u in range(SLOTS):
                    load(Pan(lo + u, it, SLOTS), A["wall"][bass.ds(it * SLOTS + (lo + u - skip), 1), :, :]
                         .rearrange("a p n -> p (a n)"))
            for p in range(lo + n * SLOTS, hi):
                load(Pan(p), A["wall"][p - skip])

        for i in range(4):
            sp.dma_start(x[:, 2 * i:2 * i + 2, :], A["x"][:, 2 * i:2 * i + 2, :]).then_inc(S(f"x_moved{i}"), 16)
        for p in range(SLOTS):
            load(Pan(p), A["wall"][p])
        run(SLOTS, NARROW, 0)
        for i in range(4):
            load(Pan(NARROW + i), A["wnarrow"][i], PT * PGW)
        run(NARROW + 4, NPAN, 4)
        for i in range(4):
            sp.wait_ge(S("x_ready"), 4 * 6 + i + 1)
            sp.dma_start(A["out"][:, 2 * i:2 * i + 2, :], x[:, 2 * i:2 * i + 2, :]).then_inc(S(f"x_moved{i}"), 16)
        for i in range(4):
            sp.wait_ge(S(f"x_moved{i}"), 32)

    @block.gpsimd
    def _(pool):
        own = Own(pool, "pool_own")
        tt = nc.gpsimd.tensor_tensor

        def inv_mask(l):
            if l == 0:
                pool.wait_ge(S("ld_lvl"), 16)
                pool.wait_ge(S("rw_prod"), 8)
            else:
                reach(pool, "inv_T", l - 1)
                pool.wait_ge(S("rw_prod"), 8)
            if l == 1:
                pool.wait_ge(S("inv_x"), 1)
            nc.gpsimd.tensor_tensor(mnt[:], gm[:, :, 0, :], lvl[:, l:l + 1, :].broadcast_to([P, 8, P]),
                                    ALU.mult).then_inc(S("inv_n"), 1)

        def sc():
            projected(pool, "sc", 2)
            own(tt(ucv[:, :, 2:T + 2], z_sc[:, 2:4, :], z_sc[:, 4:6, :], ALU.mult))
            for i, tap in enumerate((ycv[:, :, :], z_sc[:, 2:4, :], z_sc[:, 4:6, :])):
                for j in range(2):
                    ins = nc.gpsimd.tensor_scalar(tap[:, j, :], ucv[:, j, i:i + T], pcol("sc_w", 2 * i + j), None,
                                                  ALU.mult)
            own(ins)
            own(tt(ycv[:], ycv[:], z_sc[:, 2:4, :], ALU.add))
            own(tt(ycv[:], ycv[:], z_sc[:, 4:6, :], ALU.add))
            tt(ycv[:], ycv[:], z_sc[:, 0:2, :], ALU.mult).then_inc(S("sc_y"), 1)

        def add_squares(buf, sem, before, done):
            for i in range(1, 4):
                pool.wait_ge(S(sem), before + i + 1)
                own(tt(buf[:, 0:2, :], buf[:, 0:2, :], buf[:, 2 * i:2 * i + 2, :], ALU.add))
            tt(buf[:, 0, :], buf[:, 0, :], buf[:, 1, :], ALU.add).then_inc(S(done), 1)

        def sums(n):
            add_squares(wk2, "sq", 4 * n, "sq_sum")

        def windows(g):
            projected(pool, "in0m", 3 - g)
            prs = slice(2 * g, 2 * g + 2)
            z, a, b = zp[:, prs, :], s2[:, prs, :], s4[:, prs, :]
            own(tt(a[:, :, 1:T + 16], z[:, :, 1:T + 16], z[:, :, 0:T + 15], ALU.add))
            if g >= 1:
                own(tt(b[:, :, 3:T + 16], a[:, :, 3:T + 16], a[:, :, 1:T + 14], ALU.add))
            if g >= 2:
                own(tt(a[:, :, 7:T + 16], b[:, :, 7:T + 16], b[:, :, 3:T + 12], ALU.add))
            if g >= 3:
                own(tt(b[:, :, 15:T + 16], a[:, :, 15:T + 16], a[:, :, 7:T + 8], ALU.add))
            s_, win = (a, b)[g % 2], 2 << g
            count = c("count", 16 * g, 16, slice(0, PGW)).unsqueeze(1).broadcast_to([PGW, 2, 16])
            tt(s_[:, :, 16:32], s_[:, :, 16:32], count, ALU.mult)
            own(nc.gpsimd.tensor_scalar(s_[:, :, 32:T + 16], s_[:, :, 32:T + 16], 1.0 / win, None, ALU.mult))
            tt(z[:, :, 16:T + 16], s_[:, :, 16:T + 16], z[:, :, 16:T + 16], ALU.subtract).then_inc(S("pool_d"), 1)

        nc.gpsimd.memset(ucv[:, :, 0:2], 0.0)
        pool.wait_ge(S("ld_par"), 16)
        walk(pool, {"pool": windows, "sums": sums, "sc": sc,
                    "mem_squares": lambda: add_squares(mwk, "mem_sq", 0, "mem_sum"),
                    "inv_first": lambda: inv_mask(0),
                    "inv_t": lambda l: inv_mask(l)})

    @block.tensor
    def _(pe):
        mm = nc.tensor.matmul
        ident, ones, bones = c("ident"), c("ones"), c("bones")
        used = {"g": 0}
        freed = {}
        read_by_dve = [0]

        def free(bank):
            if bank in freed:
                pe.wait_ge(S(freed[bank][0]), freed[bank][1])

        def tile3(out, pan, q, width, hi, lo, start, stop, skip=False):
            w_h = whi[:, pan.slot, q * width:(q + 1) * width]
            w_l = wlo[:, pan.slot, q * width:(q + 1) * width]
            mm(out, w_h, hi, start=start, stop=False, skip_group_check=skip)
            mm(out, w_h, lo, start=False, stop=False, skip_group_check=skip)
            return mm(out, w_l, hi, start=False, stop=stop, skip_group_check=skip)

        begun = {}

        def tiles_of(out, pan, w, a_h, a_l, ns):
            for n in ns:
                for k in range(KT):
                    ins = tile3(out[0:w, n, :], pan, n * KT + k, w, a_h[:, k, :], a_l[:, k, :], k == 0, k == KT - 1)
            return ins

        def first_panel(out, pan, count):
            order = {XLN["wout0"]: (3, 2, 1, 0), XLN["wout1"]: (3, 0, 1, 2)}.get(count, (0, 1, 2, 3))
            for at, i in enumerate(order):
                pe.wait_ge(S("xl"), count - 3 + at)
                for k in (2 * i, 2 * i + 1):
                    for n in range(2):
                        ins = tile3(out[:, n, :], pan, n * KT + k, P, xh[:, k, :], xl[:, k, :],
                                    at == 0 and k % 2 == 0 and n == 0, at == 3 and k % 2 == 1, skip=True)
            return ins

        pe.wait_ge(S("ld_cst"), 16)

        def norm_stat(n):
            free("M1")
            if n == 0 or n >= 3:
                pe.wait_ge(S("sq_sum" if n else "sq_sum0"), max(n - 2, 1))
                ins = mm(M[1][:, 0, :], ones, (wk2 if n else wk)[:, 0, :])
            else:
                for i in range(4):
                    pe.wait_ge(S("sq"), 4 * n + i + 1)
                    for k in (2 * i, 2 * i + 1):
                        ins = mm(M[1][:, 0, :], ones, wk2[:, k, :], start=k == 0, stop=k == KT - 1)
            ins.then_inc(S("stat"), 1)
            freed["M1"] = ("rs_read", n + 1)

        def begin(p):
            panel(p, (0,))

        def panel(p, ns=(0, 1)):
            name, i = WHAT[p]
            pan = Pan(p)
            if p in begun:
                tiles_of(begun[p], pan, P, xh, xl, (1,)).then_inc(S("pe_panel"), 1)
                return
            pe.wait_ge(S("w_lo"), p + 1)
            if name in OUTS:
                b = int(name[3])
                pe.wait_ge(S("branch"), b + 1)
                for i in range(4):
                    k = used["g"] % 2
                    used["g"] += 1
                    free(f"G{k}")
                    for n in (2 * i, 2 * i + 1):
                        for q in range(2):
                            ins = tile3(G[k][:, n % 2, :], pan, n * 2 + q, P, hh1[:, b % 2, q, :],
                                        hl1[:, b % 2, q, :], q == 0, q == 1)
                    if i < 3:
                        ins.then_inc(S("out_pair"), 1)
                    read_by_dve[0] += 1
                    freed[f"G{k}"] = ("g_dve", read_by_dve[0])
                ins.then_inc(S("pe_panel"), 1)
                return
            a_h, a_l = xh, xl
            if name[:3] == "mkv":
                pe.wait_ge(S("ml"), 1 + int(name[3]))
                a_h, a_l = mh, ml
            elif name == "in1":
                pe.wait_ge(S("ml"), 3)
                a_h, a_l = mh, ml
            if name in RES:
                bank = f"D{i}"
                out = DB[i]
                free(bank)
            else:
                k = used["g"] % 2
                used["g"] += 1
                bank, out = f"G{k}", G[k]
                free(bank)
                freed[bank] = gread[p]
            narrow = name == "in0m"
            w = PGW if narrow else P
            if i == 0 and name in XLN:
                ins = first_panel(out, pan, XLN[name])
            else:
                ins = tiles_of(out, pan, w, a_h, a_l, ns)
            if len(ns) == 1:
                begun[p] = out
                return
            ins.then_inc(S("pe_panel"), 1)
            if name in RES:
                freed[bank] = ("x_ready", 4 * RESN[name] + i + 1)

        def rw_gates():
            pe.wait_ge(S("ld_lora_pool"), 16)
            pe.wait_ge(S("rw_e2"), 1)
            for j in range(2):
                mm(DB[0][:, j, :], lora[0:64, 0, j * P:(j + 1) * P], e2[0:64, 0, :])
            for j in range(2):
                mm(DB[1][:, j, :], lora[64:128, 0, j * P:(j + 1) * P], zs[64:128, 6, :])
            for j in range(2):
                ins = mm(DB[2][:, j, :], lora[:, 1, j * P:(j + 1) * P], e2[:, 1, :])
            ins.then_inc(S("rw_low"), 1)

        def rw_key():
            pe.wait_ge(S("rw_ksq"), 1)
            mm(DB[3][:, :, :], bones, bon[:, :, :]).then_inc(S("rw_kss"), 1)

        def rw_turn():
            pe.wait_ge(S("rw_low_read"), 1)
            pe.wait_ge(S("rw_kt"), 1)
            for ch in range(2):
                for j in range(2):
                    nc.tensor.transpose(DB[0][:, ch, j * P:(j + 1) * P], zs[:, 4 + j, ch * P:(ch + 1) * P], ident)
            for j in range(2):
                nc.tensor.transpose(DB[1][:, 0, j * P:(j + 1) * P], bt[:, 2 * j, :], ident)
            for j in range(2):
                nc.tensor.transpose(DB[1][:, 1, j * P:(j + 1) * P], kt[:, 2 * j, :], ident)
            mm(DB[2][:, :, :], bones, bon[:, :, :]).then_inc(S("rw_turned"), 1)

        def rw_prod(i):
            for m in (2 * i, 2 * i + 1):
                ch, h = divmod(m, 4)
                j, o = h // 2, 64 * (h % 2)
                bank = m % 2
                free(f"M{bank}")
                if m >= 2:
                    pe.wait_ge(S("rw_prod"), m - 1)
                jc = 2 * j + ch
                rhs = ar[o:o + 64, jc, :, :]
                mm(M[bank][:, 0, :], bt[o:o + 64, jc, :], rhs)
                mm(M[bank][:, 1, :], kt[o:o + 64, jc, :], rhs).then_inc(S("rw_gp"), 1)
                freed[f"M{bank}"] = ("rw_prod", m + 1)

        def inv_first():
            pe.wait_ge(S("inv_x"), 1)
            for g in range(2):
                free(f"M{g}")
                for m in range(4):
                    ins = nc.tensor.transpose(M[g][:, m // 2, (m % 2) * P:(m % 2 + 1) * P], mxt[:, 4 * g + m, :], ident)
            ins.then_inc(S("inv_t0"), 1)
            freed["M0"] = freed["M1"] = ("inv_x0", 1)

        def inv_t(l):
            pe.wait_ge(S("inv_n"), l + 1)
            pe.wait_ge(S("inv_x0"), 1)
            if l >= 2:
                pe.wait_ge(S("inv_x"), l)
            for g in range(2):
                free(f"M{g}")
                for m in range(4):
                    ins = mm(M[g][:, m // 2, (m % 2) * P:(m % 2 + 1) * P], mnt[:, 4 * g + m, :], mx[:, 4 * g + m, :])
            ins.then_inc(S("inv_T"), 1)
            freed["M0"] = freed["M1"] = ("inv_c", l)

        def inv_x(l):
            pe.wait_ge(S("inv_c"), l)
            if l == 1:
                pe.wait_ge(S("rw_bonus"), 1)
                pe.wait_ge(S("sg_y"), 1)
            for g in range(2):
                if l >= 2:
                    pe.wait_ge(S("inv_x"), l)
                for m in range(4):
                    ins = mm(DB[2 + g][:, m // 2, (m % 2) * P:(m % 2 + 1) * P], mt1[:, 4 * g + m, :], mxt[:, 4 * g + m, :])
            if l < len(LEVELS) - 1:
                for g in range(2):
                    for m in range(4):
                        ins = mm(M[g][:, m // 2, (m % 2) * P:(m % 2 + 1) * P], mxt[:, 4 * g + m, :], mt1[:, 4 * g + m, :])
                freed["M0"] = freed["M1"] = ("inv_x", l + 1)
            ins.then_inc(S("inv_p"), 1)

        def rw_rhs(ch):
            free("M0")
            free("M1")
            if ch == 0:
                pe.wait_ge(S("inv_x"), len(LEVELS))
            else:
                pe.wait_ge(S("rw_state"), 1)
            for h in range(4):
                j, o = h // 2, 64 * (h % 2)
                out = M[h % 2][:, 0, j * 64:(j + 1) * 64]
                ins = mm(out, gm[:, 4 * ch + h, 2, :], vn[:, ch, h * 64:(h + 1) * 64],
                         start=True, stop=ch == 0)
                if ch:
                    ins = mm(out, ar[o:o + 64, 2 * j + ch, 0, :], st[o:o + 64, j, :],
                             start=False, stop=True)
            ins.then_inc(S("rw_rhs"), 1)
            freed["M0"] = freed["M1"] = ("rw_b0", 2 * ch + 2)

        def rw_sol(ch):
            free("M0")
            for h in range(4):
                ins = mm(M[0][:, 0, h * 64:(h + 1) * 64], mxt[:, 4 * ch + h, :], b0[:, ch, h, :])
            ins.then_inc(S("rw_sol"), 1)
            freed["M0"] = ("rw_uu", ch + 1)

        def rw_state():
            pe.wait_ge(S("rw_uu"), 1)
            free("M1")
            for h in range(4):
                j, o = h // 2, 64 * (h % 2)
                out = M[1][o:o + 64, j, 0:64]
                mm(out, bkn[:, j, o:o + 64], uu[:, 0, h, :], start=True, stop=False)
                ins = mm(out, bkn[:, 2 + j, o:o + 64], vn[:, 0, h * 64:(h + 1) * 64], start=False, stop=True)
            ins.then_inc(S("rw_sp"), 1)
            freed["M1"] = ("rw_state", 1)

        def rw_out():
            pe.wait_ge(S("rw_uu"), 2)
            for h in range(4):
                j, o = h // 2, 64 * (h % 2)
                for ch in range(2):
                    out = DB[2][o:o + 64, j, ch * P:(ch + 1) * P]
                    mm(out, uu[:, ch, h, :], gm[:, 4 * ch + h, 1, :], start=True, stop=False)
                    ins = mm(out, vn[:, ch, h * 64:(h + 1) * 64], gm[:, 4 * ch + h, 3, :], start=False, stop=ch == 0)
                    if ch:
                        ins = mm(out, st[o:o + 64, j, :], ar[o:o + 64, 2 * j + ch, 1, :], start=False, stop=True)
            ins.then_inc(S("rw_yp"), 1)

        def rw_gn1():
            pe.wait_ge(S("rw_y"), 1)
            mm(DB[3][:, :, :], bones, y[:, :, :]).then_inc(S("rw_mean"), 1)

        def rw_gn2():
            pe.wait_ge(S("rw_ysq"), 1)
            mm(DB[3][:, :, :], bones, ysq[:, :, :]).then_inc(S("rw_var"), 1)
            freed.update({"D0": ("sb_out", 4), "D1": ("sb_arg", 4), "D2": ("rw_y", 1), "D3": ("rw_rs_read", 1)})

        def sg_sum(src, sem, need):
            pe.wait_ge(S(need[0]), need[1])
            for j in range(2):
                ins = mm(DB[3][:, 0, :], ones, src[:, j, :], start=j == 0, stop=j == 1)
            ins.then_inc(S(sem), 1)

        def sg_turn():
            pe.wait_ge(S("sg_norm"), 1)
            for n in range(2):
                for j in range(2):
                    ins = nc.tensor.transpose(DB[3][:, n, j * P:(j + 1) * P], sgv[:, j, n * P:(n + 1) * P], ident)
            ins.then_inc(S("sg_turned"), 1)

        def sg_mix():
            pe.wait_ge(S("sg_vn"), 1)
            pe.wait_ge(S("sg_tril"), 1)
            pe.wait_ge(S("ld_sgb"), 16)
            for n in range(2):
                for g in range(4):
                    j, o = g // 2, 64 * (g % 2)
                    out = DB[3][o:o + 64, j, n * P:(n + 1) * P]
                    mm(out, sgn[:, n, g * 64:(g + 1) * 64], sgw[:, g, :], start=True, stop=False)
                    ins = mm(out, ones[0:1, 0:64], sgb[0:1, g * P:(g + 1) * P], start=False, stop=True)
            ins.then_inc(S("sg_mixed"), 1)

        def sb_turn():
            projected(pe, "sb", 2)
            pe.wait_ge(S("rw_nat"), 1)
            for s_ in range(2):
                for j in range(2):
                    ins = nc.tensor.transpose(DB[1][:, s_, j * P:(j + 1) * P], z_sb[:, 4 + j, s_ * P:(s_ + 1) * P], ident)
            ins.then_inc(S("sb_turned"), 1)

        d0 = DB[0]
        d1 = DB[1]

        def sb_z(h):
            j, o = h // 2, 64 * (h % 2)
            if h:
                pe.wait_ge(S("sb_out"), h)
            mm(flat(d0)[:, 0:256], z_sb[o:o + 64, 2 + j, 0:P], z_sb[o:o + 64, j, :])
            mm(flat(d0)[:, 256:384], z_sb[o:o + 64, 2 + j, P:T], z_sb[o:o + 64, j, P:T]).then_inc(S("sb_zp"), 1)

        def sb_q(h):
            pe.wait_ge(S("ld_masks"), 16)
            pe.wait_ge(S("sb_sp"), h + 1)
            if h == 0:
                pe.wait_ge(S("sb_vn"), 1)
            mm(flat(d1)[:, 0:256], c("suffix"), l3[:, 0:256], start=True, stop=False, skip_group_check=True)
            mm(flat(d1)[:, 128:256], ones, l3[:, 256:384], start=False, stop=True, skip_group_check=True)
            mm(flat(d1)[:, 256:384], c("suffix"), l3[:, 256:384], skip_group_check=True).then_inc(S("sb_qp"), 1)

        def sb_o(h):
            o = 64 * (h % 2)
            pe.wait_ge(S("sb_att"), h + 1)
            out = flat(d0)[o:o + 64, 0:256]
            mm(out, sbv[:, 0, h * 64:(h + 1) * 64], l3[:, 0:256], start=True, stop=False, skip_group_check=True)
            mm(out[:, 128:256], sbv[:, 1, h * 64:(h + 1) * 64], l3[:, 256:384], start=False, stop=True,
               skip_group_check=True).then_inc(S("sb_op"), 1)

        def ffn(f):
            ni, nu, p0, r0 = FF[f]
            ring = G if nu == 2 else GR
            for b in ("G0", "G1", "M0", "D0", "D1", "D2", "D3"):
                free(b)

            def up(j, pans, js):
                for u, pan in enumerate(pans):
                    pe.wait_ge(S("w_lo"), pan.p + 1)
                    if js >= nu % 2 + 1:
                        pe.wait_ge(S(f"up_read{f}"), nu * (j - 1) + u + 1 if nu == 2 else j - 1)
                    bank = ring[u if nu == 2 else js % 3]
                    if pan.p0 == p0 and isinstance(pan.p, int) and pan.p == p0:
                        ins = first_panel(bank, pan, XLN[WHAT[p0][0]])
                    else:
                        ins = tiles_of(bank, pan, P, xh, xl, (0, 1))
                    ins.then_inc(S("pe_panel"), 1)
                    if isinstance(j, int) and j == 0 and f:
                        norm_stat(2 * f + 2)

            def down(i, pan, js, last):
                pe.wait_ge(S("w_lo"), pan.p + 1)
                pe.wait_ge(S(f"hid{f}"), nu * i + nu)
                for n in range(8):
                    for q in range(2):
                        ins = tile3(DB[n // 2][:, n % 2, :], pan, 2 * n + q, P, hh[:, js % 3, q, :],
                                    hl[:, js % 3, q, :], js == 0 and n % 2 == 0 and q == 0, last and q == 1, skip=True)
                    if last and n in (1, 3, 5):
                        ins.then_inc(S("down_pair"), 1)
                ins.then_inc(S("pe_panel"), 1)

            ffn_walk(pe, f, up, down)
            for i in range(4):
                freed[f"D{i}"] = ("x_ready", 4 * FRES[f] + i + 1)
            n = ni * nu
            for b in ("G0", "G1", "M0"):
                freed[b] = (f"up_read{f}", n)

        def mem_stat():
            free("M1")
            pe.wait_ge(S("mem_sum"), 1)
            mm(M[1][:, 0, :], ones, mwk[:, 0, :]).then_inc(S("mem_st"), 1)
            freed["M1"] = ("mem_rs_read", 1)

        def hn(i):
            pe.wait_ge(S("hn_sq"), i + 1)
            free("M1")
            mm(M[1][:, :, :], bones, hsq[:, :, :]).then_inc(S("hn_ss"), 1)
            freed["M1"] = ("hn_read", i + 1)

        def turn(src, need, sem, bank):
            projected(pe, *need)
            free(bank)
            b = {"M0": M[0], "D3": DB[3]}[bank]
            for s_ in range(2):
                for j in range(2):
                    ins = nc.tensor.transpose(b[:, s_, j * P:(j + 1) * P], src[:, j, s_ * P:(s_ + 1) * P], ident)
            ins.then_inc(S(sem), 1)

        def turn_mv(l):
            turn(mv, (f"mkv{l}", 1), "mv_t", "M0")
            freed["M0"] = ("mvn", l + 1)

        def turn_v():
            turn(vs, ("kv", 1), "vs_t", "M0")
            freed["M0"] = ("vsn", 1)

        def score_m(l):
            pe.wait_ge(S("hn"), 2 if l == 0 else 5)
            for h in range(4):
                j, o = h // 2, 64 * (h % 2)
                free(f"D{h}")
                for tt in range(2):
                    ins = mm(DB[h][:, tt, :], mq[o:o + 64, j, tt * P:(tt + 1) * P], mk[o:o + 64, j, :])
                ins.then_inc(S("sm"), 1)
                freed[f"D{h}"] = ("sm_exp", 8 * l + 2 * h + 2)

        def turn_p(l):
            pm = (pm0, pm1)[l]
            for h in range(4):
                free(f"D{h}")
                pe.wait_ge(S("sm_p"), 4 * l + h + 1)
                for mt in range(2):
                    for tt in range(2):
                        ins = nc.tensor.transpose(DB[h][:, mt, tt * P:(tt + 1) * P],
                                                  pm[:, 2 * h + tt, mt * P:(mt + 1) * P], ident)
                ins.then_inc(S("sm_t"), 1)
                freed[f"D{h}"] = ("sm_pt", 4 * l + h + 1)

        def pv_m(l):
            ptm = (ptm0, ptm1)[l]
            free("M0")
            pe.wait_ge(S("mvn"), l + 1)
            pe.wait_ge(S("sm_pt"), 4 * l + 4)
            for h in range(4):
                j, o = h // 2, 64 * (h % 2)
                for mt in range(2):
                    ins = mm(M[0][o:o + 64, j, :], mvn[:, mt, h * 64:(h + 1) * 64], ptm[:, h, mt, :],
                             start=mt == 0, stop=mt == 1)
            ins.then_inc(S("pvm"), 1)
            freed["M0"] = ("xl", 17 if l == 0 else 29)

        def pool_mm():
            pe.wait_ge(S("ld_lora_pool"), 32)
            for i in range(3):
                free(f"D{i}")
            for n, g in enumerate((3, 2, 1, 0)):
                pe.wait_ge(S("pool_d"), n + 1)
                at = g * 2 * PGW
                for lo, hi in ([(0, 128), (128, 192)], [(0, 64), (64, 192)])[g % 2]:
                    t, o = divmod(at + lo, P)
                    for ck in range(2):
                        ins = mm(DB[t // 2][o:o + hi - lo, t % 2, :], poolw[:, g, ck, lo:hi],
                                 zp[:, 2 * g + ck, 16:16 + T], start=ck == 0, stop=ck == 1)
                if g < 3:
                    ins.then_inc(S("pool_p"), 1)
                    freed[f"D{g}"] = ("xl", 17 + n)

        def score_s(g):
            pe.wait_ge(S("hn"), 6 + g)
            pe.wait_ge(S("ksw"), 1)
            for h in range(4 * g, 4 * g + 4):
                b = h % 4
                free(f"D{b}")
                j, o = h // 2, 64 * (h % 2)
                kvh = h // 3
                src = ks if kvh % 2 == h % 2 else ksw
                f_ = flat(DB[b])
                mm(f_[:, 0:P], qs[o:o + 64, j, 0:P], src[o:o + 64, kvh // 2, 0:P])
                mm(f_[:, P:3 * P], qs[o:o + 64, j, P:T], src[o:o + 64, kvh // 2, :]).then_inc(S("ws"), 1)
                freed[f"D{b}"] = ("ws_read", h + 1)

        def pv_s(j):
            for h in (2 * j, 2 * j + 1):
                b = h % 2
                free(f"D{b}")
                pe.wait_ge(S("ws_p"), h + 1)
                for i in range(3):
                    ins = nc.tensor.transpose(flat(DB[b])[:, i * P:(i + 1) * P], ss[:, h, i * P:(i + 1) * P], ident)
                ins.then_inc(S("ws_t"), 1)
                freed[f"D{b}"] = ("ws_pt", h + 1)
            bank = ("D2", "D3", "M1")[j // 2]
            B = (DB[2], DB[3], M[1])[j // 2]
            if j % 2 == 0:
                free(bank)
            pe.wait_ge(S("vsn"), 1)
            for h in (2 * j, 2 * j + 1):
                o, kvh = 64 * (h % 2), h // 3
                pe.wait_ge(S("ws_pt"), h + 1)
                v = [vsn[:, i, kvh * 64:(kvh + 1) * 64] for i in range(2)]
                pr = [pt[:, h % 8, i * P:(i + 1) * P] for i in range(3)]
                mm(B[o:o + 64, j % 2, 0:P], v[0], pr[0])
                mm(B[o:o + 64, j % 2, P:T], v[0], pr[1], start=True, stop=False)
                ins = mm(B[o:o + 64, j % 2, P:T], v[1], pr[2], start=False, stop=True)
            ins.then_inc(S("ws_o"), 1)
            freed[bank] = ("xl", 30 + j // 2)

        walk(pe, {"begin": begin, "norm": norm_stat, "root": norm_stat, "panel": panel,
                  "rw_gates": rw_gates, "rw_key": rw_key, "rw_turn": rw_turn, "rw_prod": rw_prod,
                  "inv_first": inv_first, "inv_t": inv_t, "inv_x": inv_x, "rw_rhs": rw_rhs, "rw_sol": rw_sol,
                  "rw_state": rw_state, "rw_out": rw_out, "rw_gn1": rw_gn1, "rw_gn2": rw_gn2,
                  "sg_mean": lambda: sg_sum(z_sg[:, 2:4, :], "sg_s", ("sg_gelu", 1)),
                  "sg_var": lambda: sg_sum(sgn, "sg_v", ("sg_sq", 1)),
                  "sg_turn": sg_turn, "sg_mix": sg_mix, "sb_turn": sb_turn, "sb_z": sb_z, "sb_q": sb_q,
                  "sb_o": sb_o, "ffn": ffn, "mem_stat": mem_stat, "hn": hn, "turn_mv": turn_mv,
                  "turn_v": turn_v, "score_m": score_m, "turn_p": turn_p, "pv_m": pv_m, "pool_mm": pool_mm,
                  "score_s": score_s, "pv_s": pv_s})

    HEADS = [(mk, "mk_g", 0, ("mkv0", 0)), (mq, None, 0, ("in0q", 0)), (mk, "mk_g", 1, ("mkv1", 0)),
             (ks, "k_g", 0, ("kv", 0)), (mq, None, 1, ("in1", 0)), (qs[:, 0:2, :], None, 2, ("in1", 1)),
             (qs[:, 2:4, :], None, 2, ("in1", 2)), (qs[:, 4:6, :], None, 2, ("in1", 3))]
    NORMS = {0: (0, 0, 0, ("mix_g", 0)), 1: (4, 8, PAN["wo"] + 4, ("ffn_g", 0)),
             3: (8, 12, PAN["mkv0"], ("mix2_g", 0)), 4: (12, 20, PAN["wout0"] + 4, ("mlp_g", 0)),
             5: (16, 24, PAN["mkv1"], ("kv_g", 0)), 6: (24, 32, PAN["wout1"] + 4, ("mlp_g", 8))}
    slopes = [2.0 ** (-8.0 * (i + 1) / QH) for i in range(QH)]

    @block.scalar
    def _(act):
        fn = nc.scalar.activation
        own = Own(act, "act_own")

        def signal(ins, name):
            ins.then_inc(S(name), 1)

        table = [None]

        def tables(name):
            if table[0] != name:
                nc.scalar.preload_act_table_set(name)
                table[0] = name

        def ln(*args, **kw):
            tables("natural_log_exp_and_others")
            return fn(*args, ACT.Ln, **kw)

        tables("natural_log_exp_and_others")
        for name, dst, src in (("cst", cst[:, 0:CC["suffix"]], A["cst"][:, 0:CC["suffix"]]), ("par", par[:], A["par"]),
                               ("lora_pool", lora[:], A["lora"]),
                               ("masks", cst[:, CC["suffix"]:NCC], A["cst"][:, CC["suffix"]:NCC]),
                               ("sgw_mem", sgw[:], A["sg_w"]), ("lvl", lvl[:], A["lvl"]),
                               ("sgb", sgb[:], A["sg_b"])):
            act.dma_start(dst, src).then_inc(S("ld_" + name), 16)

        done = [0]

        def split(pan):
            w = PT * (PGW if isinstance(pan.p, int) and NARROW <= pan.p < NARROW + 4 else P)
            act.wait_ge(S(f"w_land{pan.slot}"), 16 * (pan.turn + 1))
            if not (isinstance(pan.p, int) and pan.p < SLOTS):
                act.wait_ge(S("pe_panel"), pan.p - SLOTS + 1)
            signal(fn(whi[:, pan.slot, 0:w], raw[:, pan.slot, 0:w], ACT.Copy), "w_hi")

        def split_to(p):
            while done[0] < min(p, NPAN):
                split(Pan(done[0]))
                done[0] += 1

        NORM_AFTER = {"wout0": 4, "wout1": 6}

        def squares(n):
            for i in range(3 if n in NORM_AFTER.values() else 0, 4):
                square(n, i)

        def square(n, i):
            w = wk if n == 0 else wk2
            if n == 0:
                act.wait_ge(S(f"x_moved{i}"), 16)
            else:
                act.wait_ge(S("x_ready"), 4 * (n - 1) + i + 1)
            if i == 0:
                if n == 1:
                    act.wait_ge(S("branch"), 4)
                    act.wait_ge(S("pe_panel"), PAN["out3"] + 1)
                if n == 2:
                    act.wait_ge(S("xl"), 12)
                if n >= 3:
                    act.wait_ge(S("stat"), n)
                if n == 4:
                    act.wait_ge(S("pool_d"), 4)
                if n == 6:
                    act.wait_ge(S("ws_t"), QH)
            signal(fn(w[:, 2 * i:2 * i + 2, :], x[:, 2 * i:2 * i + 2, :], ACT.Square), "sq")

        def root(n):
            act.wait_ge(S("stat"), n + 1)
            if n == 0:
                act.wait_ge(S("ld_cst"), 16)
            if n == 1:
                act.wait_ge(S("sg_norm"), 1)
            own(ln(rstd[:], M[1][:, 0, :], bias=eps(EPS6), scale=1.0 / D))
            signal(fn(rstd[:], rstd[:], ACT.Exp, scale=-0.5), "rs")

        def high(n):
            a, b, pan, _ = NORMS[n]
            reach(act, "pe_panel", pan)
            if b:
                act.wait_ge(S("xl"), b)
            for i in range(4):
                act.wait_ge(S("nrm"), a + i + 1)
                signal(fn(xh[:, 2 * i:2 * i + 2, :], (wk if n == 0 else wk2)[:, 2 * i:2 * i + 2, :], ACT.Copy), "xh")

        def norm(n):
            squares(n)
            root(n)
            if n == 0:
                split_to(1)
            high(n)

        def parts(n):
            _, b, pan, (gain, g0) = NORMS[n]
            act.wait_ge(S("pe_panel"), pan)
            act.wait_ge(S("xl"), b)
            for i in range(4):
                act.wait_ge(S("x_ready"), 4 * (n - 1) + i + 1)
                for k in (2 * i, 2 * i + 1):
                    ins = fn(xh[:, k, :], x[:, k, :], ACT.Copy, scale=pcol(gain, g0 + k))
                signal(ins, "xh")
            squares(n)

        def high_m(k, src):
            if k == 1:
                act.wait_ge(S("branch"), 4)
            act.wait_ge(S("pe_panel"), (0, PAN["out3"] + 1, PAN["mkv0"] + 2)[k])
            signal(fn(mh[:], src[:], ACT.Copy), "mh")

        def parts5b():
            act.wait_ge(S("pe_panel"), PAN["mkv1"] + 2)
            for k in range(KT):
                ins = fn(mh[:, k, :], x[:, k, :], ACT.Copy, scale=pcol("mix2_g", 8 + k))
            signal(ins, "mh")

        def panel(p):
            split_to(p + 3)
            name, i = WHAT[p]
            if name in ("wout0", "wout1") and i:
                square(NORM_AFTER[name], i - 1)
            if name in RES + OUTS + SCALED:
                return
            bank = G[gbank[p]]
            act.wait_ge(S("pe_panel"), p + 1)
            src = bank[:, :, :]
            if name[:4] == "gate":
                tables("exp_and_others")
                if name == "gate0" and i == 0:
                    act.wait_ge(S("sg_gelu"), 1)
                if name == "gate0" and i >= 2:
                    act.wait_ge(S("sg_y"), 1)
                if name == "gate1":
                    act.wait_ge(S("g_dve"), i + 1)
                elif name != "gate0":
                    act.wait_ge(S("merged"), 4 * (int(name[4]) - 2) + i + 1)
                for u in range(2):
                    col = 8 * int(name[4]) + 2 * i + u
                    ins = fn(sig[:, 2 * i + u, :], bank[:, u, :], ACT.Tanh, bias=half[:, col:col + 1], scale=0.5)
                signal(ins, "g_act")
                return
            if name == "rw":
                if i == 0:
                    act.wait_ge(S("zeros"), 1)
                dst = z_rw[:, 2 * i:2 * i + 2, 1:T + 1]
            elif name == "sc":
                dst = z_sc[:, 2 * i:2 * i + 2, :]
            elif name == "sg":
                dst = z_sg[:, 2 * i:2 * i + 2, :]
            elif name == "sb":
                dst = z_sb[:, 2 * i:2 * i + 2, :]
            else:
                dst = (mk, mv)[i][:, :, :]
            signal(fn(dst, src, ACT.Copy), "g_act")

        def rw_low():
            act.wait_ge(S("rw_shift"), 4)
            tables("exp_and_others")
            fn(e2[:, 0, :], zs[:, 6, :], ACT.Tanh)
            signal(fn(e2[:, 1, :], zs[:, 7, :], ACT.Tanh, scale=0.5), "rw_e")

        def rw_gates():
            act.wait_ge(S("rw_low"), 1)
            act.wait_ge(S("half"), 1)
            tables("exp_and_others")
            for j in range(2):
                fn(ew[:, j, :], DB[0][:, j, :], ACT.Tanh, bias=half[:, 32 + j:33 + j], scale=0.5)
            for j in range(2):
                fn(ew[:, 2 + j, :], DB[1][:, j, :], ACT.Tanh, bias=half[:, 34 + j:35 + j], scale=0.5)
            signal(fn(gg[:], DB[2][:, :, :], ACT.Copy), "rw_low_read")

        def rw_cum():
            act.wait_ge(S("rw_cum"), 1)
            fn(em[:], cum[:], ACT.Exp, scale=-DECAY)
            fn(ei[:], cum[:, :, 1:P + 1], ACT.Exp, scale=DECAY)
            signal(fn(esc[:], esc[:], ACT.Exp, scale=-DECAY), "rw_dec")

        def rw_key():
            act.wait_ge(S("rw_kmax"), 1)
            own(ln(e2[:], bon[:], scale=2.0 ** 20))
            signal(fn(e2[:], e2[:], ACT.Exp, bias=eps(KKB), scale=-0.5), "rw_krs")

        def rw_turn():
            act.wait_ge(S("rw_turned"), 1)
            act.wait_ge(S("rw_e2"), 1)
            fn(vn[:], DB[0][:, :, :], ACT.Copy)
            signal(fn(bkn[:].rearrange("p a b -> p (a b)"), flat(DB[1]), ACT.Copy), "rw_nat")

        def inv_first():
            act.wait_ge(S("inv_t0"), 1)
            for g in range(2):
                ins = fn(mx[:, 4 * g:4 * g + 4, :].rearrange("p a b -> p (a b)"), flat(M[g]), ACT.Copy)
            signal(ins, "inv_x0")

        def inv_t(l):
            act.wait_ge(S("inv_T"), l)
            for g in range(2):
                ins = fn(mt1[:, 4 * g:4 * g + 4, :].rearrange("p a b -> p (a b)"), flat(M[g]), ACT.Copy)
            signal(ins, "inv_c")

        def rw_rhs(ch):
            act.wait_ge(S("rw_rhs"), ch + 1)
            for half in range(2):
                signal(fn(b0[:, ch, half::2, :], M[half][:, 0, 0:P].rearrange("p (j v) -> p j v", j=2), ACT.Copy),
                       "rw_b0")

        def rw_sol(ch):
            act.wait_ge(S("rw_sol"), ch + 1)
            signal(fn(uu[:, ch, :, :].rearrange("p h v -> p (h v)"), M[0][:, 0, :], ACT.Copy), "rw_uu")

        def rw_out():
            act.wait_ge(S("rw_yp"), 1)
            signal(fn(y[:], DB[2][:, :, :], ACT.Copy), "rw_y")

        def rw_gn1():
            act.wait_ge(S("rw_yc"), 1)
            signal(fn(ysq[:], y[:], ACT.Square), "rw_ysq")

        def rw_gn2():
            act.wait_ge(S("rw_var"), 1)
            own(ln(yr[:], DB[3][:, :, :], bias=eps(EPSG), scale=1.0 / 64))
            signal(fn(yr[:], yr[:], ACT.Exp, scale=-0.5), "rw_rs")
            act.wait_ge(S("rw_fin"), 1)
            act.wait_ge(S("pe_panel"), PAN["out1"] + 1)
            signal(fn(hh1[:, 1, :, :], y[:], ACT.Copy), "branch_h")

        def sc():
            act.wait_ge(S("sc_y"), 1)
            signal(fn(hh1[:, 0, :, :], ycv[:], ACT.Copy), "branch_h")

        def sg_gelu():
            projected(act, "sg", 1)
            signal(fn(sgt[:], z_sg[:], ACT.Square), "sg_z2")
            act.wait_ge(S("sg_z3"), 1)
            tables("exp_and_others")
            signal(fn(sgt[:], sgt[:], ACT.Tanh, scale=math.sqrt(2.0 / math.pi)), "sg_e")

        def sg_mean():
            act.wait_ge(S("sg_c"), 1)
            signal(fn(sgn[:], sgv[:], ACT.Square), "sg_sq")

        def sg_var():
            act.wait_ge(S("sg_v"), 1)
            act.wait_ge(S("nrm"), 4)
            own(ln(rstd[:], DB[3][:, 0, :], bias=eps(EPS5), scale=1.0 / BW))
            signal(fn(rstd[:], rstd[:], ACT.Exp, scale=-0.5), "sg_rs")

        def sg_turn():
            act.wait_ge(S("sg_turned"), 1)
            signal(fn(sgn[:], DB[3][:, :, :], ACT.Copy), "sg_vn")

        def sg_mix():
            act.wait_ge(S("sg_y"), 1)
            signal(fn(hh1[:, 1, :, :], z_sg[:, 0:2, :], ACT.Copy), "branch_h")

        def sb_turn():
            act.wait_ge(S("sb_turned"), 1)
            act.wait_ge(S("rw_kt"), 1)
            signal(fn(sbv[:], DB[1][:, :, :], ACT.Copy), "sb_vn")

        def sb_e(h):
            act.wait_ge(S("sb_zp"), h + 1)
            if h == 0:
                act.wait_ge(S("sg_mixed"), 1)
            else:
                act.wait_ge(S("sb_att"), h)
            signal(fn(z3[:], flat(DB[0])[:, 0:3 * P], ACT.Copy, scale=0.125), "sb_zs")
            act.wait_ge(S("sb_abs"), h + 1)
            own(fn(l3[:], l3[:], ACT.Exp))
            signal(ln(l3[:], l3[:], bias=eps(ONE)), "sb_ln")

        def sb_a(h):
            act.wait_ge(S("sb_arg"), h + 1)
            signal(fn(z3[:], z3[:], ACT.Exp), "sb_exp")

        def sb_o(h):
            j, o = h // 2, 64 * (h % 2)
            act.wait_ge(S("sb_op"), h + 1)
            ins = fn(z_sb[o:o + 64, j, :], flat(DB[0])[o:o + 64, 0:T], ACT.Copy)
            signal(ins, "sb_out")
            if h == 3:
                act.wait_ge(S("sb_out"), 4)
                act.wait_ge(S("pe_panel"), PAN["out0"] + 1)
                signal(fn(hh1[:, 0, :, :], z_sb[:, 0:2, :], ACT.Copy), "branch_h")

        def merge_split():
            act.wait_ge(S("pe_panel"), PAN["gate3"] + 4)
            for i in range(4):
                act.wait_ge(S("merged"), 8 + i + 1)
                signal(fn(xh[:, 2 * i:2 * i + 2, :], merged[:, 2 * i:2 * i + 2, :], ACT.Copy, scale=0.5),
                       "xh")

        def ffn(f):
            ni, nu, p0, _ = FF[f]

            def high_hid(j, u, js):
                act.wait_ge(S("prod"), 2 * j + u + 1)
                if u == 0 and js >= 2:
                    act.wait_ge(S("pe_panel"), p0 + 2 * nu + (j - 3) * (nu + 1) + 1)
                signal(fn(hh[:, js % 3, u, :], hid[:, js % 3, u, :], ACT.Copy), f"hid_h{f}")

            def up(j, pans, js):
                for u, pan in enumerate(pans):
                    more(pan, 2)
                    act.wait_ge(S("pe_panel"), pan.p + 1)
                    if nu == 2:
                        if js == 0 and u == 0:
                            act.wait_ge(S("zeros2"), 1)
                        if js >= 1:
                            act.wait_ge(S("prod"), 2 * j + u - 1)
                        fn(upad[:, u, :, 2:T + 2], G[u][:, :, :], ACT.Copy)
                        for s_ in range(2):
                            w2 = par[:, bass.ds(2 * j + (PC["conv"] + 2 * 2 * FT1 + s_ * FT1 + u), 1)]
                            ins = fn(cv[:, u, s_, :], G[u][:, s_, :], ACT.Copy, scale=w2)
                        signal(ins, f"up_read{f}")
                        if u:
                            high_hid(j, 0, js)
                        act.wait_ge(S("conv"), 2 * j + u + 1)
                        signal(fn(sgm[:, u, :], cv[:, u, 0, :], ACT.Tanh, scale=0.5), "silu_e")
                    else:
                        if js == 0:
                            root(2 * f + 2)
                        act.wait_ge(S(f"up_read{f}"), j + 1)
                        if js >= 2:
                            act.wait_ge(S(f"hid{f}"), j - 1)
                        fn(hid[:, js % 3, :, :], rel[:, js % 3, :, :], ACT.Square)
                        if js >= 2:
                            act.wait_ge(S("pe_panel"), p0 + 2 * nu + (j - 3) * (nu + 1) + 1)
                        signal(fn(hh[:, js % 3, :, :], rel[:, js % 3, :, :], ACT.Square), f"hid_h{f}")
                if nu == 2 and js == 0:
                    high_hid(0, 1, 0)

            def down(i, pan, js, last):
                tail = isinstance(i, int) and i == ni - 2
                if not tail:
                    more(pan, 2)
                if nu == 2 and not last:
                    high_hid(i + 1, 1, js + 1)
                if tail:
                    more(pan, 2)

            def more(pan, ahead):
                q = Pan(pan.p0 + ahead)
                if isinstance(pan.p, int):
                    split_to(pan.p + ahead + 1)
                else:
                    q.p = pan.p + ahead
                    q.turn = pan.turn + (pan.p0 + ahead) // SLOTS - pan.p0 // SLOTS
                    split(q)

            if nu == 2:
                tables("exp_and_others")
            ffn_walk(act, f, up, down, done)
            tables("natural_log_exp_and_others")

        def mem_load():
            act.wait_ge(S("branch"), 4)
            act.wait_ge(S("pe_panel"), PAN["out3"] + 1)
            act.dma_start(mem[:], A["mem"]).then_inc(S("ld_sgw_mem"), 16)
            act.dma_start(poolw[:], A["pool_w"]).then_inc(S("ld_lora_pool"), 16)

        def mem_squares():
            act.wait_ge(S("ld_sgw_mem"), 32)
            for i in range(4):
                signal(fn(mwk[:, 2 * i:2 * i + 2, :], mem[:, 2 * i:2 * i + 2, :], ACT.Square), "mem_sq")

        def mem_stat():
            act.wait_ge(S("mem_st"), 1)
            own(ln(mrstd[:], M[1][:, 0, :], bias=eps(EPS6), scale=1.0 / D))
            signal(fn(mrstd[:], mrstd[:], ACT.Exp, scale=-0.5), "mem_rs")

        def mem_norm(l):
            act.wait_ge(S("mem_n"), l + 1)
            high_m(l + 1, mwk)

        def hn(i):
            src, _, _, need = HEADS[i]
            projected(act, *need)
            if i:
                act.wait_ge(S("hn_ss"), i)
            signal(fn(hsq[:], src if i > 4 else src[:], ACT.Square), "hn_sq")
            act.wait_ge(S("hn_ss"), i + 1)
            if i:
                act.wait_ge(S("hn"), i)
            own(ln(hy[:], M[1][:, :, :], bias=eps(EPS6), scale=1.0 / 64))
            signal(fn(hy[:], hy[:], ACT.Exp, scale=-0.5), "hn_y")

        def turn_mv(l):
            act.wait_ge(S("mv_t"), l + 1)
            signal(fn(mvn[:], M[0][:, :, :], ACT.Copy), "mvn")

        def turn_v():
            act.wait_ge(S("vs_t"), 1)
            signal(fn(vsn[:], M[0][:, :, :], ACT.Copy), "vsn")

        def score_m(l):
            for h in range(4):
                act.wait_ge(S("sm_max"), 4 * l + h + 1)
                if h == 0:
                    act.wait_ge(S("ml"), 2)
                for tt in range(2):
                    a = 2 * h + tt
                    signal(fn((pm0, pm1)[l][:, a, :], DB[h][:, tt, :], ACT.Exp, bias=hmax[:, 1, a:a + 1],
                              accum_out=hmax[:, 2, a:a + 1]), "sm_exp")

        def turn_p(l):
            for h in range(4):
                act.wait_ge(S("sm_t"), 4 * l + h + 1)
                signal(fn((ptm0, ptm1)[l][:, h, :, :], DB[h][:, :, :], ACT.Copy), "sm_pt")

        def pv_m(l):
            act.wait_ge(S("pvm"), l + 1)
            act.wait_ge(S("pe_panel"), (PAN["in0m"] + 4, PAN["kv"] + 2)[l])
            signal(fn(xh[:, 6:8, :], M[0][:, :, :], ACT.Copy), "xh")

        def pool_mm():
            act.wait_ge(S("pe_panel"), PAN["in0m"] + 4)
            for n, i in enumerate((2, 1, 0)):
                act.wait_ge(S("pool_p"), n + 1)
                for u in range(2):
                    ins = fn(xh[:, 2 * i + u, :], DB[i][:, u, :], ACT.Copy, scale=pcol("pool_s", 2 * i + u))
                signal(ins, "xh")

        def exp_s(g):
            act.wait_ge(S("ws_max"), g + 1)
            own(fn(wmax[:, 0, 8 * g:8 * g + 8], wmax[:, 0, 8 * g:8 * g + 8], ACT.Exp))
            for h in range(4 * g, 4 * g + 4):
                for b, (lo, hi) in enumerate(((0, P), (P, 3 * P))):
                    a = 2 * h + b
                    ins = fn(ss[:, h, lo:hi], ss[:, h, lo:hi], ACT.Exp, bias=wmax[:, 1, a:a + 1],
                             accum_out=wmax[:, 2, a:a + 1])
            signal(ins, "ws_exp")

        def pv_s(j):
            for h in (2 * j, 2 * j + 1):
                act.wait_ge(S("ws_t"), h + 1)
                if h >= 8:
                    act.wait_ge(S("ws_o"), (h - 8) // 2 + 1)
                if h == 0:
                    act.wait_ge(S("pvm"), 2)
                signal(fn(pt[:, h % 8, :], flat(DB[h % 2])[:, 0:3 * P], ACT.Copy), "ws_pt")
            if j % 2:
                act.wait_ge(S("ws_o"), j + 1)
                act.wait_ge(S("pe_panel"), PAN["kv"] + 2)
                signal(fn(xh[:, j - 1:j + 1, :], (DB[2], DB[3], M[1])[j // 2][:, :, :], ACT.Copy), "xh")

        walk(act, {"norm": norm, "squares": squares, "root": root, "parts": parts, "parts5b": parts5b, "panel": panel,
                   "rw_low": rw_low, "rw_gates": rw_gates, "rw_cum": rw_cum, "rw_key": rw_key,
                   "rw_turn": rw_turn, "inv_first": inv_first, "inv_t": inv_t, "rw_rhs": rw_rhs,
                   "rw_sol": rw_sol, "rw_out": rw_out, "rw_gn1": rw_gn1, "rw_gn2": rw_gn2, "sc": sc,
                   "sg_gelu": sg_gelu, "sg_mean": sg_mean, "sg_var": sg_var, "sg_turn": sg_turn,
                   "sg_mix": sg_mix, "sb_turn": sb_turn, "sb_e": sb_e, "sb_a": sb_a, "sb_o": sb_o,
                   "merge_split": merge_split, "ffn": ffn, "mem_load": mem_load, "mem_squares": mem_squares,
                   "mem_stat": mem_stat,
                   "mem_norm": mem_norm, "hn": hn, "turn_mv": turn_mv, "turn_v": turn_v, "score_m": score_m, "turn_p": turn_p,
                   "pv_m": pv_m, "pool_mm": pool_mm, "exp_s": exp_s, "pv_s": pv_s})

    @block.vector
    def _(dve):
        tt, ts, stt = nc.vector.tensor_tensor, nc.vector.tensor_scalar, nc.vector.scalar_tensor_tensor
        own = Own(dve, "dve_own")
        MUL, ADD, SUB, MAX, MIN = ALU.mult, ALU.add, ALU.subtract, ALU.max, ALU.min
        done = [0]

        def signal(ins, name):
            ins.then_inc(S(name), 1)

        def f32(ap):
            return ap.bitcast(F32)

        def split(pan):
            w = PT * (PGW if isinstance(pan.p, int) and NARROW <= pan.p < NARROW + 4 else P)
            dve.wait_ge(S("w_hi"), pan.p + 1)
            signal(tt(wlo[:, pan.slot, 0:w], raw[:, pan.slot, 0:w], f32(whi[:, pan.slot, 0:w]), SUB), "w_lo")

        def split_to(p):
            while done[0] < min(p, NPAN):
                split(Pan(done[0]))
                done[0] += 1

        def newton(y, a, n, bias, tmp, read=None):
            own(tt(tmp, y, y, MUL))
            ins = stt(tmp, a, n * bias, tmp, ADD, MUL)
            if read is None:
                own(ins)
            else:
                signal(ins, read[0])
                dve.wait_ge(S(read[0]), read[1])
            own(ts(tmp, tmp, -0.5 / n, 1.5, MUL, ADD))
            own(tt(y, y, tmp, MUL))

        def low(k, i, src):
            dve.wait_ge(S("xh"), k)
            signal(tt(xl[:, 2 * i:2 * i + 2, :], src, f32(xh[:, 2 * i:2 * i + 2, :]), SUB), "xl")

        def low_b(k, slot, src):
            dve.wait_ge(S("branch_h"), k)
            signal(tt(hl1[:, slot, :, :], src, f32(hh1[:, slot, :, :]), SUB), "branch")

        def scaled(dst, src, scale, gain, i, name, g0):
            stt(dst[:, 2 * i, :], src[:, 2 * i, :], pcol(gain, g0 + 2 * i), scale[:], MUL, MUL)
            signal(stt(dst[:, 2 * i + 1, :], src[:, 2 * i + 1, :], pcol(gain, g0 + 2 * i + 1), scale[:], MUL, MUL), name)

        def root(n):
            dve.wait_ge(S("rs"), n + 1)
            newton(rstd[:], M[1][:, 0, :], D, 1e-6, rtmp[:], ("rs_read", n + 1))

        def norm(n):
            if n == 0:
                for i in range(1, 4):
                    dve.wait_ge(S("sq"), i + 1)
                    own(tt(wk[:, 0:2, :], wk[:, 0:2, :], wk[:, 2 * i:2 * i + 2, :], ADD))
                signal(tt(wk[:, 0, :], wk[:, 0, :], wk[:, 1, :], ADD), "sq_sum0")
            root(n)
            a, b, _, (gain, g0) = NORMS[n]
            w = wk if n == 0 else wk2
            for i in range(4):
                scaled(w, x, rstd, gain, i, "nrm", g0)
                if n == 0 and i == 0:
                    split_to(1)
                low(b + i + 1, i, w[:, 2 * i:2 * i + 2, :])
            if n == 1:
                dve.wait_ge(S("pe_panel"), PAN["out3"] + 1)
                signal(nc.vector.memset(upad[:, :, :, 0:2], 0.0), "zeros2")

        def final_norm():
            for i in range(4):
                scaled(x, x, rstd, "fin_g", i, "x_ready", 0)
            nc.vector.memset(zp[:, :, 0:16], 0.0)

        def parts(n):
            _, b, _, (gain, g0) = NORMS[n]
            for i in range(4):
                dve.wait_ge(S("x_ready"), 4 * (n - 1) + i + 1)
                dve.wait_ge(S("xh"), b + i + 1)
                for k in (2 * i, 2 * i + 1):
                    ins = stt(xl[:, k, :], x[:, k, :], pcol(gain, g0 + k), f32(xh[:, k, :]), MUL, SUB)
                signal(ins, "xl")

        def parts5b():
            dve.wait_ge(S("mh"), 3)
            for k in range(KT):
                ins = stt(ml[:, k, :], x[:, k, :], pcol("mix2_g", 8 + k), f32(mh[:, k, :]), MUL, SUB)
            signal(ins, "ml")

        def panel(p):
            name, i = WHAT[p]
            if name not in OUTS:
                split_to(p + 3)
            if name in RES:
                dve.wait_ge(S("pe_panel"), p + 1)
                signal(tt(x[:, 2 * i:2 * i + 2, :], x[:, 2 * i:2 * i + 2, :], DB[i][:, :, :], ADD), "x_ready")
            elif name in OUTS:
                b = int(name[3])
                for i in range(4):
                    if i < 3:
                        dve.wait_ge(S("out_pair"), 3 * b + i + 1)
                    else:
                        dve.wait_ge(S("pe_panel"), p + 1)
                    prs = slice(2 * i, 2 * i + 2)
                    out = merged if b == 0 else sig
                    projected(dve, f"gate{b}", i)
                    signal(stt(out[:, prs, :], sig[:, prs, :], 1.0, G[i % 2 if OUT_EVEN[b] else 1 - i % 2][:, :, :],
                               ADD, MUL), "g_dve")
                    for k in ([i - 1] if i < 3 else [2, 3]) if b else []:
                        if k >= 0:
                            dve.wait_ge(S("g_dve"), 4 * b + k + 1)
                            prs = slice(2 * k, 2 * k + 2)
                            signal(tt(merged[:, prs, :], merged[:, prs, :], sig[:, prs, :], ADD), "merged")
                if b < 3:
                    split_to(p + 3)
            elif name in SCALED and name != "in0q":
                read(p)
            elif name == "rw":
                projected(dve, name, i)
                prs = slice(2 * i, 2 * i + 2)
                own(tt(zs[:, prs, :], z_rw[:, prs, 0:T], z_rw[:, prs, 1:T + 1], SUB))
                stt(zs[:, 2 * i, :], zs[:, 2 * i, :], pcol("mu", 2 * i), z_rw[:, 2 * i, 1:T + 1], MUL, ADD)
                signal(stt(zs[:, 2 * i + 1, :], zs[:, 2 * i + 1, :], pcol("mu", 2 * i + 1),
                           z_rw[:, 2 * i + 1, 1:T + 1], MUL, ADD), "rw_shift")

        def read(p):
            name, i = WHAT[p]
            dve.wait_ge(S("pe_panel"), p + 1)
            rows = slice(0, PGW if name == "in0m" else P)
            if name == "in0q" or (name == "in1" and i == 0):
                dst = mq[:, :, :]
            elif name == "in0m":
                dst = zp[:, 6 - 2 * i:8 - 2 * i, 16:16 + T]
            elif name == "kv":
                dst = (ks, vs)[i][:, :, :]
            else:
                dst = qs[:, 2 * i - 2:2 * i, :]
            signal(tt(dst, G[gbank[p]][rows, :, :], rstd[rows, :].unsqueeze(1).broadcast_to([rows.stop, 2, T]), MUL),
                   "g_scaled")

        use, OUT_EVEN = 0, {}
        for step in W:
            if step[0] == "panel":
                nm = WHAT[step[1]][0]
                if nm in OUTS:
                    OUT_EVEN[int(nm[3])] = use % 2 == 0
                    use += 4
                elif nm not in RES:
                    use += 1

        def rw_low():
            dve.wait_ge(S("rw_e"), 1)
            signal(ts(e2[:, 1, :], e2[:, 1, :], 0.5, 0.5, MUL, ADD), "rw_e2")

        def rw_gates():
            dve.wait_ge(S("rw_low_read"), 1)
            own(ts(ew[:], ew[:], 0.5, 0.5, MUL, ADD))

        def rw_cum():
            for jc in range(4):
                j, ch = divmod(jc, 2)
                ins = nc.vector.tensor_tensor_scan(cum[:, jc, 1:P + 1], c("ones"), ew[:, j, ch * P:(ch + 1) * P],
                                                   0.0, MUL, ADD)
            own(ins)
            own(nc.vector.tensor_copy(mid[:], cum[:, :, 64:65]))
            own(tt(cum[:], cum[:], mid[:].broadcast_to([P, 4, P + 1]), SUB))
            signal(tt(esc[:], cum[:, 0:4:2, P:P + 1].rearrange("p a b -> p (a b)"),
                      mid[:, 1:4:2, :].rearrange("p a b -> p (a b)"), ADD), "rw_cum")

        def rw_key():
            for j in range(2):
                ins = ts(kk[:, j, :], zs[:, 2 + j, :], pcol("k_k", j), None, MUL)
            own(ins)
            signal(tt(bon[:], kk[:], kk[:], MUL), "rw_ksq")
            for j in range(2):
                ins = ts(kp[:, j, :], ew[:, 2 + j, :], 1.0, pcol("k_a", j), SUB, MUL)
            own(ins)
            own(stt(kp[:], kp[:], 1.0, zs[:, 2:4, :], ADD, MUL))
            dve.wait_ge(S("rw_kss"), 1)
            signal(ts(bon[:], DB[3][:, :, :], 1e-24, None, MAX), "rw_kmax")
            dve.wait_ge(S("rw_krs"), 1)
            newton(e2[:], bon[:], 1, 0.0, vn[:])
            own(stt(kk[:], kk[:], -1.0, e2[:], MUL, MUL))
            own(stt(ew[:, 2:4, :], kk[:], -1.0, ew[:, 2:4, :], MUL, MUL))

        def rw_mix():
            dve.wait_ge(S("rw_dec"), 1)
            tt(ar[:, :, 0, :], four(kk), em[:, :, 0:P], MUL)
            tt(ar[:, :, 1, :], four(zs[:, 0:2, :]), em[:, :, 1:P + 1], MUL)
            tt(bt[:], four(ew[:, 2:4, :]), ei[:], MUL)
            tt(kt[:], four(kp), ei[:], MUL)
            for j in range(2):
                ins = stt(bon[:, j, :], zs[:, j, :], pcol("r_k", j), kp[:, j, :], MUL, MUL)
            signal(ins, "rw_kt")

        def rw_turn():
            dve.wait_ge(S("rw_turned"), 1)
            signal(tt(bon[:], DB[2][:, :, :], zs[:, 4:6, :], MUL), "rw_bonus")

        def rw_prod(i):
            mask = cst[:, CC["strict"]:CC["strict"] + 2 * P].unsqueeze(1).broadcast_to([P, 2, 2 * P])
            for m in (2 * i, 2 * i + 1):
                dve.wait_ge(S("rw_gp"), m + 1)
                if m == 0:
                    dve.wait_ge(S("branch"), 2)
                signal(tt(gm[:, m, :, :].rearrange("p (a b) t -> p a (b t)", a=2), M[m % 2][:, :, :], mask, MUL), "rw_prod")

        def inv_first():
            dve.wait_ge(S("inv_n"), 1)
            signal(tt(mxt[:], mnt[:], c("ident").unsqueeze(1).broadcast_to([P, 8, P]), ADD), "inv_x")

        def inv_x(l):
            dve.wait_ge(S("inv_p"), l)
            for g in range(2):
                dst = mxt[:, 4 * g:4 * g + 4, :].rearrange("p a b -> p (a b)")
                ins = tt(dst, dst, flat(DB[2 + g]), ADD)
            if l < len(LEVELS) - 1:
                for g in range(2):
                    dst = mx[:, 4 * g:4 * g + 4, :].rearrange("p a b -> p (a b)")
                    ins = tt(dst, dst, flat(M[g]), ADD)
            signal(ins, "inv_x")

        def rw_state():
            dve.wait_ge(S("rw_sp"), 1)
            for j in range(2):
                ins = ts(st[:, j, :], M[1][:, j, 0:64], esc[:, j:j + 1], None, MUL)
            signal(ins, "rw_state")

        def rw_gn1():
            dve.wait_ge(S("rw_mean"), 1)
            signal(stt(y[:], DB[3][:, :, :], -1.0 / 64, y[:], MUL, ADD), "rw_yc")

        def rw_gn2():
            dve.wait_ge(S("rw_rs"), 1)
            newton(yr[:], DB[3][:, :, :], 64, 64e-5, ysq[:], ("rw_rs_read", 1))
            for j in range(2):
                ins = stt(y[:, j, :], y[:, j, :], pcol("gn_g", j), yr[:, j, :], MUL, MUL)
            own(ins)
            for j in range(2):
                ins = stt(y[:, j, :], y[:, j, :], pcol("gn_b", j), bon[:, j, :], ADD, ADD)
            own(ins)
            signal(tt(y[:], y[:], gg[:], MUL), "rw_fin")
            low_b(4, 1, y[:])

        def sc():
            dve.wait_ge(S("sc_y"), 1)
            low_b(1, 0, ycv[:])

        def sg_gelu():
            dve.wait_ge(S("ld_sgw_mem"), 16)
            dve.wait_ge(S("ld_masks"), 16)
            signal(tt(sgw[:], sgw[:], c("incl").unsqueeze(1).broadcast_to([P, 4, P]), MUL), "sg_tril")
            dve.wait_ge(S("sg_z2"), 1)
            own(ts(sgt[:], sgt[:], 0.044715, 1.0, MUL, ADD))
            signal(tt(sgt[:], sgt[:], z_sg[:], MUL), "sg_z3")
            dve.wait_ge(S("sg_e"), 1)
            own(ts(sgt[:], sgt[:], 0.5, 0.5, MUL, ADD))
            signal(tt(z_sg[:], z_sg[:], sgt[:], MUL), "sg_gelu")

        def sg_mean():
            dve.wait_ge(S("sg_s"), 1)
            dve.wait_ge(S("sg_gelu"), 1)
            for j in range(2):
                ins = stt(sgv[:, j, :], DB[3][:, 0, :], -1.0 / BW, z_sg[:, 2 + j, :], MUL, ADD)
            signal(ins, "sg_c")

        def sg_var():
            dve.wait_ge(S("sg_rs"), 1)
            newton(rstd[:], DB[3][:, 0, :], BW, 1e-5, rtmp[:])
            for j in range(2):
                ins = stt(sgv[:, j, :], sgv[:, j, :], pcol("ln_g", j), rstd[:], MUL, MUL)
            own(ins)
            for j in range(2):
                ins = ts(sgv[:, j, :], sgv[:, j, :], pcol("ln_b", j), None, ADD)
            signal(ins, "sg_norm")

        def sg_mix():
            dve.wait_ge(S("sg_mixed"), 1)
            signal(tt(z_sg[:, 0:2, :], z_sg[:, 0:2, :], DB[3][:, :, :], MUL), "sg_y")
            low_b(2, 1, z_sg[:, 0:2, :])

        strict = c("strict").unsqueeze(1).broadcast_to([P, 2, P])

        def diag(h):
            return h[:].rearrange("p (a t) -> p a t", a=3)[:, 0:3:2, :]

        def sb_e(h):
            dve.wait_ge(S("sb_zs"), h + 1)
            reach(dve, "sb_op", h)
            signal(stt(l3[:], z3[:], -1.0, z3[:], MUL, MIN), "sb_abs")
            dve.wait_ge(S("sb_ln"), h + 1)
            own(stt(l3[:], z3[:], 0.0, l3[:], MAX, ADD))
            signal(tt(diag(l3), diag(l3), strict, MUL), "sb_sp")

        def sb_a(h):
            dve.wait_ge(S("sb_qp"), h + 1)
            own(tt(z3[:], z3[:], flat(DB[1])[:, 0:3 * P], SUB))
            signal(ts(z3[:], z3[:], 0.0, None, MIN), "sb_arg")
            dve.wait_ge(S("sb_exp"), h + 1)
            nc.vector.tensor_copy(l3[:, P:2 * P], z3[:, P:2 * P])
            signal(tt(diag(l3), diag(z3), strict, MUL), "sb_att")

        def sb_o(h):
            if h == 3:
                low_b(3, 0, z_sb[:, 0:2, :])

        def merge_split():
            for i in range(4):
                dve.wait_ge(S("merged"), 8 + i + 1)
                dve.wait_ge(S("xh"), 4 + i + 1)
                prs = slice(2 * i, 2 * i + 2)
                signal(stt(xl[:, prs, :], merged[:, prs, :], 0.5, f32(xh[:, prs, :]), MUL, SUB), "xl")

        def ffn(f):
            ni, nu, p0, _ = FF[f]

            class Step:

                def __init__(self, item, n):
                    self.item, self.n, self.k = item, n, 0

                def __call__(self, ins):
                    ins.then_inc(S(f"ffn_own{f}"), 1)
                    self.k += 1
                    dve.wait_ge(S(f"ffn_own{f}"), self.item * self.n + self.k)

            def more(pan, ahead):
                if isinstance(pan.p, int):
                    split_to(pan.p + ahead + 1)
                else:
                    q = Pan(pan.p0 + ahead)
                    q.p = pan.p + ahead
                    split(q)

            def low_hid(j, u, js):
                dve.wait_ge(S(f"hid_h{f}"), 2 * j + u + 1)
                signal(tt(hl[:, js % 3, u, :], hid[:, js % 3, u, :], f32(hh[:, js % 3, u, :]), SUB), f"hid{f}")

            def up(j, pans, js):
                for u, pan in enumerate(pans):
                    more(pan, 2)
                    if nu == 2:
                        t = 2 * j + u
                        step = Step(t, 2)
                        dve.wait_ge(S(f"up_read{f}"), t + 1)
                        for i, sh in ((1, 1), (0, 0)):
                            for s_ in range(2):
                                w = par[:, bass.ds(2 * j + (PC["conv"] + i * 2 * FT1 + s_ * FT1 + u), 1)]
                                ins = stt(cv[:, u, s_, :], upad[:, u, s_, sh:sh + T], w, cv[:, u, s_, :], MUL, ADD)
                            if i:
                                step(ins)
                            else:
                                signal(ins, "conv")
                        if u:
                            low_hid(j, 0, js)
                        dve.wait_ge(S("silu_e"), t + 1)
                        step(stt(sgm[:, u, :], sgm[:, u, :], 1.0, cv[:, u, 0, :], ADD, MUL))
                        signal(stt(hid[:, js % 3, u, :], sgm[:, u, :], 0.5, cv[:, u, 1, :], MUL, MUL), "prod")
                    else:
                        if js == 0:
                            root(2 * f + 2)
                        dve.wait_ge(S("pe_panel"), pan.p + 1)
                        signal(stt(rel[:, js % 3, :, :], GR[js % 3][:, :, :], 0.0,
                                   rstd[:].unsqueeze(1).broadcast_to([P, 2, T]), MAX, MUL), f"up_read{f}")
                        dve.wait_ge(S(f"hid_h{f}"), j + 1)
                        signal(tt(hl[:, js % 3, :, :], hid[:, js % 3, :, :], f32(hh[:, js % 3, :, :]), SUB), f"hid{f}")
                if nu == 2 and js == 0:
                    low_hid(0, 1, 0)

            def down(i, pan, js, last):
                tail = isinstance(i, int) and i == ni - 2
                if not tail:
                    more(pan, 2)
                if nu == 2 and not last:
                    low_hid(i + 1, 1, js + 1)
                if tail:
                    more(pan, 2)

            ffn_walk(dve, f, up, down, done)
            for i in range(4):
                if i < 3:
                    dve.wait_ge(S("down_pair"), 3 * f + i + 1)
                else:
                    dve.wait_ge(S("pe_panel"), p0 + ni * (nu + 1))
                signal(tt(x[:, 2 * i:2 * i + 2, :], x[:, 2 * i:2 * i + 2, :], DB[i][:, :, :], ADD), "x_ready")

        def mem_stat():
            dve.wait_ge(S("mem_rs"), 1)
            newton(mrstd[:], M[1][:, 0, :], D, 1e-6, rtmp[:], ("mem_rs_read", 1))

        def mem_norm(l):
            if l:
                dve.wait_ge(S("ml"), 1)
            for k in range(KT):
                ins = stt(mwk[:, k, :], mem[:, k, :], pcol("mem_g", 8 * l + k), mrstd[:], MUL, MUL)
            signal(ins, "mem_n")
            dve.wait_ge(S("mh"), l + 1)
            signal(tt(ml[:], mwk[:], f32(mh[:]), SUB), "ml")

        def hn(i):
            src, gain, g0, _ = HEADS[i]
            src = src if i > 4 else src[:]
            gain = pcol(gain, g0) if gain else gq8[:, g0:g0 + 1]
            dve.wait_ge(S("hn_y"), i + 1)
            newton(hy[:], M[1][:, :, :], 64, 1e-6, ht[:], ("hn_read", i + 1))
            signal(stt(src, src, gain, hy[:], MUL, MUL), "hn")

        def swap_k():
            dve.wait_ge(S("hn"), 4)
            nc.vector.tensor_copy(ksw[0:64, :, :], ks[64:128, :, :])
            signal(nc.vector.tensor_copy(ksw[64:128, :, :], ks[0:64, :, :]), "ksw")

        def score_m(l):
            pm = (pm0, pm1)[l]
            for h in range(4):
                a = slice(2 * h, 2 * h + 2)
                dve.wait_ge(S("sm"), 4 * l + h + 1)
                own(nc.vector.tensor_reduce(hmax[:, 0, a], DB[h][:, :, :], AX_X, MAX))
                signal(ts(hmax[:, 1, a], hmax[:, 0, a], -1.0, None, MUL), "sm_max")
            for h in range(4):
                a = slice(2 * h, 2 * h + 2)
                dve.wait_ge(S("sm_exp"), 8 * l + 2 * h + 2)
                own(nc.vector.reciprocal(hmax[:, 0, a], hmax[:, 2, a]))
                for t_ in range(2):
                    b = 2 * h + t_
                    ins = ts(pm[:, b, :], pm[:, b, :], hmax[:, 0, b:b + 1], None, MUL)
                signal(ins, "sm_p")

        def pv_m(l):
            low((17, 29)[l], 3, M[0][:, :, :])

        def pool_mm():
            for n, i in enumerate((2, 1, 0)):
                dve.wait_ge(S("xh"), 17 + n + 1)
                for u in range(2):
                    k = 2 * i + u
                    ins = stt(xl[:, k, :], DB[i][:, u, :], pcol("pool_s", k), f32(xh[:, k, :]), MUL, SUB)
                signal(ins, "xl")

        def score_s(g):
            for h in range(4 * g, 4 * g + 4):
                dve.wait_ge(S("ws"), h + 1)
                if h == 0:
                    dve.wait_ge(S("sm_t"), 8)
                signal(stt(ss[:, h, :], cst[:, CC["dist"]:CC["dist"] + 3 * P], slopes[h], flat(DB[h % 4])[:, 0:3 * P],
                           MUL, ADD), "ws_read")
            dve.wait_ge(S("ws_read"), 4 * g + 4)
            hs, a = slice(4 * g, 4 * g + 4), slice(8 * g, 8 * g + 8)
            top_ = wmax[:, 0, a].rearrange("p (h b) -> p h b", b=2)
            neg_ = wmax[:, 1, a].rearrange("p (h b) -> p h b", b=2)
            sink = par[:, PC["sinks"] + 4 * g:PC["sinks"] + 4 * g + 4].unsqueeze(2).broadcast_to([P, 4, 2])
            nc.vector.tensor_reduce(top_[:, :, 0:1], ss[:, hs, 0:P], AX_X, MAX)
            own(nc.vector.tensor_reduce(top_[:, :, 1:2], ss[:, hs, P:3 * P], AX_X, MAX))
            own(tt(top_, top_, sink, MAX))
            own(ts(neg_, top_, -1.0, None, MUL))
            signal(tt(top_, neg_, sink, ADD), "ws_max")

        def soft_s(g):
            a = slice(8 * g, 8 * g + 8)
            dve.wait_ge(S("ws_exp"), g + 1)
            own(tt(wmax[:, 2, a], wmax[:, 2, a], wmax[:, 0, a], ADD))
            own(nc.vector.reciprocal(wmax[:, 2, a], wmax[:, 2, a]))
            for h in range(4 * g, 4 * g + 4):
                for b, (lo, hi) in enumerate(((0, P), (P, 3 * P))):
                    ins = ts(ss[:, h, lo:hi], ss[:, h, lo:hi], wmax[:, 2, 2 * h + b:2 * h + b + 1], None, MUL)
                signal(ins, "ws_p")

        def pv_s(j):
            if j % 2:
                low(29 + j // 2 + 1, j // 2, (DB[2], DB[3], M[1])[j // 2][:, :, :])

        signal(nc.vector.memset(z_rw[:, :, 0:1], 0.0), "zeros")
        nc.vector.memset(cum[:, :, 0:1], 0.0)
        dve.wait_ge(S("ld_par"), 16)
        ts(half[:, 0:32], par[:, PC["gate_b"]:PC["gate_b"] + 32], 0.5, None, MUL)
        ts(gq8[:, 0:2], par[:, PC["mq_g"]:PC["mq_g"] + 2], 0.125, None, MUL)
        ts(gq8[:, 2:3], par[:, PC["q_g"]:PC["q_g"] + 1], 0.125, None, MUL)
        signal(ts(half[:, 32:36], par[:, PC["w0"]:PC["w0"] + 4], 0.5, None, MUL), "half")
        dve.wait_ge(S("ld_cst"), 16)
        walk(dve, {"read": read, "norm": norm, "root": root, "final_norm": final_norm, "parts": parts, "parts5b": parts5b,
                   "panel": panel, "rw_low": rw_low, "rw_gates": rw_gates, "rw_cum": rw_cum, "rw_key": rw_key,
                   "rw_mix": rw_mix, "rw_turn": rw_turn, "rw_prod": rw_prod, "inv_first": inv_first,
                   "inv_x": inv_x, "rw_state": rw_state, "rw_gn1": rw_gn1, "rw_gn2": rw_gn2, "sc": sc,
                   "sg_gelu": sg_gelu, "sg_mean": sg_mean, "sg_var": sg_var, "sg_mix": sg_mix, "sb_e": sb_e,
                   "sb_a": sb_a, "sb_o": sb_o, "merge_split": merge_split, "ffn": ffn, "mem_stat": mem_stat,
                   "mem_norm": mem_norm, "hn": hn, "swap_k": swap_k, "score_m": score_m, "pv_m": pv_m,
                   "pool_mm": pool_mm, "score_s": score_s, "soft_s": soft_s, "pv_s": pv_s})

    ctx.close()


def kernel(**a):
    import concourse.bacc as bacc
    from concourse.bass_utils import run_bass_kernel_spmd

    a = {k: np.asarray(v) for k, v in a.items()}

    def tiles(w, order=None, width=P):
        k, n = w.shape
        t = w.reshape(k // P, P, n // width, width).transpose(2, 0, 1, 3)
        if order is not None:
            t = t[order]
        return t.reshape(-1, P, width)

    def panels(t):
        n, _, w = t.shape
        return t.reshape(n // PT, PT, P, w).transpose(0, 2, 1, 3).reshape(n // PT, P, PT * w)

    def pairs(w):
        k, n = w.shape
        t = w.reshape(k // (2 * P), 2, P, n // P, P).transpose(0, 3, 1, 2, 4)
        return panels(t.reshape(-1, P, P))

    def interleave(up, down, nu):
        n = down.shape[0]
        up = up.reshape(n, nu, *up.shape[1:])
        parts = [up[0]]
        for i in range(n - 1):
            parts += [up[i + 1], down[i:i + 1]]
        return np.concatenate(parts + [down[n - 1:]])

    w_in = a["w_in"][0]
    sc_o, sb_o, rw_o, sg_o, gate_o = 0, 3 * BW, 6 * BW, 6 * BW + D, 8 * BW + D
    branch = (0, 3, 1, 2)
    outs = ("sc_out", "sg_out", "sb_out", "rw_out")
    gates = [w_in[:, gate_o + b * D:gate_o + (b + 1) * D] for b in branch]
    parts = [tiles(w_in[:, rw_o:rw_o + D]), tiles(w_in[:, sc_o:sc_o + 3 * BW]), tiles(w_in[:, sg_o:sg_o + 2 * BW]),
             tiles(w_in[:, sb_o:sb_o + 3 * BW])]
    parts = [panels(p) for p in parts]
    for g, o in zip(gates, outs):
        parts += [panels(tiles(g)), pairs(a[o][0])]
    parts.append(panels(tiles(a["w_o"][0])))
    order = [t + s * FT1 for t in range(FT1) for s in range(2)]
    parts.append(interleave(panels(tiles(a["w_up"][0], order)), pairs(a["w_down"][0]), 2))
    win2, main = a["w_in_2"], 2 * PG * PGW
    parts += [panels(tiles(a["w_mem_kv_2"][0])), panels(tiles(win2[0][:, main:])), panels(tiles(a["w_out_2"][0])),
              interleave(panels(tiles(a["w_up_2"][0])), pairs(a["w_down_2"][0]), 1),
              panels(tiles(a["w_mem_kv_2"][1])), panels(tiles(a["w_kv_2"])), panels(tiles(win2[1][:, main:])),
              panels(tiles(win2[1][:, :main])), panels(tiles(a["w_out_2"][1])),
              interleave(panels(tiles(a["w_up_2"][1])), pairs(a["w_down_2"][1]), 1)]
    wall = np.concatenate(parts)
    assert wall.shape[0] == NPAN - 4
    narrow = panels(tiles(win2[0][:, :main], [6, 7, 4, 5, 2, 3, 0, 1], PGW))

    def cols(v):
        return v.reshape(-1, P).T

    def twice(v):
        return np.concatenate([v, v]).reshape(P, 1)

    gb = a["gate_b"][0].reshape(4, D)
    par = np.concatenate(
        [cols(a["mix_norm_g"][0])] + [cols(gb[b]) for b in branch]
        + [cols(a["sc_conv_w"][0].reshape(-1)), cols(a["rw_mu"][0])]
        + [cols(a[n][0].reshape(-1)) for n in ("rw_w0", "rw_a0", "rw_k_k", "rw_k_a", "rw_r_k", "rw_gn_g", "rw_gn_b",
                                               "sg_ln_g", "sg_ln_b", "ffn_norm_g", "ffn_conv_w")]
        + [cols(a["final_norm_g"]), cols(a["norm_mix_2"].reshape(-1)), cols(a["pool_scale_2"][0]),
           cols(a["kv_norm_2"]), twice(a["k_norm_2"]), twice(a["q_norm_2"][0]), cols(a["mem_norm_2"].reshape(-1)),
           twice(a["mem_q_norm_2"][0]), twice(a["mem_q_norm_2"][1]), twice(a["mem_k_norm_2"][0]),
           twice(a["mem_k_norm_2"][1]), cols(a["norm_mlp_2"].reshape(-1)),
           np.broadcast_to(a["sinks_2"][0][None], (P, QH))], 1)
    assert par.shape == (P, NPC)

    def across(v):
        return v.T.reshape(KT, P, T).transpose(1, 0, 2)

    consts, levels = shape_constants()
    import ml_dtypes
    arrays = {
        "wall": wall, "wnarrow": narrow, "par": par, "cst": consts, "lvl": levels.astype(ml_dtypes.bfloat16),
        "x": across(a["x"][0]), "mem": across(a["mem_2"][0]),
        "lora": np.stack([np.concatenate([a["rw_w2"][0], a["rw_a2"][0]]), a["rw_g2"][0]], 1),
        "sg_w": a["sg_w"][0].transpose(2, 0, 1), "sg_b": a["sg_b"][0].reshape(1, -1),
        "pool_w": a["pool_w_2"][0].reshape(PG, 2, PGW, 2 * PGW).transpose(2, 0, 1, 3),
    }
    arrays = {k: np.ascontiguousarray(v) for k, v in arrays.items()}
    nc = bacc.Bacc("TRN2", target_bir_lowering=False, num_devices=1)
    A = {k: nc.dram_tensor(k + "_dram", v.shape, mybir.dt.from_np(v.dtype), kind="ExternalInput").ap()
         for k, v in arrays.items()}
    A["out"] = nc.dram_tensor("out_dram", (P, KT, T), F32, kind="ExternalOutput").ap()
    build(nc, A)
    r = run_bass_kernel_spmd(nc, [{k + "_dram": v for k, v in arrays.items()}], core_ids=[0])
    y = r.results[0]["out_dram"]
    return y.transpose(1, 0, 2).reshape(D, T).T.reshape(1, T, D)
```
